# Optimizing a Trainium2 kernel written in Bass

```python
import jax, jax.numpy as jnp
from jax import lax
import numpy as np

D_MODEL = 1024
BATCH = 1
SEQ = 1024
DEPTH = 1
DEC_BATCH = 1
DEC_SEQ = 64
PAST_LEN = 128

CHUNK = 64
D_MIX = D_MODEL
D_ATTN = D_MIX // 2
D_CONV = D_MIX - D_ATTN
HEAD_DIM = 64
N_HEADS = D_ATTN // HEAD_DIM
CONV_WIDTH = 31
CONV_STATE = CONV_WIDTH - 1
Q_BLOCK = 128
PEER_HEADS = 8
PEER_NKEYS = 128
PEER_EXPERTS = PEER_NKEYS * PEER_NKEYS
PEER_QDIM = 256
PEER_HALF = PEER_QDIM // 2
PEER_TOPK = 16
PEER_TOK_BLOCK = 128
D_IN_PROJ = 3 * D_ATTN + N_HEADS + 2 * D_CONV
RMS_EPS = 1e-6
LN_EPS = 1e-5

kernel_name = 'hymba_conformer_fox_peer_stream_step'

def rms_norm(x, g):
    xf = x.astype(jnp.float32)
    y = xf * lax.rsqrt(jnp.mean(xf * xf, axis=-1, keepdims=True) + RMS_EPS)
    return (y * g.astype(jnp.float32)).astype(x.dtype)

def layer_norm(x, g, b):
    xf = x.astype(jnp.float32)
    mu = jnp.mean(xf, axis=-1, keepdims=True)
    xc = xf - mu
    var = jnp.mean(xc * xc, axis=-1, keepdims=True)
    y = xc * lax.rsqrt(var + LN_EPS) * g.astype(jnp.float32) + b.astype(jnp.float32)
    return y.astype(x.dtype)

def fox_attention(q, k, v, logf, k_past, v_past, logf_past):
    B, T, H, Dh = q.shape
    P = k_past.shape[1]
    L = P + T
    k_all = jnp.concatenate([k_past, k], axis=1).astype(jnp.float32)
    v_all = jnp.concatenate([v_past, v], axis=1).astype(jnp.float32)
    c_all = jnp.cumsum(jnp.concatenate([logf_past, logf], axis=1).astype(jnp.float32), axis=1)
    c_k = jnp.transpose(c_all, (0, 2, 1))
    key_pos = jnp.arange(L)
    qb = Q_BLOCK if T % Q_BLOCK == 0 else T
    nb = T // qb
    scale = HEAD_DIM ** -0.5
    q_blocks = jnp.transpose((q.astype(jnp.float32) * scale).reshape(B, nb, qb, H, Dh), (1, 0, 2, 3, 4))
    cq_blocks = jnp.transpose(c_all[:, P:].reshape(B, nb, qb, H), (1, 0, 3, 2))
    qpos_blocks = (P + jnp.arange(T)).reshape(nb, qb)

    def one_block(args):
        q_blk, cq, qpos = args
        s = jnp.einsum('bqhd,bkhd->bhqk', q_blk, k_all)
        s = s + cq[..., :, None] - c_k[:, :, None, :]
        s = jnp.where(key_pos[None, None, None, :] <= qpos[None, None, :, None], s, -jnp.inf)
        p = jax.nn.softmax(s, axis=-1)
        return jnp.einsum('bhqk,bkhd->bqhd', p, v_all)

    o = lax.map(one_block, (q_blocks, cq_blocks, qpos_blocks))
    return jnp.transpose(o, (1, 0, 2, 3, 4)).reshape(B, T, H * Dh).astype(q.dtype)

def conv_module(a, gate, conv_past, w_dw, b_dw, ln_g, ln_b):
    u = a * jax.nn.sigmoid(gate)
    u_full = jnp.concatenate([conv_past.astype(u.dtype), u], axis=1)
    y = lax.conv_general_dilated(u_full, w_dw[:, None, :].astype(u.dtype), window_strides=(1,),
                                 padding='VALID', dimension_numbers=('NWC', 'WIO', 'NWC'),
                                 feature_group_count=u.shape[-1])
    y = layer_norm(y + b_dw, ln_g, ln_b)
    return jax.nn.silu(y), u_full[:, -CONV_STATE:]

def peer_ffn(x, w_pq, sub_keys, u_emb, v_emb):
    B, T, D = x.shape
    n = B * T
    pad = (-n) % PEER_TOK_BLOCK
    xt = jnp.pad(x.reshape(n, D), ((0, pad), (0, 0)))
    nb = xt.shape[0] // PEER_TOK_BLOCK
    keys = sub_keys.astype(jnp.float32)

    def block(xb):
        t = xb.shape[0]
        q = (xb @ w_pq).astype(jnp.float32).reshape(t, PEER_HEADS, 2, PEER_HALF)
        s = jnp.einsum('thpd,phkd->thpk', q, keys)
        top_s, top_i = lax.top_k(s, PEER_TOPK)
        cand_s = (top_s[:, :, 0, :, None] + top_s[:, :, 1, None, :]).reshape(t, PEER_HEADS, PEER_TOPK * PEER_TOPK)
        cand_i = (top_i[:, :, 0, :, None] * PEER_NKEYS + top_i[:, :, 1, None, :]).reshape(t, PEER_HEADS, PEER_TOPK * PEER_TOPK)
        best_s, best_j = lax.top_k(cand_s, PEER_TOPK)
        expert = jnp.take_along_axis(cand_i, best_j, axis=-1)
        g = jax.nn.softmax(best_s, axis=-1)
        h = jnp.einsum('td,thkd->thk', xb, u_emb[expert])
        act = (g * jax.nn.gelu(h.astype(jnp.float32), approximate=False)).astype(xb.dtype)
        return jnp.einsum('thk,thkd->td', act, v_emb[expert])

    out = lax.map(block, xt.reshape(nb, PEER_TOK_BLOCK, D))
    return out.reshape(nb * PEER_TOK_BLOCK, D)[:n].reshape(B, T, D)

def hybrid_layer(x, k_past, v_past, logf_past, conv_past, g_mix, w_in, b_f, w_dw, b_dw, ln_g, ln_b,
                 w_out, g_ffn, w_pq, sub_keys, u_emb, v_emb):
    B, T, _ = x.shape
    h = rms_norm(x, g_mix)
    z = h @ w_in
    o1 = D_ATTN; o2 = 2 * D_ATTN; o3 = 3 * D_ATTN; o4 = o3 + N_HEADS; o5 = o4 + D_CONV
    q, k, v, f_logit, a, gate = jnp.split(z, [o1, o2, o3, o4, o5], axis=-1)
    q = q.reshape(B, T, N_HEADS, HEAD_DIM)
    k = k.reshape(B, T, N_HEADS, HEAD_DIM)
    v = v.reshape(B, T, N_HEADS, HEAD_DIM)
    logf = jax.nn.log_sigmoid((f_logit + b_f).astype(jnp.float32))
    attn = fox_attention(q, k, v, logf, k_past, v_past, logf_past)
    conv, conv_state = conv_module(a, gate, conv_past, w_dw, b_dw, ln_g, ln_b)
    x = x + jnp.concatenate([attn, conv], axis=-1) @ w_out
    x = x + peer_ffn(rms_norm(x, g_ffn), w_pq, sub_keys, u_emb, v_emb)
    return x, k, v, logf.astype(x.dtype), conv_state

def setup_inputs(seed: int = 0) -> dict:
    key = jax.random.key(seed)
    ks = jax.random.split(key, 24)
    f32 = jnp.float32
    nrm = lambda i, shape, s: jax.random.normal(ks[i], shape, f32) * s
    return {
        'x_prompt': nrm(0, (BATCH, SEQ, D_MODEL), 1.0),
        'x_sample': nrm(1, (DEC_BATCH, DEC_SEQ, D_MODEL), 1.0),
        'cache_k': nrm(2, (DEPTH, DEC_BATCH, PAST_LEN, N_HEADS, HEAD_DIM), 1.0),
        'cache_v': nrm(3, (DEPTH, DEC_BATCH, PAST_LEN, N_HEADS, HEAD_DIM), 1.0),
        'cache_logf': jax.nn.log_sigmoid(3.0 + nrm(4, (DEPTH, DEC_BATCH, PAST_LEN, N_HEADS), 0.5)),
        'state_conv': nrm(5, (DEPTH, DEC_BATCH, CONV_STATE, D_CONV), 0.5),
        'g_mix': 1.0 + nrm(6, (DEPTH, D_MODEL), 0.01),
        'w_in': nrm(7, (DEPTH, D_MODEL, D_IN_PROJ), D_MODEL ** -0.5),
        'b_f': 3.0 + nrm(8, (DEPTH, N_HEADS), 0.5),
        'w_dw': nrm(9, (DEPTH, CONV_WIDTH, D_CONV), CONV_WIDTH ** -0.5),
        'b_dw': nrm(10, (DEPTH, D_CONV), 0.01),
        'ln_g': 1.0 + nrm(11, (DEPTH, D_CONV), 0.01),
        'ln_b': nrm(12, (DEPTH, D_CONV), 0.01),
        'w_out': nrm(13, (DEPTH, D_MIX, D_MODEL), D_MIX ** -0.5),
        'g_ffn': 1.0 + nrm(14, (DEPTH, D_MODEL), 0.01),
        'w_pq': nrm(15, (DEPTH, D_MODEL, PEER_HEADS * PEER_QDIM), D_MODEL ** -0.5),
        'sub_keys': nrm(16, (DEPTH, 2, PEER_HEADS, PEER_NKEYS, PEER_HALF), PEER_HALF ** -0.5),
        'u_emb': nrm(17, (DEPTH, PEER_EXPERTS, D_MODEL), D_MODEL ** -0.5),
        'v_emb': nrm(18, (DEPTH, PEER_EXPERTS, D_MODEL), PEER_HEADS ** -0.5),
        'g_final': 1.0 + nrm(19, (D_MODEL,), 0.01),
    }

def reference(x_prompt, x_sample, cache_k, cache_v, cache_logf, state_conv, g_mix, w_in, b_f, w_dw, b_dw,
              ln_g, ln_b, w_out, g_ffn, w_pq, sub_keys, u_emb, v_emb, g_final):
    xp, xs = x_prompt, x_sample
    bp = xp.shape[0]
    kp_l, vp_l, fp_l, cp_l, ks_l, vs_l, fs_l, cs_l = [], [], [], [], [], [], [], []
    for l in range(DEPTH):
        w = (g_mix[l], w_in[l], b_f[l], w_dw[l], b_dw[l], ln_g[l], ln_b[l], w_out[l], g_ffn[l],
             w_pq[l], sub_keys[l], u_emb[l], v_emb[l])
        empty_kv = jnp.zeros((bp, 0, N_HEADS, HEAD_DIM), xp.dtype)
        empty_f = jnp.zeros((bp, 0, N_HEADS), jnp.float32)
        zero_conv = jnp.zeros((bp, CONV_STATE, D_CONV), xp.dtype)
        xp, kp, vp, fp, cp = hybrid_layer(xp, empty_kv, empty_kv, empty_f, zero_conv, *w)
        xs, ks_, vs_, fs_, cs_ = hybrid_layer(xs, cache_k[l], cache_v[l], cache_logf[l], state_conv[l], *w)
        kp_l.append(kp); vp_l.append(vp); fp_l.append(fp); cp_l.append(cp)
        ks_l.append(ks_); vs_l.append(vs_); fs_l.append(fs_); cs_l.append(cs_)
    y_prompt = rms_norm(xp, g_final)
    y_sample = rms_norm(xs, g_final)
    return (y_prompt, y_sample,
            jnp.stack(kp_l), jnp.stack(vp_l), jnp.stack(fp_l), jnp.stack(cp_l),
            jnp.stack(ks_l), jnp.stack(vs_l), jnp.stack(fs_l), jnp.stack(cs_l))


_drawn_inputs = setup_inputs


def setup_inputs(seed=0):
    import zlib

    import numpy as np

    out = dict(_drawn_inputs(seed))
    spreads = {}
    factors = {'cache_logf': 178.624,
     'g_mix': 4.077,
     'b_dw': 11.899,
     'ln_g': 25.58,
     'ln_b': 26.133,
     'g_ffn': 17.059,
     'g_final': 181.68,
     'cache_k': 3.908,
     'cache_v': 3.18}
    for name, (base, spread) in spreads.items():
        noise = np.random.default_rng([zlib.crc32(name.encode()), seed]).standard_normal(out[name].shape)
        drawn = base * np.exp(spread * noise) if base else spread * noise
        out[name] = __import__('jax').numpy.asarray(drawn.astype(out[name].dtype))
    for name, factor in factors.items():
        out[name] = (out[name] * factor).astype(out[name].dtype)
    return out
```

```python
from contextlib import ExitStack

import numpy as np
import concourse.bass as bass
from concourse import mybir

F32 = mybir.dt.float32
U32 = mybir.dt.uint32
ALU = mybir.AluOpType
ACT = mybir.ActivationFunctionType
AX = mybir.AxisListType

P = 128
BANK = 512
MASKED = -1e30
RMS_EPS = 1e-6
LN_EPS = 1e-5


class Named:
    pass


class Chain:

    def __init__(self, eng, sem, base=0, held=None):
        self.eng, self.sem, self.base, self.n, self.held = eng, sem, base, 0, held

    def wait(self, sem, value):
        self.eng.wait_ge(sem, value)
        if self.held is not None:
            self.eng.sem_inc(self.held, 1)

    def link(self, ins):
        ins.then_inc(self.sem, 1)
        self.n += 1
        self.wait(self.sem, self.base + self.n)

    def at(self, base):
        self.base, self.n = base, 0
        return self


def sizes(x_prompt, x_sample, cache_k, w_in, w_dw, w_pq, sub_keys, u_emb):
    s = Named()
    s.D = x_prompt.shape[2]
    s.T = x_prompt.shape[1]
    s.TS = x_sample.shape[1]
    s.PAST, s.H, s.HD = cache_k.shape[2:]
    s.DA = s.H * s.HD
    s.TAPS, s.DC = w_dw.shape[1:]
    s.NIN = w_in.shape[2]
    s.DCH = s.D // P
    s.CCH = s.DC // P
    s.NB = s.T // P
    s.SAMPLE_KB = s.NB + 1
    s.NKB = s.NB + 2
    s.PH = sub_keys.shape[2]
    s.NKEYS = sub_keys.shape[3]
    s.HALF = sub_keys.shape[4]
    s.K = 16
    s.E = u_emb.shape[1]
    assert s.PAST == P and s.HALF == P and s.NKEYS == P and s.TS == P // 2 and s.H == 8 and s.PH == 8
    return s


def build(nc, x_prompt, x_sample, cache_k, cache_v, cache_logf, state_conv, g_mix, w_in, b_f, w_dw, b_dw,
          ln_g, ln_b, w_out, g_ffn, w_pq, sub_keys, u_emb, v_emb, g_final,
          y_prompt, y_sample, k_prompt, v_prompt, logf_prompt, conv_prompt,
          k_sample, v_sample, logf_sample, conv_sample):
    s = sizes(x_prompt, x_sample, cache_k, w_in, w_dw, w_pq, sub_keys, u_emb)
    d = Named()
    d.x_prompt, d.x_sample, d.cache_k, d.cache_v, d.cache_logf, d.state_conv = x_prompt, x_sample, cache_k, cache_v, cache_logf, state_conv
    d.g_mix, d.w_in, d.b_f, d.w_dw, d.b_dw, d.ln_g = g_mix, w_in, b_f, w_dw, b_dw, ln_g
    d.ln_b, d.w_out, d.g_ffn, d.w_pq, d.sub_keys, d.u_emb = ln_b, w_out, g_ffn, w_pq, sub_keys, u_emb
    d.v_emb, d.g_final, d.k_prompt, d.v_prompt, d.logf_prompt, d.conv_prompt = v_emb, g_final, k_prompt, v_prompt, logf_prompt, conv_prompt
    d.k_sample, d.v_sample, d.logf_sample, d.conv_sample, d.y_prompt, d.y_sample = k_sample, v_sample, logf_sample, conv_sample, y_prompt, y_sample
    d.x1 = nc.dram_tensor("x1_rows", (s.NB + 1, P, s.D), F32, kind="Internal").ap()
    d.xn2 = nc.dram_tensor("xn2_rows", (s.NB + 1, P, s.D), F32, kind="Internal").ap()
    d.peer = nc.dram_tensor("peer_rows", (s.NB + 1, P, s.D), F32, kind="Internal").ap()
    with ExitStack() as ctx:
        g = Named()
        g.ident = ctx.enter_context(nc.sbuf_tensor("ident", [P, P], F32))
        g.neg_half = ctx.enter_context(nc.sbuf_tensor("neg_half", [P, 1], F32))
        g.ps = ctx.enter_context(nc.psum_tensor("ps", [P, 8, BANK], F32))
        with ExitStack() as mix:
            c = caches(nc, s, mix)
            phase_a(nc, s, d, g, c)
            phase_b(nc, s, d, g, c)
        phase_c(nc, s, d, g)
        phase_d(nc, s, d, g)


def caches(nc, s, ctx):
    c = Named()

    def sb(name, shape):
        return ctx.enter_context(nc.sbuf_tensor(name, shape, F32))

    c.keysT = sb("keysT", [s.HD + 1, s.H, s.NKB * P])
    c.values = sb("values", [P, s.NKB, s.DA])
    c.queries = sb("queries", [P, s.NB + 1, s.DA])
    c.convT = sb("convT", [P, s.CCH, (s.NB + 1) * P])
    c.cum = sb("cum", [P, s.NB + 1, s.H])
    c.vecT = sb("vecT", [P, s.DCH + 3 * s.CCH])
    c.g_mix = c.vecT[:, 0:s.DCH]
    c.b_dw, c.ln_g, c.ln_b = (c.vecT[:, s.DCH + i * s.CCH:s.DCH + (i + 1) * s.CCH] for i in range(3))
    return c


def phase_a(nc, s, d, g, c):
    with ExitStack() as ctx:
        def sb(name, shape):
            return ctx.enter_context(nc.sbuf_tensor(name, shape, F32))

        def sem(name):
            return ctx.enter_context(nc.semaphore(name))

        COLS = {}
        at = 0
        for name, width in (("q", s.DA), ("k", s.DA), ("v", s.DA), ("f", s.H), ("a", s.DC), ("gate", s.DC)):
            COLS[name] = (at, width)
            at += width
        ORDER = ("gate", "a", "f", "q", "k", "v")
        NPROJ = len(ORDER)
        HALO = s.TAPS - 1

        w_in = sb("w_in_sb", [P, s.DCH, s.NIN])
        x = sb("x_a", [P, s.D])
        xn = sb("xn_a", [P, s.D])
        hT = sb("hT_a", [P, s.DCH, P])
        k_aug = sb("k_aug", [P, s.H, s.HD + 1])
        sig = sb("sig_a", [P, s.DC])
        u = sb("u_a", [P, s.DC])
        uT = sb("uT_a", [P, s.CCH, HALO + P])
        upto = sb("upto", [P, P])
        last_row = sb("last_row", [P, P])
        bf = sb("bf_rows", [P, s.H])
        ss = sb("ss_a", [P, 1])
        ms = sb("ms_a", [P, 1])
        rstd = sb("rstd_a", [P, 1])
        z = sb("z_a", [P, s.H])
        az = sb("az_a", [P, s.H])
        ez = sb("ez_a", [P, s.H])
        ln = sb("ln_a", [P, s.H])
        pz = sb("pz_a", [P, 4, s.H])
        logf = sb("logf_a", [P, s.H])
        logfs = sb("logfs", [P, s.NB + 1, s.H])
        cum = sb("cum_a", [P, s.H])
        cum_past = sb("cum_past", [P, s.H])
        logf_past = sb("logf_past", [P, s.H])
        taps = sb("taps", [s.TAPS, s.DC])
        tapsT = sb("tapsT", [P, s.CCH, s.TAPS])
        NVEC = s.DCH + 3 * s.CCH
        vecs = sb("vecs", [NVEC, P])
        state = sb("state", [HALO, s.DC])
        stateT = sb("stateT", [P, s.CCH, HALO])

        w_here = {n: sem("w_here_" + n) for n in ORDER}
        x_here = sem("x_here_a")
        small_here = sem("small_here")
        past_here = sem("past_here")
        consts = sem("consts_a")
        setup_psum = sem("setup_psum")
        setup_sb = sem("setup_sb")
        ms_ready = sem("ms_ready_a")
        rstd_ready = sem("rstd_ready_a")
        xn_ready = sem("xn_ready_a")
        hT_psum = sem("hT_psum_a")
        hT_ready = sem("hT_ready_a")
        proj_psum = sem("proj_psum")
        sig_ready = sem("sig_ready_a")
        u_ready = sem("u_ready")
        uT_psum = sem("uT_psum")
        uT_ready = sem("uT_ready")
        z_ready = sem("z_ready")
        ez_ready = sem("ez_ready")
        ln_ready = sem("ln_ready")
        logf_ready = sem("logf_ready")
        cum_psum = sem("cum_psum")
        cum_ready = sem("cum_ready")
        kaug_ready = sem("kaug_ready")
        q_ready = sem("q_ready_a")
        k_ready = sem("k_ready")
        v_ready = sem("v_ready")
        kT_psum = sem("kT_psum")
        kT_ready = sem("kT_ready")
        k_stored = sem("k_stored")
        v_stored = sem("v_stored")
        misc_stored = sem("misc_stored")
        act_chain, dve_chain, pool_chain = sem("act_chain_a"), sem("dve_chain_a"), sem("pool_chain_a")
        pool_held = sem("pool_held_a")

        ps = g.ps
        BLOCKS = s.NB + 1
        HB, GATE, A_, F_, Q_, K_, V_ = 0, 2, 3, 4, 5, 6, 7
        BANK_OF = {"gate": GATE, "a": A_, "f": F_, "q": Q_, "k": K_, "v": V_}
        KTB, UTB = 2, 0
        PAST = 1

        block = ctx.enter_context(nc.Block())

        @block.sync
        def _(sp):
            sp.dma_start(x[:, :], d.x_prompt[0, 0:P, :]).then_inc(x_here, 16)
            sp.dma_start(vecs[0:s.DCH, :], d.g_mix[0].rearrange("(c p) -> c p", p=P)).then_inc(small_here, 16)
            for i, v in enumerate((d.b_dw, d.ln_g, d.ln_b)):
                lo = s.DCH + i * s.CCH
                sp.dma_start(vecs[lo:lo + s.CCH, :], v[0].rearrange("(c p) -> c p", p=P)).then_inc(small_here, 16)
            sp.dma_start(taps[:, :], d.w_dw[0]).then_inc(small_here, 16)
            sp.dma_start(state[:, :], d.state_conv[0, 0]).then_inc(small_here, 16)
            sp.dma_start(bf[:, :], d.b_f[0].partition_broadcast(P)).then_inc(small_here, 16)
            sp.dma_start(k_aug[:, :, 0:s.HD], d.cache_k[0, 0]).then_inc(past_here, 16)
            sp.dma_start(logf_past[:, :], d.cache_logf[0, 0]).then_inc(past_here, 16)
            sp.dma_start(c.values[:, s.NB, :], d.cache_v[0, 0].rearrange("t h e -> t (h e)")).then_inc(past_here, 16)
            w_rows = d.w_in[0].rearrange("(c p) n -> p c n", p=P)
            for name in ORDER:
                lo, width = COLS[name]
                sp.dma_start(w_in[:, :, lo:lo + width], w_rows[:, :, lo:lo + width]).then_inc(w_here[name], 16)

            def stores(b, kb, k_out, v_out, rows):
                sp.wait_ge(k_ready, b + 2)
                sp.dma_start(k_out, k_aug[0:rows, :, 0:s.HD]).then_inc(k_stored, 16)
                sp.wait_ge(v_ready, b + 2)
                sp.dma_start(v_out, c.values[0:rows, kb, :]).then_inc(v_stored, 16)

            def prompt_stores(b):
                if isinstance(b, int):
                    v = c.values[:, b, :]
                else:
                    v = c.values[:, bass.ds(b, 1), :].rearrange("p a n -> p (a n)")
                sp.wait_ge(k_ready, b + 2)
                sp.dma_start(k_rows[bass.ds(b * P, P)], k_aug[:, :, 0:s.HD]).then_inc(k_stored, 16)
                sp.wait_ge(v_ready, b + 2)
                sp.dma_start(v_rows[bass.ds(b * P, P), :], v).then_inc(v_stored, 16)

            sp.sem_inc(k_stored, 16)
            k_rows = d.k_prompt[0, 0]
            v_rows = d.v_prompt[0, 0].rearrange("t h e -> t (h e)")
            with sp.Fori(0, s.NB - 1) as b:
                sp.wait_ge(xn_ready, b + 1)
                sp.dma_start(x[:, :], d.x_prompt[0, bass.ds((b + 1) * P, P), :]).then_inc(x_here, 16)
                prompt_stores(b)
            sp.wait_ge(xn_ready, s.NB)
            sp.dma_start(x[0:s.TS, :], d.x_sample[0]).then_inc(x_here, 16)
            prompt_stores(s.NB - 1)
            sp.wait_ge(u_ready, 1 + s.NB)
            sp.dma_start(d.conv_prompt[0, 0], u[P - HALO:P, :]).then_inc(misc_stored, 16)
            stores(s.NB, s.SAMPLE_KB, d.k_sample[0, 0], d.v_sample[0, 0].rearrange("t h e -> t (h e)"), s.TS)
            sp.wait_ge(u_ready, 1 + BLOCKS)
            sp.dma_start(d.conv_sample[0, 0], u[s.TS - HALO:s.TS, :]).then_inc(misc_stored, 16)
            sp.wait_ge(logf_ready, 1 + 2 * BLOCKS)
            sp.dma_start(d.logf_prompt[0, 0].rearrange("(b p) h -> p b h", p=P), logfs[:, 0:s.NB, :]).then_inc(misc_stored, 16)
            sp.dma_start(d.logf_sample[0, 0], logfs[0:s.TS, s.NB, :]).then_inc(misc_stored, 16)
            sp.wait_ge(k_stored, 16 * (1 + BLOCKS))
            sp.wait_ge(v_stored, 16 * BLOCKS)
            sp.wait_ge(misc_stored, 64)

        @block.gpsimd
        def _(pool):
            chain = Chain(pool, pool_chain, held=pool_held)
            chain.link(nc.gpsimd.memset(g.ident[:, :], 0.0))
            nc.gpsimd.affine_select(out=g.ident[:, :], in_=g.ident[:, :], compare_op=ALU.not_equal, fill=1.0,
                                    base=0, pattern=[[-1, P]], channel_multiplier=1).then_inc(consts, 1)
            nc.gpsimd.memset(g.neg_half[:, :], -0.5)
            chain.link(nc.gpsimd.memset(upto[:, :], 1.0))
            nc.gpsimd.affine_select(out=upto[:, :], in_=upto[:, :], compare_op=ALU.is_ge, fill=0.0,
                                    base=0, pattern=[[1, P]], channel_multiplier=-1).then_inc(consts, 1)
            chain.link(nc.gpsimd.memset(last_row[:, :], 0.0))
            nc.gpsimd.affine_select(out=last_row[:, :], in_=last_row[:, :], compare_op=ALU.not_equal, fill=1.0,
                                    base=1 - P, pattern=[[0, P]], channel_multiplier=1).then_inc(consts, 1)
            pool.wait_ge(past_here, 48)
            pool.wait_ge(cum_ready, 1)
            nc.gpsimd.tensor_scalar(k_aug[:, :, s.HD], cum_past[:, :], -1.0, None, ALU.mult).then_inc(kaug_ready, 1)
            SETUP_LINKS = chain.n
            LINKS = 3

            def rms_scale(b):
                chain.wait(ms_ready, b + 1)
                nc.gpsimd.tensor_tensor(out=rstd[:, :], in0=ms[:, :], in1=g.neg_half[:, :], op=ALU.pow).then_inc(rstd_ready, 1)

            def log_forget(b, blk):
                chain.wait(ez_ready, b + 1)
                chain.link(nc.gpsimd.tensor_scalar(pz[:, 0, :], ez[:, :], 1.0, -1.0, ALU.add, ALU.add))
                nc.gpsimd.tensor_tensor(out=pz[:, 1, :], in0=ez[:, :], in1=pz[:, 0, :], op=ALU.subtract)
                chain.wait(ln_ready, b + 1)
                chain.link(nc.gpsimd.tensor_scalar(pz[:, 3, :], z[:, :], 0.0, None, ALU.min))
                chain.link(nc.gpsimd.tensor_tensor(out=pz[:, 2, :], in0=ln[:, :], in1=pz[:, 1, :], op=ALU.add))
                chain.wait(cum_psum, b + 1)
                nc.gpsimd.tensor_tensor(out=logf[:, :], in0=pz[:, 3, :], in1=pz[:, 2, :], op=ALU.subtract).then_inc(logf_ready, 1)
                chain.wait(logf_ready, 2 * b + 2)
                nc.gpsimd.tensor_copy(blk(logfs), logf[:, :]).then_inc(logf_ready, 1)

            def cum_columns(b, blk):
                chain.wait(cum_ready, PAST + b + 1)
                nc.gpsimd.tensor_copy(blk(c.cum), cum[:, :])
                chain.wait(kT_psum, PAST + b)
                nc.gpsimd.tensor_scalar(k_aug[:, :, s.HD], cum[:, :], -1.0, None, ALU.mult).then_inc(kaug_ready, 1)

            pool.sem_inc(logf_ready, 1)
            rms_scale(0)
            with pool.Fori(0, s.NB) as b:
                chain.at(SETUP_LINKS + b * LINKS)
                blk = lambda t: t[:, bass.ds(b, 1), :].rearrange("p a n -> p (a n)")
                rms_scale(b + 1)
                log_forget(b, blk)
                cum_columns(b, blk)
                assert chain.n == LINKS
            chain.at(SETUP_LINKS + s.NB * LINKS)
            log_forget(s.NB, lambda t: t[:, s.NB, :])
            cum_columns(s.NB, lambda t: t[:, s.NB, :])

        @block.scalar
        def _(act):
            chain = Chain(act, act_chain)
            act.wait_ge(setup_psum, 3)
            nc.scalar.copy(tapsT[:, :, :], ps[:, Q_, 0:s.CCH * s.TAPS].rearrange("p (c j) -> p c j", c=s.CCH)).then_inc(setup_sb, 1)
            nc.scalar.copy(c.vecT[:, :], ps[:, K_, 0:NVEC]).then_inc(setup_sb, 1)
            nc.scalar.copy(stateT[:, :, :], ps[:, V_, 0:s.CCH * HALO].rearrange("p (c j) -> p c j", c=s.CCH)).then_inc(setup_sb, 1)
            act.wait_ge(cum_psum, 1)
            nc.scalar.copy(cum_past[:, :], ps[:, F_, s.H:2 * s.H]).then_inc(cum_ready, 1)

            def keys_out(kcount, kb):
                act.wait_ge(kT_psum, kcount)
                for i in range(2):
                    src = ps[0:s.HD + 1, KTB + i, :].rearrange("p (h t) -> p h t", t=P)
                    ins = nc.scalar.copy(c.keysT[:, 4 * i:4 * i + 4, bass.ds(kb * P, P)], src)
                ins.then_inc(kT_ready, 1)

            def row_scale(b):
                act.wait_ge(x_here, 16 * (b + 1))
                chain.link(nc.scalar.activation(xn[:, :], x[:, :], ACT.Square, accum_out=ss[:, :]))
                nc.scalar.activation(ms[:, :], ss[:, :], ACT.Copy, bias=RMS_EPS, scale=1.0 / s.D).then_inc(ms_ready, 1)

            def normed(b):
                act.wait_ge(rstd_ready, b + 1)
                nc.scalar.mul(xn[:, :], x[:, :], rstd[:, 0:1]).then_inc(xn_ready, 1)

            def iteration(b, kb, q_dst, v_dst, prepare_next):
                act.wait_ge(hT_psum, 2 * b + 2)
                act.wait_ge(setup_sb, 2)
                for i in range(s.DCH):
                    ins = nc.scalar.mul(hT[:, i, :], ps[:, HB + i // 4, (i % 4) * P:(i % 4 + 1) * P], c.g_mix[:, i:i + 1])
                ins.then_inc(hT_ready, 1)
                if prepare_next:
                    row_scale(b + 1)
                act.wait_ge(proj_psum, NPROJ * b + 1)
                act.wait_ge(u_ready, b + 1)
                nc.scalar.activation(sig[:, :], ps[:, GATE, :], ACT.Sigmoid).then_inc(sig_ready, 1)
                if prepare_next:
                    normed(b + 1)
                act.wait_ge(z_ready, b + 1)
                act.wait_ge(logf_ready, 2 * b + 1)
                chain.link(nc.scalar.activation(az[:, :], z[:, :], ACT.Abs))
                nc.scalar.activation(ez[:, :], az[:, :], ACT.Exp, scale=-1.0).then_inc(ez_ready, 1)
                act.wait_ge(ez_ready, b + 1)
                nc.scalar.activation(ln[:, :], ez[:, :], ACT.Ln, bias=1.0).then_inc(ln_ready, 1)
                act.wait_ge(proj_psum, NPROJ * b + 4)
                nc.scalar.mul(q_dst, ps[:, Q_, :], s.HD ** -0.5).then_inc(q_ready, 1)
                act.wait_ge(proj_psum, NPROJ * b + 5)
                act.wait_ge(kT_psum, PAST + b)
                act.wait_ge(k_stored, 16 * b + 16)
                nc.scalar.copy(k_aug[:, :, 0:s.HD], ps[:, K_, :].rearrange("p (h e) -> p h e", e=s.HD)).then_inc(k_ready, 1)
                act.wait_ge(cum_psum, PAST + b + 1)
                act.wait_ge(kaug_ready, PAST + b)
                nc.scalar.copy(cum[:, :], ps[:, F_, s.H:2 * s.H]).then_inc(cum_ready, 1)
                act.wait_ge(proj_psum, NPROJ * b + 6)
                nc.scalar.copy(v_dst, ps[:, V_, :]).then_inc(v_ready, 1)
                keys_out(PAST + b + 1, kb)

            keys_out(PAST, s.NB)
            for free in (q_ready, k_ready, v_ready):
                act.sem_inc(free, 1)
            row_scale(0)
            normed(0)
            SETUP_LINKS, LINKS = chain.n, 2
            with act.Fori(0, s.NB) as b:
                chain.at(SETUP_LINKS + b * LINKS)
                iteration(b, b, c.queries[:, bass.ds(b, 1), :].rearrange("p a n -> p (a n)"),
                          c.values[:, bass.ds(b, 1), :].rearrange("p a n -> p (a n)"), True)
                assert chain.n == LINKS
            chain.at(SETUP_LINKS + s.NB * LINKS)
            iteration(s.NB, s.SAMPLE_KB, c.queries[:, s.NB, :], c.values[:, s.SAMPLE_KB, :], False)

        @block.tensor
        def _(pe):
            pe.wait_ge(consts, 3)
            pe.wait_ge(small_here, 16 * 7)
            for i in range(s.CCH):
                pe.transpose(ps[:, Q_, i * s.TAPS:(i + 1) * s.TAPS], taps[:, i * P:(i + 1) * P], g.ident[0:s.TAPS, 0:s.TAPS])
            pe.transpose(ps[:, K_, 0:NVEC], vecs[:, :], g.ident[0:NVEC, 0:NVEC])
            for i in range(s.CCH):
                ins = pe.transpose(ps[:, V_, i * HALO:(i + 1) * HALO], state[:, i * P:(i + 1) * P], g.ident[0:HALO, 0:HALO])
            ins.then_inc(setup_psum, 3)
            pe.wait_ge(past_here, 48)
            pe.matmul(ps[:, F_, s.H:2 * s.H], upto[:, :], logf_past[:, :], start=True, stop=True).then_inc(cum_psum, 1)

            def keys_in(kcount):
                pe.wait_ge(kaug_ready, kcount)
                for h in range(s.H):
                    ins = pe.transpose(ps[0:s.HD + 1, KTB + h // 4, (h % 4) * P:(h % 4 + 1) * P], k_aug[:, h, :], g.ident[:, :])
                ins.then_inc(kT_psum, 1)

            def iteration(b, cum_before):
                pe.wait_ge(uT_ready, b + 1)
                pe.wait_ge(xn_ready, b + 1)
                for i in range(s.DCH):
                    ins = pe.transpose(ps[:, HB + i // 4, (i % 4) * P:(i % 4 + 1) * P], xn[:, i * P:(i + 1) * P], g.ident[:, :])
                    if i % 4 == 3:
                        ins.then_inc(hT_psum, 1)
                pe.wait_ge(hT_ready, b + 1)
                for name in ORDER:
                    lo, width = COLS[name]
                    pe.wait_ge(w_here[name], 16)
                    if name == "gate":
                        pe.wait_ge(kT_ready, PAST + b)
                    if name == "f":
                        pe.wait_ge(cum_ready, PAST + b)
                    if name == "q":
                        pe.wait_ge(q_ready, b + 1)
                    if name == "k":
                        pe.wait_ge(k_ready, b + 1)
                    if name == "v":
                        pe.wait_ge(logf_ready, 2 * b + 2)
                        pe.matmul(ps[:, F_, s.H:2 * s.H], upto[:, :], logf[:, :], start=True, stop=False)
                        pe.matmul(ps[:, F_, s.H:2 * s.H], last_row[:, :], cum_before, start=False, stop=True).then_inc(cum_psum, 1)
                        pe.wait_ge(v_ready, b + 1)
                    for i in range(s.DCH):
                        ins = pe.matmul(ps[:, BANK_OF[name], 0:width], hT[:, i, :], w_in[:, i, lo:lo + width],
                                        start=(i == 0), stop=(i == s.DCH - 1))
                    ins.then_inc(proj_psum, 1)
                pe.wait_ge(u_ready, b + 2)
                for i in range(s.CCH):
                    ins = pe.transpose(ps[:, UTB, i * P:(i + 1) * P], u[:, i * P:(i + 1) * P], g.ident[:, :])
                ins.then_inc(uT_psum, 1)
                keys_in(PAST + b + 1)

            keys_in(PAST)
            with pe.Fori(0, s.NB) as b:
                iteration(b, cum[:, :])
            iteration(s.NB, cum_past[:, :])

        @block.vector
        def _(dve):
            chain = Chain(dve, dve_chain)
            chain.link(nc.vector.memset(cum[:, :], 0.0))
            chain.link(nc.vector.memset(uT[:, :, 0:HALO], 0.0))
            dve.wait_ge(setup_sb, 3)

            def iteration(b, y_of, last):
                dve.wait_ge(proj_psum, NPROJ * b + 2)
                dve.wait_ge(sig_ready, b + 1)
                nc.vector.tensor_tensor(out=u[:, :], in0=ps[:, A_, :], in1=sig[:, :], op=ALU.mult).then_inc(u_ready, 1)
                dve.wait_ge(proj_psum, NPROJ * b + 3)
                nc.vector.tensor_tensor(out=z[:, :], in0=ps[:, F_, 0:s.H], in1=bf[:, :], op=ALU.add).then_inc(z_ready, 1)
                dve.wait_ge(uT_psum, b + 1)
                nc.vector.tensor_copy(uT[:, :, HALO:HALO + P], ps[:, UTB, :].rearrange("p (c t) -> p c t", t=P)).then_inc(uT_ready, 1)
                dve.wait_ge(uT_ready, b + 2)
                for j in range(s.TAPS):
                    for i in range(s.CCH):
                        src, dst = uT[:, i, j:j + P], y_of(i)
                        if j == 0:
                            ins = nc.vector.tensor_scalar(dst, src, tapsT[:, i, 0:1], c.b_dw[:, i:i + 1], ALU.mult, ALU.add)
                        else:
                            dve.wait_ge(dve_chain, chain.base + chain.n - s.CCH + 1)
                            ins = nc.vector.scalar_tensor_tensor(out=dst, in0=src, scalar=tapsT[:, i, j:j + 1], in1=dst,
                                                                 op0=ALU.mult, op1=ALU.add)
                        ins.then_inc(dve_chain, 1)
                        chain.n += 1
                dve.wait_ge(dve_chain, chain.base + chain.n)
                if not last:
                    chain.link(nc.vector.tensor_copy(uT[:, :, 0:HALO], uT[:, :, P:P + HALO]))

            for free in (u_ready, uT_ready):
                dve.sem_inc(free, 1)
            SETUP_LINKS, LINKS = chain.n, s.TAPS * s.CCH + 1
            with dve.Fori(0, s.NB) as b:
                chain.at(SETUP_LINKS + b * LINKS)
                iteration(b, lambda i: c.convT[:, i, bass.ds(b * P, P)], False)
                assert chain.n == LINKS
            chain.at(SETUP_LINKS + s.NB * LINKS)
            chain.link(nc.vector.tensor_copy(uT[:, :, 0:HALO], stateT[:, :, :]))
            dve.wait_ge(misc_stored, 16)
            iteration(s.NB, lambda i: c.convT[:, i, s.NB * P:(s.NB + 1) * P], True)


def phase_b(nc, s, d, g, c):
    with ExitStack() as ctx:
        def sb(name, shape):
            return ctx.enter_context(nc.sbuf_tensor(name, shape, F32))

        def sem(name):
            return ctx.enter_context(nc.semaphore(name))

        HALF = s.NB // 2
        SPAN = HALF * P
        assert SPAN == BANK and s.CCH == 4 and s.DA == BANK

        w_out = sb("w_out_sb", [P, s.DCH, s.D])
        mask = sb("mask", [P, 2 * SPAN - P])
        q_aug = sb("q_aug", [P, s.H, s.HD + 1])
        qT = sb("qT_b", [s.HD + 1, s.H, P])
        y_st = sb("y_st", [P, s.CCH, P])
        cb = sb("cum_b", [P, s.H])
        scores = sb("scores", [P, 2, s.T])
        probs = sb("probs", [P, 2, s.T])
        probsT = sb("probsT", [P, s.T])
        top = sb("row_max", [P, s.H])
        ntop = sb("neg_row_max", [P, s.H])
        rs = sb("row_sum", [P, s.H])
        rinv = sb("row_sum_inv", [P, s.H])
        stats = sb("ln_stats", [P, 6])
        mv = sb("ln_mv", [P, 2])
        var = sb("ln_var", [P, 1])
        lnr = sb("ln_rstd", [P, 1])
        z = sb("z_b", [P, s.DC])
        sig = sb("sig_b", [P, s.CCH, P])
        yn = sb("yn_b", [P, s.CCH, P])
        o = sb("o_b", [P, s.DA])
        catT = sb("catT", [P, s.DCH, P])
        xres = sb("xres_b", [P, s.D])
        x1 = sb("x1_b", [P, s.D])
        sq = sb("sq_b", [P, s.D])
        xn = sb("xn_b", [P, s.D])
        gf = sb("g_ffn_rows", [P, s.D])
        rms = sb("rms_b", [P, 3])

        w_here, x_here, gf_here = sem("w_here_b"), sem("x_here_b"), sem("gf_here")
        consts = sem("consts_b")
        q_staged, y_staged, c_staged = sem("q_staged"), sem("y_staged"), sem("c_staged")
        qT_psum, qT_ready = sem("qT_psum"), sem("qT_ready")
        s_psum, top_ready, p_ready = sem("s_psum"), sem("top_ready"), sem("p_ready")
        pT_psum, pTa_ready, pTd_ready, pv_psum = sem("pT_psum"), sem("pTa_ready"), sem("pTd_ready"), sem("pv_psum")
        y_psum, mv_ready, lnr_ready, z_ready = sem("y_psum"), sem("mv_ready"), sem("lnr_ready"), sem("z_ready_b")
        zT_psum, sig_ready, conv_ready = sem("zT_psum"), sem("sig_ready_b"), sem("conv_ready")
        o_ready, oT_psum, oT_ready = sem("o_ready"), sem("oT_psum"), sem("oT_ready")
        x1_psum, x1_ready, ss_ready, xn_ready = sem("x1_psum"), sem("x1_ready"), sem("ss_ready"), sem("xn_ready_b")
        x1_stored, xn_stored = sem("x1_stored"), sem("xn_stored")
        dve_chain, pool_chain, pool_held, dve_held = (sem(n + "_b") for n in ("dve_chain", "pool_chain", "pool_held", "dve_held"))

        ps = g.ps
        S_, PT_, O_, T_, X1_ = 0, 4, 6, 7, 2
        H = s.H
        BLOCKS = s.NB + 1
        low = dict(nkb=HALF, kb0=0, mask_at=lambda b: SPAN - P - b * P)
        high = dict(nkb=s.NB, kb0=0, mask_at=lambda b: SPAN - P + SPAN - b * P)
        sample = dict(nkb=2, kb0=s.NB, mask_at=lambda b: SPAN - 2 * P)

        def over_blocks(eng, body):
            with eng.Fori(0, HALF) as b:
                body(b, **low)
            with eng.Fori(HALF, s.NB) as b:
                body(b, **high)
            body(s.NB, **sample)

        block = ctx.enter_context(nc.Block())

        @block.sync
        def _(sp):
            sp.dma_start(xres[:, :], d.x_prompt[0, 0:P, :]).then_inc(x_here, 16)
            sp.dma_start(w_out[:, :, :], d.w_out[0].rearrange("(c p) n -> p c n", p=P)).then_inc(w_here, 16)
            sp.dma_start(gf[:, :], d.g_ffn[0].partition_broadcast(P)).then_inc(gf_here, 16)
            x1_rows = d.x1.rearrange("b p n -> (b p) n")
            xn_rows = d.xn2.rearrange("b p n -> (b p) n")

            def store_x1(b):
                sp.dma_start(x1_rows[bass.ds(b * P, P), :], x1[:, :]).then_inc(x1_stored, 16)

            def store_xn(b):
                sp.wait_ge(xn_ready, b + 2)
                sp.dma_start(xn_rows[bass.ds(b * P, P), :], xn[:, :]).then_inc(xn_stored, 16)

            sp.sem_inc(x1_stored, 16)
            sp.sem_inc(xn_stored, 16)
            with sp.Fori(0, s.NB - 1) as b:
                sp.wait_ge(x1_ready, b + 2)
                sp.dma_start(xres[:, :], d.x_prompt[0, bass.ds((b + 1) * P, P), :]).then_inc(x_here, 16)
                store_x1(b)
                store_xn(b)
            sp.wait_ge(x1_ready, s.NB + 1)
            sp.dma_start(xres[0:s.TS, :], d.x_sample[0]).then_inc(x_here, 16)
            store_x1(s.NB - 1)
            store_xn(s.NB - 1)
            sp.wait_ge(x1_ready, s.NB + 2)
            store_x1(s.NB)
            store_xn(s.NB)
            sp.wait_ge(x1_stored, 16 * (BLOCKS + 1))
            sp.wait_ge(xn_stored, 16 * (BLOCKS + 1))

        @block.gpsimd
        def _(pool):
            chain = Chain(pool, pool_chain, held=pool_held)
            chain.link(nc.gpsimd.memset(mask[:, :], 0.0))
            nc.gpsimd.affine_select(out=mask[:, :], in_=mask[:, :], compare_op=ALU.is_ge, fill=MASKED,
                                    base=SPAN - P, pattern=[[-1, 2 * SPAN - P]], channel_multiplier=1).then_inc(consts, 1)
            nc.gpsimd.memset(q_aug[:, :, s.HD], 1.0)
            SETUP_LINKS, LINKS = chain.n, 4

            def stage(b, queries, conv, cum):
                chain.wait(qT_psum, b + 1)
                nc.gpsimd.tensor_copy(q_aug[:, :, 0:s.HD], queries.rearrange("p (h e) -> p h e", e=s.HD)).then_inc(q_staged, 1)
                chain.wait(top_ready, H * b + 1)
                nc.gpsimd.tensor_copy(cb[:, :], cum).then_inc(c_staged, 1)
                chain.wait(y_psum, b + 1)
                nc.gpsimd.tensor_copy(y_st[:, :, :], conv).then_inc(y_staged, 1)

            def layer_norm_scale(b):
                chain.wait(mv_ready, b + 1)
                chain.link(nc.gpsimd.tensor_scalar(var[:, :], mv[:, 1:2], LN_EPS, None, ALU.add))
                nc.gpsimd.tensor_tensor(out=lnr[:, :], in0=var[:, :], in1=g.neg_half[:, :], op=ALU.pow).then_inc(lnr_ready, 1)

            def rms_rows(b):
                chain.wait(ss_ready, b + 1)
                chain.link(nc.gpsimd.tensor_scalar(rms[:, 1:2], rms[:, 0:1], 1.0 / s.D, RMS_EPS, ALU.mult, ALU.add))
                chain.link(nc.gpsimd.tensor_tensor(out=rms[:, 2:3], in0=rms[:, 1:2], in1=g.neg_half[:, :], op=ALU.pow))
                chain.wait(xn_stored, 16 * (b + 1))
                chain.link(nc.gpsimd.tensor_scalar(xn[:, :], x1[:, :], rms[:, 2:3], None, ALU.mult))
                nc.gpsimd.tensor_tensor(out=xn[:, :], in0=xn[:, :], in1=gf[:, :], op=ALU.mult).then_inc(xn_ready, 1)

            pool.sem_inc(xn_ready, 1)
            pool.wait_ge(gf_here, 16)
            stage(0, c.queries[:, 0, :], c.convT[:, :, 0:P], c.cum[:, 0, :])
            with pool.Fori(0, s.NB) as b:
                chain.at(SETUP_LINKS + b * LINKS)
                layer_norm_scale(b)
                stage(b + 1, c.queries[:, bass.ds(b + 1, 1), :].rearrange("p a n -> p (a n)"),
                      c.convT[:, :, bass.ds((b + 1) * P, P)],
                      c.cum[:, bass.ds(b + 1, 1), :].rearrange("p a n -> p (a n)"))
                rms_rows(b)
                assert chain.n == LINKS
            chain.at(SETUP_LINKS + s.NB * LINKS)
            layer_norm_scale(s.NB)
            rms_rows(s.NB)

        @block.tensor
        def _(pe):
            for free in (qT_psum, y_psum):
                pe.sem_inc(free, 1)

            def body(b, nkb, kb0, mask_at):
                def scores_of(h):
                    width = min(nkb * P, BANK)
                    spans = range(0, nkb * P, BANK)
                    for i, at in enumerate(spans):
                        out = ps[:, S_ + 2 * (h % 2) + i, 0:width]
                        final = at == spans[-1]
                        ins = pe.matmul(out, qT[:, h, :], c.keysT[:, h, kb0 * P + at:kb0 * P + at + width],
                                        start=True, stop=not final)
                        if final:
                            ins = pe.matmul(out, g.ident[:, :], mask[:, bass.ds(mask_at(b), width)], start=False, stop=True)
                    ins.then_inc(s_psum, 1)

                def turn_probs(h):
                    pe.wait_ge(p_ready, 2 + H * b + h + 1)
                    for i in range(nkb):
                        ins = pe.transpose(ps[:, PT_ + i // 4, (i % 4) * P:(i % 4 + 1) * P],
                                           probs[:, h % 2, i * P:(i + 1) * P], g.ident[:, :])
                    ins.then_inc(pT_psum, 1)

                def weigh_values(h):
                    pe.wait_ge(pTa_ready, H * b + h + 1)
                    if nkb > HALF:
                        pe.wait_ge(pTd_ready, H * (b - HALF) + h + 1)
                    for i in range(nkb):
                        ins = pe.matmul(ps[:, O_, h * s.HD:(h + 1) * s.HD], probsT[:, i * P:(i + 1) * P],
                                        c.values[:, kb0 + i, h * s.HD:(h + 1) * s.HD], start=(i == 0), stop=(i == nkb - 1))
                    ins.then_inc(pv_psum, 1)

                pe.wait_ge(q_staged, b + 1)
                for h in range(H):
                    ins = pe.transpose(ps[0:s.HD + 1, PT_ + h // 4, (h % 4) * P:(h % 4 + 1) * P], q_aug[:, h, :], g.ident[:, :])
                ins.then_inc(qT_psum, 1)
                pe.wait_ge(consts, 1)
                pe.wait_ge(qT_ready, b + 1)
                scores_of(0)
                pe.wait_ge(x1_ready, b + 1)
                scores_of(1)
                pe.wait_ge(y_staged, b + 1)
                for i in range(s.CCH):
                    ins = pe.transpose(ps[:, T_, i * P:(i + 1) * P], y_st[:, i, :], g.ident[:, :])
                ins.then_inc(y_psum, 1)
                for h in range(H):
                    turn_probs(h)
                    if h + 2 < H:
                        scores_of(h + 2)
                    weigh_values(h)
                    if h == 0:
                        pe.wait_ge(z_ready, b + 1)
                        for i in range(s.CCH):
                            ins = pe.transpose(ps[:, T_, i * P:(i + 1) * P], z[:, i * P:(i + 1) * P], g.ident[:, :])
                        ins.then_inc(zT_psum, 1)
                pe.wait_ge(conv_ready, b + 2)
                pe.wait_ge(o_ready, b + 1)
                for i in range(s.CCH):
                    ins = pe.transpose(ps[:, T_, i * P:(i + 1) * P], o[:, i * P:(i + 1) * P], g.ident[:, :])
                ins.then_inc(oT_psum, 1)
                pe.wait_ge(w_here, 16)
                pe.wait_ge(oT_ready, b + 1)
                for half in range(s.D // BANK):
                    for i in range(s.DCH):
                        ins = pe.matmul(ps[:, X1_ + half, :], catT[:, i, :], w_out[:, i, half * BANK:(half + 1) * BANK],
                                        start=(i == 0), stop=(i == s.DCH - 1))
                ins.then_inc(x1_psum, 1)

            over_blocks(pe, body)

        @block.scalar
        def _(act):
            act.sem_inc(p_ready, 2)

            def body(b, nkb, kb0, mask_at):
                def exp(h):
                    act.wait_ge(top_ready, 1 + H * b + h + 1)
                    nc.scalar.activation(probs[:, h % 2, 0:nkb * P], scores[:, h % 2, 0:nkb * P], ACT.Exp,
                                         bias=ntop[:, h:h + 1], accum_out=rs[:, h:h + 1]).then_inc(p_ready, 1)

                act.wait_ge(qT_psum, b + 2)
                for i in range(2):
                    ins = nc.scalar.copy(qT[:, 4 * i:4 * i + 4, :], ps[0:s.HD + 1, PT_ + i, :].rearrange("p (h t) -> p h t", t=P))
                ins.then_inc(qT_ready, 1)
                exp(0)
                for h in range(H):
                    if h + 1 < H:
                        exp(h + 1)
                    act.wait_ge(pT_psum, H * b + h + 1)
                    width = min(nkb, 4) * P
                    nc.scalar.copy(probsT[:, 0:width], ps[:, PT_, 0:width]).then_inc(pTa_ready, 1)
                    if h == 1:
                        act.wait_ge(zT_psum, b + 1)
                        act.wait_ge(conv_ready, b + 1)
                        for i in range(s.CCH):
                            ins = nc.scalar.activation(sig[:, i, :], ps[:, T_, i * P:(i + 1) * P], ACT.Sigmoid,
                                                       bias=c.ln_b[:, i:i + 1], scale=c.ln_g[:, i:i + 1])
                        ins.then_inc(sig_ready, 1)
                act.wait_ge(oT_psum, b + 1)
                nc.scalar.copy(catT[:, 0:s.CCH, :], ps[:, T_, :].rearrange("p (c t) -> p c t", t=P)).then_inc(oT_ready, 1)

            over_blocks(act, body)

        @block.vector
        def _(dve):
            chain = Chain(dve, dve_chain)
            for free in (conv_ready, x1_ready, top_ready):
                dve.sem_inc(free, 1)
            LINKS = H + 3

            def body(b, nkb, kb0, mask_at):
                chain.at(b * LINKS)

                def row_max(h):
                    dve.wait_ge(s_psum, H * b + h + 1)
                    dve.wait_ge(p_ready, H * b + h + 1)
                    banks = ps[:, S_ + 2 * (h % 2):S_ + 2 * (h % 2) + 2, :].rearrange("p a n -> p (a n)")
                    chain.link(nc.vector.tensor_scalar(scores[:, h % 2, 0:nkb * P], banks[:, 0:nkb * P], cb[:, h:h + 1], None,
                                                       ALU.add, ALU.max, accum_out=top[:, h:h + 1]))
                    nc.vector.tensor_scalar(ntop[:, h:h + 1], top[:, h:h + 1], -1.0, None, ALU.mult).then_inc(top_ready, 1)

                dve.wait_ge(c_staged, b + 1)
                row_max(0)
                row_max(1)
                dve.wait_ge(y_psum, b + 2)
                chain.link(nc.vector.bn_stats(stats[:, :], ps[:, T_, :]))
                dve.sem_inc(dve_held, 1)
                nc.vector.bn_aggr(mv[:, :], stats[:, :]).then_inc(mv_ready, 1)
                dve.wait_ge(mv_ready, b + 1)
                dve.wait_ge(lnr_ready, b + 1)
                nc.vector.tensor_scalar(z[:, :], ps[:, T_, :], mv[:, 0:1], lnr[:, 0:1], ALU.subtract, ALU.mult).then_inc(z_ready, 1)
                for h in range(H):
                    if nkb > HALF:
                        dve.wait_ge(pT_psum, H * b + h + 1)
                        nc.vector.tensor_copy(probsT[:, BANK:nkb * P], ps[:, PT_ + 1, 0:nkb * P - BANK]).then_inc(pTd_ready, 1)
                    if h + 2 < H:
                        row_max(h + 2)
                    if h == 1:
                        dve.wait_ge(sig_ready, b + 1)
                        for i in range(s.CCH):
                            ins = nc.vector.tensor_scalar(yn[:, i, :], ps[:, T_, i * P:(i + 1) * P], c.ln_g[:, i:i + 1],
                                                          c.ln_b[:, i:i + 1], ALU.mult, ALU.add)
                        chain.link(ins)
                        nc.vector.tensor_tensor(out=catT[:, s.CCH:s.DCH, :], in0=yn[:, :, :], in1=sig[:, :, :],
                                                op=ALU.mult).then_inc(conv_ready, 1)
                dve.wait_ge(pv_psum, H * (b + 1))
                chain.link(nc.vector.reciprocal(rinv[:, :], rs[:, :]))
                nc.vector.tensor_tensor(out=o[:, :].rearrange("p (h e) -> p h e", e=s.HD),
                                        in0=ps[:, O_, :].rearrange("p (h e) -> p h e", e=s.HD),
                                        in1=rinv[:, :].unsqueeze(2).broadcast_to([P, H, s.HD]), op=ALU.mult).then_inc(o_ready, 1)
                dve.wait_ge(x1_psum, b + 1)
                dve.wait_ge(x_here, 16 * (b + 1))
                dve.wait_ge(x1_stored, 16 * (b + 1))
                dve.wait_ge(xn_ready, b + 1)
                nc.vector.tensor_tensor(out=x1[:, :], in0=ps[:, X1_:X1_ + 2, :].rearrange("p a n -> p (a n)"), in1=xres[:, :],
                                        op=ALU.add).then_inc(x1_ready, 1)
                dve.wait_ge(x1_ready, b + 2)
                nc.vector.tensor_tensor_reduce(out=sq[:, :], in0=x1[:, :], in1=x1[:, :], scale=1.0, scalar=0.0, op0=ALU.mult,
                                               op1=ALU.add, accum_out=rms[:, 0:1]).then_inc(ss_ready, 1)
                assert chain.n == LINKS

            over_blocks(dve, body)


def phase_c(nc, s, d, g):
    with ExitStack() as ctx:
        def sb(name, shape, dt=F32):
            return ctx.enter_context(nc.sbuf_tensor(name, shape, dt))

        def sem(name):
            return ctx.enter_context(nc.semaphore(name))

        K, PH = s.K, s.PH
        RING = 8
        DIAGS = 4
        AHEAD = 6
        PAIR = 2 * s.HALF
        NEG = -3.0e38

        w_pq = sb("w_pq_sb", [P, s.DCH, PH * PAIR])
        keysT = sb("sub_keysT", [P, 2, PH, s.NKEYS])
        xn_next = sb("xn_next", [P, s.D])
        xn = sb("xn_c", [P, s.D])
        xnT = sb("xnT_c", [P, s.DCH, P])
        u_rows = sb("u_rows", [P, RING, s.D])
        v_rows = sb("v_rows", [P, RING, s.D])
        keys = v_rows[:, 0:2, :].rearrange("p a n -> p (a n)").rearrange("p (x e) -> p x e", e=s.HALF)
        q = sb("q_c", [P, PAIR])
        qT = sb("qT_c", [P, 2, P])
        half_s = sb("half_scores", [P, 2, 2, s.NKEYS])
        left = sb("left_scores", [P, 2, s.NKEYS])
        top = sb("top_scores", [P, 2, K])
        top_i = sb("top_keys", [P, 2, K], U32)
        top_f = sb("top_keys_f", [P, 2, K])
        cand = sb("cand", [P, K, K])
        cand_left = sb("cand_left", [P, K, K])
        best = sb("best", [P, K])
        best_j = sb("best_j", [P, K], U32)
        ij = sb("best_ij", [P, 2, K], U32)
        ij_f = sb("best_ij_f", [P, 2, K])
        hit = sb("hit", [P, 2, K, K])
        key_f = sb("best_key_f", [P, 2, K])
        nbest = sb("neg_best", [P, 1])
        count = sb("count_to_k", [P, K])
        experts = sb("experts", [P, PH, K], U32)
        exps = sb("gate_exps", [P, PH, K])
        expsum = sb("gate_sums", [P, PH])
        gate_inv = sb("gate_inv", [P, 1])
        dots = sb("dots", [P, 2, K])
        gelu = sb("gelu_c", [P, 2, K])
        act_w = sb("act_c", [P, 2, K])
        diag = sb("diag", [P, DIAGS, P])
        zeros = sb("zeros_c", [P, BANK])
        out_rows = sb("out_rows", [P, s.D])

        w_here, keys_here, xn_here = sem("w_here_c"), sem("keys_here"), sem("xn_here")
        consts = sem("consts_c")
        keys_psum, keys_ready = sem("keys_psum"), sem("keys_ready")
        xn_moved, xnT_psum, xnT_ready = sem("xn_moved"), sem("xnT_psum"), sem("xnT_ready")
        q_psum, q_out, qT_psum, qT_out, s_psum, s_out, s_used = (
            sem(n + "_c") for n in ("q_psum", "q_out", "qT_psum", "qT_out", "s_psum", "s_out", "s_used"))
        best_ready, exps_ready, experts_ready = sem("best_ready"), sem("exps_ready"), sem("experts_ready")
        u_here = [sem(f"u_here{i}") for i in range(RING)]
        v_here = [sem(f"v_here{i}") for i in range(RING)]
        u_used, v_used = sem("u_used"), sem("v_used")
        gelu_ready, act_ready, diag_ready = sem("gelu_ready"), sem("act_ready"), sem("diag_ready")
        sum_psum, out_ready, out_stored = sem("sum_psum"), sem("out_ready"), sem("out_stored")
        dve_chain, dve_held, pool_held = sem("dve_chain_c"), sem("dve_held_c"), sem("pool_held_c")

        ps = g.ps
        ACC_, Q_, QT_, S_, XT_ = 0, 2, 3, 4, 5
        USES = K // RING
        U_FREE, V_FREE = RING, RING + K

        def head_pairs(eng, body):
            with eng.Fori(0, PH // 2) as j:
                for parity in range(2):
                    body(j * 2 + parity, parity)

        block = ctx.enter_context(nc.Block())

        @block.sync
        def _(sp):
            sp.dma_start(xn_next[:, :], d.xn2[0]).then_inc(xn_here, 16)
            for p in range(2):
                sp.dma_start(keys[:, p * PH:(p + 1) * PH, :], d.sub_keys[0, p].rearrange("h k e -> k h e")).then_inc(keys_here, 16)
            sp.dma_start(w_pq[:, :, :], d.w_pq[0].rearrange("(c p) n -> p c n", p=P)).then_inc(w_here, 16)
            sp.sem_inc(out_stored, 16)
            xn_rows = d.xn2.rearrange("b p n -> (b p) n")
            out_dram = d.peer.rearrange("b p n -> (b p) n")
            with sp.Fori(0, s.NB) as i:
                sp.wait_ge(xn_moved, i + 1)
                sp.wait_ge(xnT_psum, i + 1)
                sp.dma_start(xn_next[:, :], xn_rows[bass.ds((i + 1) * P, P), :]).then_inc(xn_here, 16)
                sp.wait_ge(out_ready, i + 2)
                sp.dma_start(out_dram[bass.ds(i * P, P), :], out_rows[:, :]).then_inc(out_stored, 16)
            sp.wait_ge(out_ready, s.NB + 2)
            sp.dma_start(d.peer[s.NB, 0:s.TS, :], out_rows[0:s.TS, :]).then_inc(out_stored, 16)
            sp.wait_ge(out_stored, 16 * (s.NB + 2))

        @block.gpsimd
        def _(pool):
            def wait(semaphore, value):
                pool.wait_ge(semaphore, value)
                pool.sem_inc(pool_held, 1)

            nc.gpsimd.memset(zeros[:, :], 0.0).then_inc(consts, 1)
            nc.gpsimd.iota(count[:, :], pattern=[[1, K]], base=0, channel_multiplier=0,
                           allow_small_or_imprecise_dtypes=True).then_inc(consts, 1)

            def gather(table, ring, here, used, free, n, h, k, rows):
                wait(used, free - RING + K * n + k + 1)
                nc.gpsimd.indirect_dma_start(
                    out=ring[0:rows, k % RING, :], out_offset=None, in_=table,
                    in_offset=bass.IndirectOffsetOnAxis(ap=experts[0:rows, h, k:k + 1], axis=0),
                ).then_inc(here[k % RING], 16)

            def gather_u(n, h, k, rows):
                gather(d.u_emb[0], u_rows, u_here, u_used, U_FREE, n, h, k, rows)

            def gather_v(n, h, k, rows):
                gather(d.v_emb[0], v_rows, v_here, v_used, V_FREE, n, h, k, rows)

            pool.wait_ge(experts_ready, 1)
            for k in range(K):
                gather_u(0, 0, k, P)
            with pool.Fori(0, s.NB) as i:
                for h in range(PH):
                    wait(experts_ready, i * PH + h + 2)
                    for k in range(K):
                        gather_u(i * PH + h + 1, (h + 1) % PH, k, P)
                        gather_v(i * PH + h, h, k, P)
            for h in range(PH):
                n = s.NB * PH + h
                for k in range(K):
                    if h + 1 < PH:
                        gather_u(n + 1, h + 1, k, s.TS)
                    gather_v(n, h, k, s.TS)

        @block.tensor
        def _(pe):
            pe.wait_ge(keys_here, 32)
            for x in range(2 * PH):
                ins = pe.transpose(ps[:, 2 + x // 4, (x % 4) * P:(x % 4 + 1) * P], keys[:, x, :], g.ident[:, :])
            ins.then_inc(keys_psum, 1)

            def turn_rows(b):
                pe.wait_ge(xn_here, 16 * (b + 1))
                for x in range(s.DCH):
                    ins = pe.transpose(ps[:, XT_ + x // 4, (x % 4) * P:(x % 4 + 1) * P], xn_next[:, x * P:(x + 1) * P], g.ident[:, :])
                ins.then_inc(xnT_psum, 1)

            def query(b, r, h):
                pe.wait_ge(xnT_ready, b + 1)
                for x in range(s.DCH):
                    ins = pe.matmul(ps[:, Q_, 0:PAIR], xnT[:, x, :], w_pq[:, x, bass.ds(h * PAIR, PAIR)],
                                    start=(x == 0), stop=(x == s.DCH - 1))
                ins.then_inc(q_psum, 1)

            def turn_query(r):
                pe.wait_ge(q_out, r + 1)
                for p in range(2):
                    ins = pe.transpose(ps[:, QT_, p * P:(p + 1) * P], q[:, p * P:(p + 1) * P], g.ident[:, :])
                ins.then_inc(qT_psum, 1)

            def score(r, h):
                pe.wait_ge(qT_out, r + 1)
                pe.wait_ge(s_out, r + 1)
                for p in range(2):
                    keys_h = keysT[:, p, bass.ds(h, 1), :].rearrange("p a k -> p (a k)")
                    ins = pe.matmul(ps[:, S_, p * P:(p + 1) * P], qT[:, p, :], keys_h, start=True, stop=True)
                ins.then_inc(s_psum, 1)

            def weigh(n, k, rows):
                pe.wait_ge(v_here[k % RING], 16 * (USES * n + k // RING + 1))
                pe.wait_ge(diag_ready, 2 * K + K * n + k + 1)
                for half in range(s.D // BANK):
                    ins = pe.matmul(ps[0:rows, ACC_ + half, :], diag[0:rows, k % DIAGS, 0:rows],
                                    v_rows[0:rows, k % RING, half * BANK:(half + 1) * BANK], start=False, stop=False)
                ins.then_inc(v_used, 1)

            def sums(rows, first):
                for half in range(s.D // BANK):
                    ins = pe.matmul(ps[0:rows, ACC_ + half, :], zeros[0:rows, 0:rows], zeros[0:rows, 0:BANK],
                                    start=first, stop=not first)
                return ins

            pe.sem_inc(v_used, V_FREE)
            pe.wait_ge(keys_ready, 1)
            turn_rows(0)
            pe.wait_ge(w_here, 16)

            def first_route(h, parity):
                query(0, h, h)
                turn_query(h)
                score(h, h)

            head_pairs(pe, first_route)
            pe.wait_ge(consts, 2)
            with pe.Fori(0, s.NB) as i:
                turn_rows(i + 1)
                pe.wait_ge(out_ready, i + 1)
                sums(P, True)

                def head(h, parity):
                    n = i * PH + h
                    for k in range(K):
                        weigh(n, k, P)
                        if k == 0:
                            query(i + 1, n + PH, h)
                        if k == 3:
                            turn_query(n + PH)
                        if k == 6:
                            score(n + PH, h)

                head_pairs(pe, head)
                sums(P, False).then_inc(sum_psum, 1)
            pe.wait_ge(out_ready, s.NB + 1)
            sums(s.TS, True)
            for h in range(PH):
                for k in range(K):
                    weigh(s.NB * PH + h, k, s.TS)
            sums(s.TS, False).then_inc(sum_psum, 1)

        @block.scalar
        def _(act):
            act.wait_ge(keys_psum, 1)
            for x in range(2 * PH // 4):
                dst = keysT[:, x // 2, 4 * (x % 2):4 * (x % 2) + 4, :]
                ins = nc.scalar.copy(dst, ps[:, 2 + x, :].rearrange("p (h k) -> p h k", k=s.NKEYS))
            ins.then_inc(keys_ready, 1)

            def rows_out(b):
                act.wait_ge(xnT_psum, b + 1)
                for x in range(2):
                    ins = nc.scalar.copy(xnT[:, 4 * x:4 * x + 4, :], ps[:, XT_ + x, :].rearrange("p (c t) -> p c t", t=P))
                ins.then_inc(xnT_ready, 1)

            def query_out(r):
                act.wait_ge(q_psum, r + 1)
                nc.scalar.copy(q[:, :], ps[:, Q_, 0:PAIR]).then_inc(q_out, 1)

            def turned_out(r):
                act.wait_ge(qT_psum, r + 1)
                nc.scalar.copy(qT[:, :, :], ps[:, QT_, 0:PAIR].rearrange("p (a t) -> p a t", t=P)).then_inc(qT_out, 1)

            def scores_out(r, parity):
                act.wait_ge(s_psum, r + 1)
                act.wait_ge(s_used, r + 1)
                nc.scalar.copy(half_s[:, parity, :, :], ps[:, S_, 0:2 * s.NKEYS].rearrange("p (a k) -> p a k", a=2)).then_inc(s_out, 1)

            def gate_exps(r, slot):
                act.wait_ge(best_ready, r + 1)
                nc.scalar.activation(exps[:, bass.ds(slot, 1), :].rearrange("p a k -> p (a k)"), best[:, :], ACT.Exp,
                                     bias=nbest[:, 0:1], accum_out=expsum[:, bass.ds(slot, 1)]).then_inc(exps_ready, 1)

            def gelus(n, parity, rows):
                act.wait_ge(u_used, U_FREE + K * (n + 1))
                act.wait_ge(act_ready, n + 1)
                nc.scalar.activation(gelu[0:rows, parity, :], dots[0:rows, parity, :], ACT.Gelu).then_inc(gelu_ready, 1)

            def diagonals(n, parity, ks, rows):
                for k in ks:
                    act.wait_ge(act_ready, n + 2)
                    act.wait_ge(v_used, V_FREE + K * n + k - DIAGS + 1)
                    nc.scalar.mul(diag[0:rows, k % DIAGS, 0:rows], g.ident[0:rows, 0:rows],
                                  act_w[0:rows, parity, k:k + 1]).then_inc(diag_ready, 1)

            act.sem_inc(s_out, 1)
            act.sem_inc(diag_ready, 2 * K)
            act.sem_inc(out_ready, 1)
            rows_out(0)
            with act.Fori(0, AHEAD // 2) as j:
                for parity in range(2):
                    r = j * 2 + parity
                    query_out(r)
                    turned_out(r)
                    scores_out(r, parity)
                    gate_exps(r, r)
            for r in range(AHEAD, PH):
                query_out(r)
                turned_out(r)
                scores_out(r, r % 2)
            with act.Fori(0, s.NB) as i:
                rows_out(i + 1)

                def head(h, parity):
                    n = i * PH + h
                    gelus(n, parity, P)
                    diagonals(n, parity, range(0, 3), P)
                    query_out(n + PH)
                    diagonals(n, parity, range(3, 6), P)
                    turned_out(n + PH)
                    gate_exps(n + AHEAD, (h + AHEAD) % PH)
                    diagonals(n, parity, range(6, 9), P)
                    scores_out(n + PH, parity)
                    diagonals(n, parity, range(9, K), P)

                head_pairs(act, head)
                act.wait_ge(sum_psum, i + 1)
                act.wait_ge(out_stored, 16 * (i + 1))
                nc.scalar.copy(out_rows[:, :], ps[:, ACC_:ACC_ + 2, :].rearrange("p a n -> p (a n)")).then_inc(out_ready, 1)
            for h in range(PH):
                n = s.NB * PH + h
                gelus(n, h % 2, s.TS)
                diagonals(n, h % 2, range(0, 6), s.TS)
                if h + AHEAD < PH:
                    gate_exps(n + AHEAD, h + AHEAD)
                diagonals(n, h % 2, range(6, K), s.TS)
            act.wait_ge(sum_psum, s.NB + 1)
            act.wait_ge(out_stored, 16 * (s.NB + 1))
            nc.scalar.copy(out_rows[0:s.TS, :], ps[0:s.TS, ACC_:ACC_ + 2, :].rearrange("p a n -> p (a n)")).then_inc(out_ready, 1)

        @block.vector
        def _(dve):
            chain = Chain(dve, dve_chain)

            def settle(ins):
                chain.link(ins)
                dve.sem_inc(dve_held, 1)

            def choose(r, parity, slot, refill=None):
                dve.wait_ge(s_out, r + 2)
                dve.sem_inc(dve_held, 1)
                sc = half_s[:, parity, :, :]
                for p in range(2):
                    ins = nc.vector.max(top[:, p, 0:8], sc[:, p, :])
                settle(ins)
                for p in range(2):
                    nc.vector.max_index(top_i[:, p, 0:8], top[:, p, 0:8], sc[:, p, :])
                for p in range(2):
                    ins = nc.vector.match_replace(left[:, p, :], top[:, p, 0:8], sc[:, p, :], NEG)
                ins.then_inc(s_used, 1)
                dve.wait_ge(s_used, 2 + r + 1)
                dve.sem_inc(dve_held, 1)
                for p in range(2):
                    ins = nc.vector.max(top[:, p, 8:K], left[:, p, :])
                settle(ins)
                for p in range(2):
                    ins = nc.vector.max_index(top_i[:, p, 8:K], top[:, p, 8:K], left[:, p, :])
                nc.vector.tensor_tensor(out=cand[:, :, :], in0=top[:, 0, :].unsqueeze(2).broadcast_to([P, K, K]),
                                        in1=top[:, 1, :].unsqueeze(1).broadcast_to([P, K, K]), op=ALU.add).then_inc(dve_chain, 1)
                chain.n += 1
                dve.wait_ge(dve_chain, chain.base + chain.n)
                chain.link(nc.vector.tensor_copy(top_f[:, :, :], top_i[:, :, :]))
                dve.wait_ge(exps_ready, r + 1)
                dve.sem_inc(dve_held, 1)
                flat, flat_left = (t[:, :, :].rearrange("p a b -> p (a b)") for t in (cand, cand_left))
                settle(nc.vector.max(best[:, 0:8], flat))
                nc.vector.max_index(best_j[:, 0:8], best[:, 0:8], flat)
                settle(nc.vector.match_replace(flat_left, best[:, 0:8], flat, NEG))
                settle(nc.vector.max(best[:, 8:K], flat_left))
                settle(nc.vector.max_index(best_j[:, 8:K], best[:, 8:K], flat_left))
                nc.vector.tensor_scalar(nbest[:, :], best[:, 0:1], -1.0, None, ALU.mult).then_inc(best_ready, 1)
                nc.vector.tensor_scalar(ij[:, 0, :], best_j[:, :], 4, None, ALU.logical_shift_right)
                chain.link(nc.vector.tensor_scalar(ij[:, 1, :], best_j[:, :], K - 1, None, ALU.bitwise_and))
                chain.link(nc.vector.tensor_copy(ij_f[:, :, :], ij[:, :, :]))
                chain.link(nc.vector.tensor_tensor(out=hit[:, :, :, :], in0=ij_f[:, :, :].unsqueeze(3).broadcast_to([P, 2, K, K]),
                                                   in1=count[:, :].unsqueeze(1).unsqueeze(1).broadcast_to([P, 2, K, K]), op=ALU.is_equal))
                chain.link(nc.vector.tensor_tensor(out=hit[:, :, :, :], in0=hit[:, :, :, :],
                                                   in1=top_f[:, :, :].unsqueeze(2).broadcast_to([P, 2, K, K]), op=ALU.mult))
                chain.link(nc.vector.tensor_reduce(key_f[:, :, :], hit[:, :, :, :], AX.X, ALU.add))
                if refill is not None:
                    dve.wait_ge(v_used, V_FREE + K * (refill - 1))
                nc.vector.scalar_tensor_tensor(out=experts[:, bass.ds(slot, 1), :].rearrange("p a k -> p (a k)"), in0=key_f[:, 0, :],
                                               scalar=float(s.NKEYS), in1=key_f[:, 1, :], op0=ALU.mult,
                                               op1=ALU.add).then_inc(experts_ready, 1)

            def dot(n, parity, rows):
                for k in range(K):
                    dve.wait_ge(u_here[k % RING], 16 * (USES * n + k // RING + 1))
                    row = u_rows[0:rows, k % RING, :]
                    nc.vector.tensor_tensor_reduce(out=row, in0=row, in1=xn[0:rows, :], scale=1.0, scalar=0.0, op0=ALU.mult,
                                                   op1=ALU.add, accum_out=dots[0:rows, parity, k:k + 1]).then_inc(u_used, 1)

            def weights(n, parity, h, rows):
                dve.wait_ge(exps_ready, n + 2)
                chain.link(nc.vector.reciprocal(gate_inv[0:rows, :], expsum[0:rows, bass.ds(h, 1)]))
                dve.wait_ge(gelu_ready, n + 1)
                dve.wait_ge(diag_ready, K * n + K)
                nc.vector.scalar_tensor_tensor(out=act_w[0:rows, parity, :], in0=gelu[0:rows, parity, :], scalar=gate_inv[0:rows, 0:1],
                                               in1=exps[0:rows, bass.ds(h, 1), :].rearrange("p a k -> p (a k)"),
                                               op0=ALU.mult, op1=ALU.mult).then_inc(act_ready, 1)

            def take_rows(b):
                dve.wait_ge(xn_here, 16 * (b + 1))
                dve.wait_ge(u_used, U_FREE + b * PH * K)
                nc.vector.tensor_copy(xn[:, :], xn_next[:, :]).then_inc(xn_moved, 1)
                dve.wait_ge(xn_moved, b + 1)
                dve.sem_inc(dve_held, 1)

            dve.sem_inc(u_used, U_FREE)
            dve.sem_inc(s_used, 2)
            dve.sem_inc(act_ready, 1)
            dve.sem_inc(exps_ready, 1)
            dve.wait_ge(consts, 2)
            CHOOSE = 13
            with dve.Fori(0, AHEAD // 2) as j:
                for parity in range(2):
                    r = j * 2 + parity
                    chain.at(r * CHOOSE)
                    choose(r, parity, r)
                    assert chain.n == CHOOSE, chain.n
            with dve.Fori(0, s.NB) as i:
                take_rows(i)

                def head(h, parity):
                    n = i * PH + h
                    dot(n, parity, P)
                    chain.at(AHEAD * CHOOSE + n * (CHOOSE + 1))
                    weights(n, parity, h, P)
                    choose(n + AHEAD, parity, (h + AHEAD) % PH, refill=n)

                head_pairs(dve, head)
            take_rows(s.NB)
            chain.at(AHEAD * CHOOSE + s.NB * PH * (CHOOSE + 1))
            for h in range(PH):
                n = s.NB * PH + h
                dot(n, h % 2, s.TS)
                weights(n, h % 2, h, s.TS)
                if h + AHEAD < PH:
                    choose(n + AHEAD, h % 2, h + AHEAD, refill=n)


def phase_d(nc, s, d, g):
    with ExitStack() as ctx:
        def sb(name, shape):
            return ctx.enter_context(nc.sbuf_tensor(name, shape, F32))

        def sem(name):
            return ctx.enter_context(nc.semaphore(name))

        x1, peer, y, sq = (sb(n + "_d", [P, 2, s.D]) for n in ("x1", "peer", "y", "sq"))
        gf = sb("g_final_rows", [P, s.D])
        rms = sb("rms_d", [P, 2, 3])
        gf_here = sem("gf_here_d")
        x1_here = [sem(f"x1_here_d{i}") for i in range(2)]
        peer_here = [sem(f"peer_here_d{i}") for i in range(2)]
        y_stored = [sem(f"y_stored{i}") for i in range(2)]
        y_ready, ms_ready, rstd_ready = (sem(n + "_d") for n in ("y_ready", "ms_ready", "rstd_ready"))
        dve_chain = sem("dve_chain_d")
        BLOCKS = s.NB + 1
        rows_of = lambda b: P if b < s.NB else s.TS

        block = ctx.enter_context(nc.Block())

        @block.sync
        def _(sp):
            def load(b):
                n = rows_of(b)
                if b >= 2:
                    sp.wait_ge(y_ready, b - 1)
                sp.dma_start(x1[0:n, b % 2, :], d.x1[b, 0:n, :]).then_inc(x1_here[b % 2], 16)
                sp.dma_start(peer[0:n, b % 2, :], d.peer[b, 0:n, :]).then_inc(peer_here[b % 2], 16)

            load(0)
            sp.dma_start(gf[:, :], d.g_final.partition_broadcast(P)).then_inc(gf_here, 16)
            load(1)
            for b in range(BLOCKS):
                n = rows_of(b)
                sp.wait_ge(y_ready, b + 1)
                dst = d.y_prompt[0, b * P:(b + 1) * P, :] if b < s.NB else d.y_sample[0]
                sp.dma_start(dst, y[0:n, b % 2, :]).then_inc(y_stored[b % 2], 16)
                if b + 2 < BLOCKS:
                    load(b + 2)
            for i in range(2):
                sp.wait_ge(y_stored[i], 16 * ((BLOCKS + 1 - i) // 2))

        @block.gpsimd
        def _(pool):
            for b in range(BLOCKS):
                n = rows_of(b)
                pool.wait_ge(ms_ready, b + 1)
                nc.gpsimd.tensor_tensor(out=rms[0:n, b % 2, 2:3], in0=rms[0:n, b % 2, 1:2], in1=g.neg_half[0:n, :],
                                        op=ALU.pow).then_inc(rstd_ready, 1)

        @block.vector
        def _(dve):
            chain = Chain(dve, dve_chain)

            def sums(b):
                n, i = rows_of(b), b % 2
                dve.wait_ge(x1_here[i], 16 * (b // 2 + 1))
                dve.wait_ge(peer_here[i], 16 * (b // 2 + 1))
                if b >= 2:
                    dve.wait_ge(y_ready, b - 1)
                chain.link(nc.vector.tensor_tensor(out=x1[0:n, i, :], in0=x1[0:n, i, :], in1=peer[0:n, i, :], op=ALU.add))
                chain.link(nc.vector.tensor_tensor_reduce(out=sq[0:n, i, :], in0=x1[0:n, i, :], in1=x1[0:n, i, :], scale=1.0, scalar=0.0,
                                                          op0=ALU.mult, op1=ALU.add, accum_out=rms[0:n, i, 0:1]))
                nc.vector.tensor_scalar(rms[0:n, i, 1:2], rms[0:n, i, 0:1], 1.0 / s.D, RMS_EPS, ALU.mult, ALU.add).then_inc(ms_ready, 1)

            def scale(b):
                n, i = rows_of(b), b % 2
                dve.wait_ge(rstd_ready, b + 1)
                if b >= 2:
                    dve.wait_ge(y_stored[i], 16 * (b // 2))
                nc.vector.scalar_tensor_tensor(out=y[0:n, i, :], in0=x1[0:n, i, :], scalar=rms[0:n, i, 2:3], in1=gf[0:n, :],
                                               op0=ALU.mult, op1=ALU.mult).then_inc(y_ready, 1)

            dve.wait_ge(gf_here, 16)
            sums(0)
            for b in range(BLOCKS):
                if b + 1 < BLOCKS:
                    sums(b + 1)
                scale(b)


INPUTS = ["x_prompt", "x_sample", "cache_k", "cache_v", "cache_logf", "state_conv", "g_mix", "w_in", "b_f", "w_dw",
          "b_dw", "ln_g", "ln_b", "w_out", "g_ffn", "w_pq", "sub_keys", "u_emb", "v_emb", "g_final"]


def kernel(**inputs):
    import concourse.bacc as bacc
    from concourse.bass_utils import run_bass_kernel_spmd

    nc = bacc.Bacc("TRN2", target_bir_lowering=False, num_devices=1)
    arrays, args = {}, []
    for name in INPUTS:
        a = np.ascontiguousarray(inputs[name])
        arrays["in_" + name] = a
        args.append(nc.dram_tensor("in_" + name, a.shape, mybir.dt.from_np(a.dtype), kind="ExternalInput").ap())
    x_p, x_s, ck = (inputs[n].shape for n in ("x_prompt", "x_sample", "cache_k"))
    depth, heads, hd = ck[0], ck[3], ck[4]
    conv = inputs["state_conv"].shape[2:]
    outs = [x_p, x_s,
            (depth, *x_p[:2], heads, hd), (depth, *x_p[:2], heads, hd), (depth, *x_p[:2], heads), (depth, x_p[0], *conv),
            (depth, *x_s[:2], heads, hd), (depth, *x_s[:2], heads, hd), (depth, *x_s[:2], heads), (depth, x_s[0], *conv)]
    for i, shape in enumerate(outs):
        args.append(nc.dram_tensor(f"out_{i}", shape, F32, kind="ExternalOutput").ap())
    build(nc, *args)
    r = run_bass_kernel_spmd(nc, [arrays], core_ids=[0])
    return tuple(r.results[0][f"out_{i}"] for i in range(len(outs)))
```

```python
from contextlib import ExitStack

import numpy as np
import concourse.bass as bass
from concourse import mybir

F32 = mybir.dt.float32
U32 = mybir.dt.uint32
ALU = mybir.AluOpType
ACT = mybir.ActivationFunctionType
AX = mybir.AxisListType

P = 128
BANK = 512
MASKED = -1e30
RMS_EPS = 1e-6
LN_EPS = 1e-5


class Named:
    pass


class Chain:

    def __init__(self, eng, sem, base=0, held=None):
        self.eng, self.sem, self.base, self.n, self.held = eng, sem, base, 0, held

    def wait(self, sem, value):
        self.eng.wait_ge(sem, value)
        if self.held is not None:
            self.eng.sem_inc(self.held, 1)

    def link(self, ins):
        ins.then_inc(self.sem, 1)
        self.n += 1
        self.wait(self.sem, self.base + self.n)

    def at(self, base):
        self.base, self.n = base, 0
        return self


def sizes(x_prompt, x_sample, cache_k, w_in, w_dw, w_pq, sub_keys, u_emb):
    s = Named()
    s.D = x_prompt.shape[2]
    s.T = x_prompt.shape[1]
    s.TS = x_sample.shape[1]
    s.PAST, s.H, s.HD = cache_k.shape[2:]
    s.DA = s.H * s.HD
    s.TAPS, s.DC = w_dw.shape[1:]
    s.NIN = w_in.shape[2]
    s.DCH = s.D // P
    s.CCH = s.DC // P
    s.NB = s.T // P
    s.SAMPLE_KB = s.NB + 1
    s.NKB = s.NB + 2
    s.PH = sub_keys.shape[2]
    s.NKEYS = sub_keys.shape[3]
    s.HALF = sub_keys.shape[4]
    s.K = 16
    s.E = u_emb.shape[1]
    assert s.PAST == P and s.HALF == P and s.NKEYS == P and s.TS == P // 2 and s.H == 8 and s.PH == 8
    return s


def build(nc, x_prompt, x_sample, cache_k, cache_v, cache_logf, state_conv, g_mix, w_in, b_f, w_dw, b_dw,
          ln_g, ln_b, w_out, g_ffn, w_pq, sub_keys, u_emb, v_emb, g_final,
          y_prompt, y_sample, k_prompt, v_prompt, logf_prompt, conv_prompt,
          k_sample, v_sample, logf_sample, conv_sample):
    s = sizes(x_prompt, x_sample, cache_k, w_in, w_dw, w_pq, sub_keys, u_emb)
    d = Named()
    d.x_prompt, d.x_sample, d.cache_k, d.cache_v, d.cache_logf, d.state_conv = x_prompt, x_sample, cache_k, cache_v, cache_logf, state_conv
    d.g_mix, d.w_in, d.b_f, d.w_dw, d.b_dw, d.ln_g = g_mix, w_in, b_f, w_dw, b_dw, ln_g
    d.ln_b, d.w_out, d.g_ffn, d.w_pq, d.sub_keys, d.u_emb = ln_b, w_out, g_ffn, w_pq, sub_keys, u_emb
    d.v_emb, d.g_final, d.k_prompt, d.v_prompt, d.logf_prompt, d.conv_prompt = v_emb, g_final, k_prompt, v_prompt, logf_prompt, conv_prompt
    d.k_sample, d.v_sample, d.logf_sample, d.conv_sample, d.y_prompt, d.y_sample = k_sample, v_sample, logf_sample, conv_sample, y_prompt, y_sample
    d.x1 = nc.dram_tensor("x1_rows", (s.NB + 1, P, s.D), F32, kind="Internal").ap()
    d.xn2 = nc.dram_tensor("xn2_rows", (s.NB + 1, P, s.D), F32, kind="Internal").ap()
    with ExitStack() as ctx:
        g = Named()
        g.ident = ctx.enter_context(nc.sbuf_tensor("ident", [P, P], F32))
        g.neg_half = ctx.enter_context(nc.sbuf_tensor("neg_half", [P, 1], F32))
        g.ps = ctx.enter_context(nc.psum_tensor("ps", [P, 8, BANK], F32))
        with ExitStack() as mix:
            c = caches(nc, s, mix)
            phase_a(nc, s, d, g, c)
            phase_b(nc, s, d, g, c)
        phase_c(nc, s, d, g)


def caches(nc, s, ctx):
    c = Named()

    def sb(name, shape):
        return ctx.enter_context(nc.sbuf_tensor(name, shape, F32))

    c.keysT = sb("keysT", [s.HD + 1, s.H, s.NKB * P])
    c.values = sb("values", [P, s.NKB, s.DA])
    c.queries = sb("queries", [P, s.NB + 1, s.DA])
    c.convT = sb("convT", [P, s.CCH, (s.NB + 1) * P])
    c.cum = sb("cum", [P, s.NB + 1, s.H])
    c.vecT = sb("vecT", [P, s.DCH + 3 * s.CCH])
    c.g_mix = c.vecT[:, 0:s.DCH]
    c.b_dw, c.ln_g, c.ln_b = (c.vecT[:, s.DCH + i * s.CCH:s.DCH + (i + 1) * s.CCH] for i in range(3))
    return c


def phase_a(nc, s, d, g, c):
    with ExitStack() as ctx:
        def sb(name, shape):
            return ctx.enter_context(nc.sbuf_tensor(name, shape, F32))

        def sem(name):
            return ctx.enter_context(nc.semaphore(name))

        COLS = {}
        at = 0
        for name, width in (("q", s.DA), ("k", s.DA), ("v", s.DA), ("f", s.H), ("a", s.DC), ("gate", s.DC)):
            COLS[name] = (at, width)
            at += width
        ORDER = ("gate", "a", "f", "q", "k", "v")
        NPROJ = len(ORDER)
        HALO = s.TAPS - 1

        w_in = sb("w_in_sb", [P, s.DCH, s.NIN])
        x = sb("x_a", [P, s.D])
        xn = sb("xn_a", [P, s.D])
        hT = sb("hT_a", [P, s.DCH, P])
        k_aug = sb("k_aug", [P, s.H, s.HD + 1])
        sig = sb("sig_a", [P, s.DC])
        u = sb("u_a", [P, s.DC])
        uT = sb("uT_a", [P, s.CCH, HALO + P])
        upto = sb("upto", [P, P])
        last_row = sb("last_row", [P, P])
        bf = sb("bf_rows", [P, s.H])
        ss = sb("ss_a", [P, 1])
        ms = sb("ms_a", [P, 1])
        rstd = sb("rstd_a", [P, 1])
        z = sb("z_a", [P, s.H])
        az = sb("az_a", [P, s.H])
        ez = sb("ez_a", [P, s.H])
        ln = sb("ln_a", [P, s.H])
        pz = sb("pz_a", [P, 4, s.H])
        logf = sb("logf_a", [P, s.H])
        logfs = sb("logfs", [P, s.NB + 1, s.H])
        cum = sb("cum_a", [P, s.H])
        cum_past = sb("cum_past", [P, s.H])
        logf_past = sb("logf_past", [P, s.H])
        taps = sb("taps", [s.TAPS, s.DC])
        tapsT = sb("tapsT", [P, s.CCH, s.TAPS])
        NVEC = s.DCH + 3 * s.CCH
        vecs = sb("vecs", [NVEC, P])
        state = sb("state", [HALO, s.DC])
        stateT = sb("stateT", [P, s.CCH, HALO])

        w_here = {n: sem("w_here_" + n) for n in ORDER}
        x_here = sem("x_here_a")
        small_here = sem("small_here")
        past_here = sem("past_here")
        consts = sem("consts_a")
        setup_psum = sem("setup_psum")
        setup_sb = sem("setup_sb")
        ms_ready = sem("ms_ready_a")
        rstd_ready = sem("rstd_ready_a")
        xn_ready = sem("xn_ready_a")
        hT_psum = sem("hT_psum_a")
        hT_ready = sem("hT_ready_a")
        proj_psum = sem("proj_psum")
        sig_ready = sem("sig_ready_a")
        u_ready = sem("u_ready")
        uT_psum = sem("uT_psum")
        uT_ready = sem("uT_ready")
        z_ready = sem("z_ready")
        ez_ready = sem("ez_ready")
        ln_ready = sem("ln_ready")
        logf_ready = sem("logf_ready")
        cum_psum = sem("cum_psum")
        cum_ready = sem("cum_ready")
        kaug_ready = sem("kaug_ready")
        q_ready = sem("q_ready_a")
        k_ready = sem("k_ready")
        v_ready = sem("v_ready")
        kT_psum = sem("kT_psum")
        kT_ready = sem("kT_ready")
        k_stored = sem("k_stored")
        v_stored = sem("v_stored")
        misc_stored = sem("misc_stored")
        act_chain, dve_chain, pool_chain = sem("act_chain_a"), sem("dve_chain_a"), sem("pool_chain_a")
        pool_held = sem("pool_held_a")

        ps = g.ps
        BLOCKS = s.NB + 1
        HB, GATE, A_, F_, Q_, K_, V_ = 0, 2, 3, 4, 5, 6, 7
        BANK_OF = {"gate": GATE, "a": A_, "f": F_, "q": Q_, "k": K_, "v": V_}
        KTB, UTB = 2, 0
        PAST = 1

        block = ctx.enter_context(nc.Block())

        @block.sync
        def _(sp):
            sp.dma_start(x[:, :], d.x_prompt[0, 0:P, :]).then_inc(x_here, 16)
            sp.dma_start(vecs[0:s.DCH, :], d.g_mix[0].rearrange("(c p) -> c p", p=P)).then_inc(small_here, 16)
            for i, v in enumerate((d.b_dw, d.ln_g, d.ln_b)):
                lo = s.DCH + i * s.CCH
                sp.dma_start(vecs[lo:lo + s.CCH, :], v[0].rearrange("(c p) -> c p", p=P)).then_inc(small_here, 16)
            sp.dma_start(taps[:, :], d.w_dw[0]).then_inc(small_here, 16)
            sp.dma_start(state[:, :], d.state_conv[0, 0]).then_inc(small_here, 16)
            sp.dma_start(bf[:, :], d.b_f[0].partition_broadcast(P)).then_inc(small_here, 16)
            sp.dma_start(k_aug[:, :, 0:s.HD], d.cache_k[0, 0]).then_inc(past_here, 16)
            sp.dma_start(logf_past[:, :], d.cache_logf[0, 0]).then_inc(past_here, 16)
            sp.dma_start(c.values[:, s.NB, :], d.cache_v[0, 0].rearrange("t h e -> t (h e)")).then_inc(past_here, 16)
            w_rows = d.w_in[0].rearrange("(c p) n -> p c n", p=P)
            for name in ORDER:
                lo, width = COLS[name]
                sp.dma_start(w_in[:, :, lo:lo + width], w_rows[:, :, lo:lo + width]).then_inc(w_here[name], 16)

            def stores(b, kb, k_out, v_out, rows):
                sp.wait_ge(k_ready, b + 2)
                sp.dma_start(k_out, k_aug[0:rows, :, 0:s.HD]).then_inc(k_stored, 16)
                sp.wait_ge(v_ready, b + 2)
                sp.dma_start(v_out, c.values[0:rows, kb, :]).then_inc(v_stored, 16)

            def prompt_stores(b):
                if isinstance(b, int):
                    v = c.values[:, b, :]
                else:
                    v = c.values[:, bass.ds(b, 1), :].rearrange("p a n -> p (a n)")
                sp.wait_ge(k_ready, b + 2)
                sp.dma_start(k_rows[bass.ds(b * P, P)], k_aug[:, :, 0:s.HD]).then_inc(k_stored, 16)
                sp.wait_ge(v_ready, b + 2)
                sp.dma_start(v_rows[bass.ds(b * P, P), :], v).then_inc(v_stored, 16)

            sp.sem_inc(k_stored, 16)
            k_rows = d.k_prompt[0, 0]
            v_rows = d.v_prompt[0, 0].rearrange("t h e -> t (h e)")
            with sp.Fori(0, s.NB - 1) as b:
                sp.wait_ge(xn_ready, b + 1)
                sp.dma_start(x[:, :], d.x_prompt[0, bass.ds((b + 1) * P, P), :]).then_inc(x_here, 16)
                prompt_stores(b)
            sp.wait_ge(xn_ready, s.NB)
            sp.dma_start(x[0:s.TS, :], d.x_sample[0]).then_inc(x_here, 16)
            prompt_stores(s.NB - 1)
            sp.wait_ge(u_ready, 1 + s.NB)
            sp.dma_start(d.conv_prompt[0, 0], u[P - HALO:P, :]).then_inc(misc_stored, 16)
            stores(s.NB, s.SAMPLE_KB, d.k_sample[0, 0], d.v_sample[0, 0].rearrange("t h e -> t (h e)"), s.TS)
            sp.wait_ge(u_ready, 1 + BLOCKS)
            sp.dma_start(d.conv_sample[0, 0], u[s.TS - HALO:s.TS, :]).then_inc(misc_stored, 16)
            sp.wait_ge(logf_ready, 1 + 2 * BLOCKS)
            sp.dma_start(d.logf_prompt[0, 0].rearrange("(b p) h -> p b h", p=P), logfs[:, 0:s.NB, :]).then_inc(misc_stored, 16)
            sp.dma_start(d.logf_sample[0, 0], logfs[0:s.TS, s.NB, :]).then_inc(misc_stored, 16)
            sp.wait_ge(k_stored, 16 * (1 + BLOCKS))
            sp.wait_ge(v_stored, 16 * BLOCKS)
            sp.wait_ge(misc_stored, 64)

        @block.gpsimd
        def _(pool):
            chain = Chain(pool, pool_chain, held=pool_held)
            chain.link(nc.gpsimd.memset(g.ident[:, :], 0.0))
            nc.gpsimd.affine_select(out=g.ident[:, :], in_=g.ident[:, :], compare_op=ALU.not_equal, fill=1.0,
                                    base=0, pattern=[[-1, P]], channel_multiplier=1).then_inc(consts, 1)
            nc.gpsimd.memset(g.neg_half[:, :], -0.5)
            chain.link(nc.gpsimd.memset(upto[:, :], 1.0))
            nc.gpsimd.affine_select(out=upto[:, :], in_=upto[:, :], compare_op=ALU.is_ge, fill=0.0,
                                    base=0, pattern=[[1, P]], channel_multiplier=-1).then_inc(consts, 1)
            chain.link(nc.gpsimd.memset(last_row[:, :], 0.0))
            nc.gpsimd.affine_select(out=last_row[:, :], in_=last_row[:, :], compare_op=ALU.not_equal, fill=1.0,
                                    base=1 - P, pattern=[[0, P]], channel_multiplier=1).then_inc(consts, 1)
            pool.wait_ge(past_here, 48)
            pool.wait_ge(cum_ready, 1)
            nc.gpsimd.tensor_scalar(k_aug[:, :, s.HD], cum_past[:, :], -1.0, None, ALU.mult).then_inc(kaug_ready, 1)
            SETUP_LINKS = chain.n
            LINKS = 3

            def rms_scale(b):
                chain.wait(ms_ready, b + 1)
                nc.gpsimd.tensor_tensor(out=rstd[:, :], in0=ms[:, :], in1=g.neg_half[:, :], op=ALU.pow).then_inc(rstd_ready, 1)

            def log_forget(b, blk):
                chain.wait(ez_ready, b + 1)
                chain.link(nc.gpsimd.tensor_scalar(pz[:, 0, :], ez[:, :], 1.0, -1.0, ALU.add, ALU.add))
                nc.gpsimd.tensor_tensor(out=pz[:, 1, :], in0=ez[:, :], in1=pz[:, 0, :], op=ALU.subtract)
                chain.wait(ln_ready, b + 1)
                chain.link(nc.gpsimd.tensor_scalar(pz[:, 3, :], z[:, :], 0.0, None, ALU.min))
                chain.link(nc.gpsimd.tensor_tensor(out=pz[:, 2, :], in0=ln[:, :], in1=pz[:, 1, :], op=ALU.add))
                chain.wait(cum_psum, b + 1)
                nc.gpsimd.tensor_tensor(out=logf[:, :], in0=pz[:, 3, :], in1=pz[:, 2, :], op=ALU.subtract).then_inc(logf_ready, 1)
                chain.wait(logf_ready, 2 * b + 2)
                nc.gpsimd.tensor_copy(blk(logfs), logf[:, :]).then_inc(logf_ready, 1)

            def cum_columns(b, blk):
                chain.wait(cum_ready, PAST + b + 1)
                nc.gpsimd.tensor_copy(blk(c.cum), cum[:, :])
                chain.wait(kT_psum, PAST + b)
                nc.gpsimd.tensor_scalar(k_aug[:, :, s.HD], cum[:, :], -1.0, None, ALU.mult).then_inc(kaug_ready, 1)

            pool.sem_inc(logf_ready, 1)
            rms_scale(0)
            with pool.Fori(0, s.NB) as b:
                chain.at(SETUP_LINKS + b * LINKS)
                blk = lambda t: t[:, bass.ds(b, 1), :].rearrange("p a n -> p (a n)")
                rms_scale(b + 1)
                log_forget(b, blk)
                cum_columns(b, blk)
                assert chain.n == LINKS
            chain.at(SETUP_LINKS + s.NB * LINKS)
            log_forget(s.NB, lambda t: t[:, s.NB, :])
            cum_columns(s.NB, lambda t: t[:, s.NB, :])

        @block.scalar
        def _(act):
            chain = Chain(act, act_chain)
            act.wait_ge(setup_psum, 3)
            nc.scalar.copy(tapsT[:, :, :], ps[:, Q_, 0:s.CCH * s.TAPS].rearrange("p (c j) -> p c j", c=s.CCH)).then_inc(setup_sb, 1)
            nc.scalar.copy(c.vecT[:, :], ps[:, K_, 0:NVEC]).then_inc(setup_sb, 1)
            nc.scalar.copy(stateT[:, :, :], ps[:, V_, 0:s.CCH * HALO].rearrange("p (c j) -> p c j", c=s.CCH)).then_inc(setup_sb, 1)
            act.wait_ge(cum_psum, 1)
            nc.scalar.copy(cum_past[:, :], ps[:, F_, s.H:2 * s.H]).then_inc(cum_ready, 1)

            def keys_out(kcount, kb):
                act.wait_ge(kT_psum, kcount)
                for i in range(2):
                    src = ps[0:s.HD + 1, KTB + i, :].rearrange("p (h t) -> p h t", t=P)
                    ins = nc.scalar.copy(c.keysT[:, 4 * i:4 * i + 4, bass.ds(kb * P, P)], src)
                ins.then_inc(kT_ready, 1)

            def row_scale(b):
                act.wait_ge(x_here, 16 * (b + 1))
                chain.link(nc.scalar.activation(xn[:, :], x[:, :], ACT.Square, accum_out=ss[:, :]))
                nc.scalar.activation(ms[:, :], ss[:, :], ACT.Copy, bias=RMS_EPS, scale=1.0 / s.D).then_inc(ms_ready, 1)

            def normed(b):
                act.wait_ge(rstd_ready, b + 1)
                nc.scalar.mul(xn[:, :], x[:, :], rstd[:, 0:1]).then_inc(xn_ready, 1)

            def iteration(b, kb, q_dst, v_dst, prepare_next):
                act.wait_ge(hT_psum, 2 * b + 2)
                act.wait_ge(setup_sb, 2)
                for i in range(s.DCH):
                    ins = nc.scalar.mul(hT[:, i, :], ps[:, HB + i // 4, (i % 4) * P:(i % 4 + 1) * P], c.g_mix[:, i:i + 1])
                ins.then_inc(hT_ready, 1)
                if prepare_next:
                    row_scale(b + 1)
                act.wait_ge(proj_psum, NPROJ * b + 1)
                act.wait_ge(u_ready, b + 1)
                nc.scalar.activation(sig[:, :], ps[:, GATE, :], ACT.Sigmoid).then_inc(sig_ready, 1)
                if prepare_next:
                    normed(b + 1)
                act.wait_ge(z_ready, b + 1)
                act.wait_ge(logf_ready, 2 * b + 1)
                chain.link(nc.scalar.activation(az[:, :], z[:, :], ACT.Abs))
                nc.scalar.activation(ez[:, :], az[:, :], ACT.Exp, scale=-1.0).then_inc(ez_ready, 1)
                act.wait_ge(ez_ready, b + 1)
                nc.scalar.activation(ln[:, :], ez[:, :], ACT.Ln, bias=1.0).then_inc(ln_ready, 1)
                act.wait_ge(proj_psum, NPROJ * b + 4)
                nc.scalar.mul(q_dst, ps[:, Q_, :], s.HD ** -0.5).then_inc(q_ready, 1)
                act.wait_ge(proj_psum, NPROJ * b + 5)
                act.wait_ge(kT_psum, PAST + b)
                act.wait_ge(k_stored, 16 * b + 16)
                nc.scalar.copy(k_aug[:, :, 0:s.HD], ps[:, K_, :].rearrange("p (h e) -> p h e", e=s.HD)).then_inc(k_ready, 1)
                act.wait_ge(cum_psum, PAST + b + 1)
                act.wait_ge(kaug_ready, PAST + b)
                nc.scalar.copy(cum[:, :], ps[:, F_, s.H:2 * s.H]).then_inc(cum_ready, 1)
                act.wait_ge(proj_psum, NPROJ * b + 6)
                nc.scalar.copy(v_dst, ps[:, V_, :]).then_inc(v_ready, 1)
                keys_out(PAST + b + 1, kb)

            keys_out(PAST, s.NB)
            for free in (q_ready, k_ready, v_ready):
                act.sem_inc(free, 1)
            row_scale(0)
            normed(0)
            SETUP_LINKS, LINKS = chain.n, 2
            with act.Fori(0, s.NB) as b:
                chain.at(SETUP_LINKS + b * LINKS)
                iteration(b, b, c.queries[:, bass.ds(b, 1), :].rearrange("p a n -> p (a n)"),
                          c.values[:, bass.ds(b, 1), :].rearrange("p a n -> p (a n)"), True)
                assert chain.n == LINKS
            chain.at(SETUP_LINKS + s.NB * LINKS)
            iteration(s.NB, s.SAMPLE_KB, c.queries[:, s.NB, :], c.values[:, s.SAMPLE_KB, :], False)

        @block.tensor
        def _(pe):
            pe.wait_ge(consts, 3)
            pe.wait_ge(small_here, 16 * 7)
            for i in range(s.CCH):
                pe.transpose(ps[:, Q_, i * s.TAPS:(i + 1) * s.TAPS], taps[:, i * P:(i + 1) * P], g.ident[0:s.TAPS, 0:s.TAPS])
            pe.transpose(ps[:, K_, 0:NVEC], vecs[:, :], g.ident[0:NVEC, 0:NVEC])
            for i in range(s.CCH):
                ins = pe.transpose(ps[:, V_, i * HALO:(i + 1) * HALO], state[:, i * P:(i + 1) * P], g.ident[0:HALO, 0:HALO])
            ins.then_inc(setup_psum, 3)
            pe.wait_ge(past_here, 48)
            pe.matmul(ps[:, F_, s.H:2 * s.H], upto[:, :], logf_past[:, :], start=True, stop=True).then_inc(cum_psum, 1)

            def keys_in(kcount):
                pe.wait_ge(kaug_ready, kcount)
                for h in range(s.H):
                    ins = pe.transpose(ps[0:s.HD + 1, KTB + h // 4, (h % 4) * P:(h % 4 + 1) * P], k_aug[:, h, :], g.ident[:, :])
                ins.then_inc(kT_psum, 1)

            def iteration(b, cum_before):
                pe.wait_ge(uT_ready, b + 1)
                pe.wait_ge(xn_ready, b + 1)
                for i in range(s.DCH):
                    ins = pe.transpose(ps[:, HB + i // 4, (i % 4) * P:(i % 4 + 1) * P], xn[:, i * P:(i + 1) * P], g.ident[:, :])
                    if i % 4 == 3:
                        ins.then_inc(hT_psum, 1)
                pe.wait_ge(hT_ready, b + 1)
                for name in ORDER:
                    lo, width = COLS[name]
                    pe.wait_ge(w_here[name], 16)
                    if name == "gate":
                        pe.wait_ge(kT_ready, PAST + b)
                    if name == "f":
                        pe.wait_ge(cum_ready, PAST + b)
                    if name == "q":
                        pe.wait_ge(q_ready, b + 1)
                    if name == "k":
                        pe.wait_ge(k_ready, b + 1)
                    if name == "v":
                        pe.wait_ge(logf_ready, 2 * b + 2)
                        pe.matmul(ps[:, F_, s.H:2 * s.H], upto[:, :], logf[:, :], start=True, stop=False)
                        pe.matmul(ps[:, F_, s.H:2 * s.H], last_row[:, :], cum_before, start=False, stop=True).then_inc(cum_psum, 1)
                        pe.wait_ge(v_ready, b + 1)
                    for i in range(s.DCH):
                        ins = pe.matmul(ps[:, BANK_OF[name], 0:width], hT[:, i, :], w_in[:, i, lo:lo + width],
                                        start=(i == 0), stop=(i == s.DCH - 1))
                    ins.then_inc(proj_psum, 1)
                pe.wait_ge(u_ready, b + 2)
                for i in range(s.CCH):
                    ins = pe.transpose(ps[:, UTB, i * P:(i + 1) * P], u[:, i * P:(i + 1) * P], g.ident[:, :])
                ins.then_inc(uT_psum, 1)
                keys_in(PAST + b + 1)

            keys_in(PAST)
            with pe.Fori(0, s.NB) as b:
                iteration(b, cum[:, :])
            iteration(s.NB, cum_past[:, :])

        @block.vector
        def _(dve):
            chain = Chain(dve, dve_chain)
            chain.link(nc.vector.memset(cum[:, :], 0.0))
            chain.link(nc.vector.memset(uT[:, :, 0:HALO], 0.0))
            dve.wait_ge(setup_sb, 3)

            def iteration(b, y_of, last):
                dve.wait_ge(proj_psum, NPROJ * b + 2)
                dve.wait_ge(sig_ready, b + 1)
                nc.vector.tensor_tensor(out=u[:, :], in0=ps[:, A_, :], in1=sig[:, :], op=ALU.mult).then_inc(u_ready, 1)
                dve.wait_ge(proj_psum, NPROJ * b + 3)
                nc.vector.tensor_tensor(out=z[:, :], in0=ps[:, F_, 0:s.H], in1=bf[:, :], op=ALU.add).then_inc(z_ready, 1)
                dve.wait_ge(uT_psum, b + 1)
                nc.vector.tensor_copy(uT[:, :, HALO:HALO + P], ps[:, UTB, :].rearrange("p (c t) -> p c t", t=P)).then_inc(uT_ready, 1)
                dve.wait_ge(uT_ready, b + 2)
                for j in range(s.TAPS):
                    for i in range(s.CCH):
                        src, dst = uT[:, i, j:j + P], y_of(i)
                        if j == 0:
                            ins = nc.vector.tensor_scalar(dst, src, tapsT[:, i, 0:1], c.b_dw[:, i:i + 1], ALU.mult, ALU.add)
                        else:
                            dve.wait_ge(dve_chain, chain.base + chain.n - s.CCH + 1)
                            ins = nc.vector.scalar_tensor_tensor(out=dst, in0=src, scalar=tapsT[:, i, j:j + 1], in1=dst,
                                                                 op0=ALU.mult, op1=ALU.add)
                        ins.then_inc(dve_chain, 1)
                        chain.n += 1
                dve.wait_ge(dve_chain, chain.base + chain.n)
                if not last:
                    chain.link(nc.vector.tensor_copy(uT[:, :, 0:HALO], uT[:, :, P:P + HALO]))

            for free in (u_ready, uT_ready):
                dve.sem_inc(free, 1)
            SETUP_LINKS, LINKS = chain.n, s.TAPS * s.CCH + 1
            with dve.Fori(0, s.NB) as b:
                chain.at(SETUP_LINKS + b * LINKS)
                iteration(b, lambda i: c.convT[:, i, bass.ds(b * P, P)], False)
                assert chain.n == LINKS
            chain.at(SETUP_LINKS + s.NB * LINKS)
            chain.link(nc.vector.tensor_copy(uT[:, :, 0:HALO], stateT[:, :, :]))
            dve.wait_ge(misc_stored, 16)
            iteration(s.NB, lambda i: c.convT[:, i, s.NB * P:(s.NB + 1) * P], True)


def phase_b(nc, s, d, g, c):
    with ExitStack() as ctx:
        def sb(name, shape):
            return ctx.enter_context(nc.sbuf_tensor(name, shape, F32))

        def sem(name):
            return ctx.enter_context(nc.semaphore(name))

        HALF = s.NB // 2
        SPAN = HALF * P
        assert SPAN == BANK and s.CCH == 4 and s.DA == BANK

        w_out = sb("w_out_sb", [P, s.DCH, s.D])
        mask = sb("mask", [P, 2 * SPAN - P])
        q_aug = sb("q_aug", [P, s.H, s.HD + 1])
        qT = sb("qT_b", [s.HD + 1, s.H, P])
        y_st = sb("y_st", [P, s.CCH, P])
        cb = sb("cum_b", [P, s.H])
        scores = sb("scores", [P, 2, s.T])
        probs = sb("probs", [P, 2, s.T])
        probsT = sb("probsT", [P, s.T])
        top = sb("row_max", [P, s.H])
        ntop = sb("neg_row_max", [P, s.H])
        rs = sb("row_sum", [P, s.H])
        rinv = sb("row_sum_inv", [P, s.H])
        stats = sb("ln_stats", [P, 6])
        mv = sb("ln_mv", [P, 2])
        var = sb("ln_var", [P, 1])
        lnr = sb("ln_rstd", [P, 1])
        z = sb("z_b", [P, s.DC])
        sig = sb("sig_b", [P, s.CCH, P])
        yn = sb("yn_b", [P, s.CCH, P])
        o = sb("o_b", [P, s.DA])
        catT = sb("catT", [P, s.DCH, P])
        xres = sb("xres_b", [P, s.D])
        x1 = sb("x1_b", [P, s.D])
        sq = sb("sq_b", [P, s.D])
        xn = sb("xn_b", [P, s.D])
        gf = sb("g_ffn_rows", [P, s.D])
        rms = sb("rms_b", [P, 3])

        w_here, x_here, gf_here = sem("w_here_b"), sem("x_here_b"), sem("gf_here")
        consts = sem("consts_b")
        q_staged, y_staged, c_staged = sem("q_staged"), sem("y_staged"), sem("c_staged")
        qT_psum, qT_ready = sem("qT_psum"), sem("qT_ready")
        s_psum, top_ready, p_ready = sem("s_psum"), sem("top_ready"), sem("p_ready")
        pT_psum, pTa_ready, pTd_ready, pv_psum = sem("pT_psum"), sem("pTa_ready"), sem("pTd_ready"), sem("pv_psum")
        y_psum, mv_ready, lnr_ready, z_ready = sem("y_psum"), sem("mv_ready"), sem("lnr_ready"), sem("z_ready_b")
        zT_psum, sig_ready, conv_ready = sem("zT_psum"), sem("sig_ready_b"), sem("conv_ready")
        o_ready, oT_psum, oT_ready = sem("o_ready"), sem("oT_psum"), sem("oT_ready")
        x1_psum, x1_ready, ss_ready, xn_ready = sem("x1_psum"), sem("x1_ready"), sem("ss_ready"), sem("xn_ready_b")
        x1_stored, xn_stored = sem("x1_stored"), sem("xn_stored")
        dve_chain, pool_chain, pool_held, dve_held = (sem(n + "_b") for n in ("dve_chain", "pool_chain", "pool_held", "dve_held"))

        ps = g.ps
        S_, PT_, O_, T_, X1_ = 0, 4, 6, 7, 2
        H = s.H
        BLOCKS = s.NB + 1
        low = dict(nkb=HALF, kb0=0, mask_at=lambda b: SPAN - P - b * P)
        high = dict(nkb=s.NB, kb0=0, mask_at=lambda b: SPAN - P + SPAN - b * P)
        sample = dict(nkb=2, kb0=s.NB, mask_at=lambda b: SPAN - 2 * P)

        def over_blocks(eng, body):
            with eng.Fori(0, HALF) as b:
                body(b, **low)
            with eng.Fori(HALF, s.NB) as b:
                body(b, **high)
            body(s.NB, **sample)

        block = ctx.enter_context(nc.Block())

        @block.sync
        def _(sp):
            sp.dma_start(xres[:, :], d.x_prompt[0, 0:P, :]).then_inc(x_here, 16)
            sp.dma_start(w_out[:, :, :], d.w_out[0].rearrange("(c p) n -> p c n", p=P)).then_inc(w_here, 16)
            sp.dma_start(gf[:, :], d.g_ffn[0].partition_broadcast(P)).then_inc(gf_here, 16)
            x1_rows = d.x1.rearrange("b p n -> (b p) n")
            xn_rows = d.xn2.rearrange("b p n -> (b p) n")

            def store_x1(b):
                sp.dma_start(x1_rows[bass.ds(b * P, P), :], x1[:, :]).then_inc(x1_stored, 16)

            def store_xn(b):
                sp.wait_ge(xn_ready, b + 2)
                sp.dma_start(xn_rows[bass.ds(b * P, P), :], xn[:, :]).then_inc(xn_stored, 16)

            sp.sem_inc(x1_stored, 16)
            sp.sem_inc(xn_stored, 16)
            with sp.Fori(0, s.NB - 1) as b:
                sp.wait_ge(x1_ready, b + 2)
                sp.dma_start(xres[:, :], d.x_prompt[0, bass.ds((b + 1) * P, P), :]).then_inc(x_here, 16)
                store_x1(b)
                store_xn(b)
            sp.wait_ge(x1_ready, s.NB + 1)
            sp.dma_start(xres[0:s.TS, :], d.x_sample[0]).then_inc(x_here, 16)
            store_x1(s.NB - 1)
            store_xn(s.NB - 1)
            sp.wait_ge(x1_ready, s.NB + 2)
            store_x1(s.NB)
            store_xn(s.NB)
            sp.wait_ge(x1_stored, 16 * (BLOCKS + 1))
            sp.wait_ge(xn_stored, 16 * (BLOCKS + 1))

        @block.gpsimd
        def _(pool):
            chain = Chain(pool, pool_chain, held=pool_held)
            chain.link(nc.gpsimd.memset(mask[:, :], 0.0))
            nc.gpsimd.affine_select(out=mask[:, :], in_=mask[:, :], compare_op=ALU.is_ge, fill=MASKED,
                                    base=SPAN - P, pattern=[[-1, 2 * SPAN - P]], channel_multiplier=1).then_inc(consts, 1)
            nc.gpsimd.memset(q_aug[:, :, s.HD], 1.0)
            SETUP_LINKS, LINKS = chain.n, 4

            def stage(b, queries, conv, cum):
                chain.wait(qT_psum, b + 1)
                nc.gpsimd.tensor_copy(q_aug[:, :, 0:s.HD], queries.rearrange("p (h e) -> p h e", e=s.HD)).then_inc(q_staged, 1)
                chain.wait(top_ready, H * b + 1)
                nc.gpsimd.tensor_copy(cb[:, :], cum).then_inc(c_staged, 1)
                chain.wait(y_psum, b + 1)
                nc.gpsimd.tensor_copy(y_st[:, :, :], conv).then_inc(y_staged, 1)

            def layer_norm_scale(b):
                chain.wait(mv_ready, b + 1)
                chain.link(nc.gpsimd.tensor_scalar(var[:, :], mv[:, 1:2], LN_EPS, None, ALU.add))
                nc.gpsimd.tensor_tensor(out=lnr[:, :], in0=var[:, :], in1=g.neg_half[:, :], op=ALU.pow).then_inc(lnr_ready, 1)

            def rms_rows(b):
                chain.wait(ss_ready, b + 1)
                chain.link(nc.gpsimd.tensor_scalar(rms[:, 1:2], rms[:, 0:1], 1.0 / s.D, RMS_EPS, ALU.mult, ALU.add))
                chain.link(nc.gpsimd.tensor_tensor(out=rms[:, 2:3], in0=rms[:, 1:2], in1=g.neg_half[:, :], op=ALU.pow))
                chain.wait(xn_stored, 16 * (b + 1))
                chain.link(nc.gpsimd.tensor_scalar(xn[:, :], x1[:, :], rms[:, 2:3], None, ALU.mult))
                nc.gpsimd.tensor_tensor(out=xn[:, :], in0=xn[:, :], in1=gf[:, :], op=ALU.mult).then_inc(xn_ready, 1)

            pool.sem_inc(xn_ready, 1)
            pool.wait_ge(gf_here, 16)
            stage(0, c.queries[:, 0, :], c.convT[:, :, 0:P], c.cum[:, 0, :])
            with pool.Fori(0, s.NB) as b:
                chain.at(SETUP_LINKS + b * LINKS)
                layer_norm_scale(b)
                stage(b + 1, c.queries[:, bass.ds(b + 1, 1), :].rearrange("p a n -> p (a n)"),
                      c.convT[:, :, bass.ds((b + 1) * P, P)],
                      c.cum[:, bass.ds(b + 1, 1), :].rearrange("p a n -> p (a n)"))
                rms_rows(b)
                assert chain.n == LINKS
            chain.at(SETUP_LINKS + s.NB * LINKS)
            layer_norm_scale(s.NB)
            rms_rows(s.NB)

        @block.tensor
        def _(pe):
            for free in (qT_psum, y_psum):
                pe.sem_inc(free, 1)

            def body(b, nkb, kb0, mask_at):
                def scores_of(h):
                    width = min(nkb * P, BANK)
                    spans = range(0, nkb * P, BANK)
                    for i, at in enumerate(spans):
                        out = ps[:, S_ + 2 * (h % 2) + i, 0:width]
                        final = at == spans[-1]
                        ins = pe.matmul(out, qT[:, h, :], c.keysT[:, h, kb0 * P + at:kb0 * P + at + width],
                                        start=True, stop=not final)
                        if final:
                            ins = pe.matmul(out, g.ident[:, :], mask[:, bass.ds(mask_at(b), width)], start=False, stop=True)
                    ins.then_inc(s_psum, 1)

                def turn_probs(h):
                    pe.wait_ge(p_ready, 2 + H * b + h + 1)
                    for i in range(nkb):
                        ins = pe.transpose(ps[:, PT_ + i // 4, (i % 4) * P:(i % 4 + 1) * P],
                                           probs[:, h % 2, i * P:(i + 1) * P], g.ident[:, :])
                    ins.then_inc(pT_psum, 1)

                def weigh_values(h):
                    pe.wait_ge(pTa_ready, H * b + h + 1)
                    if nkb > HALF:
                        pe.wait_ge(pTd_ready, H * (b - HALF) + h + 1)
                    for i in range(nkb):
                        ins = pe.matmul(ps[:, O_, h * s.HD:(h + 1) * s.HD], probsT[:, i * P:(i + 1) * P],
                                        c.values[:, kb0 + i, h * s.HD:(h + 1) * s.HD], start=(i == 0), stop=(i == nkb - 1))
                    ins.then_inc(pv_psum, 1)

                pe.wait_ge(q_staged, b + 1)
                for h in range(H):
                    ins = pe.transpose(ps[0:s.HD + 1, PT_ + h // 4, (h % 4) * P:(h % 4 + 1) * P], q_aug[:, h, :], g.ident[:, :])
                ins.then_inc(qT_psum, 1)
                pe.wait_ge(consts, 1)
                pe.wait_ge(qT_ready, b + 1)
                scores_of(0)
                pe.wait_ge(x1_ready, b + 1)
                scores_of(1)
                pe.wait_ge(y_staged, b + 1)
                for i in range(s.CCH):
                    ins = pe.transpose(ps[:, T_, i * P:(i + 1) * P], y_st[:, i, :], g.ident[:, :])
                ins.then_inc(y_psum, 1)
                for h in range(H):
                    turn_probs(h)
                    if h + 2 < H:
                        scores_of(h + 2)
                    weigh_values(h)
                    if h == 0:
                        pe.wait_ge(z_ready, b + 1)
                        for i in range(s.CCH):
                            ins = pe.transpose(ps[:, T_, i * P:(i + 1) * P], z[:, i * P:(i + 1) * P], g.ident[:, :])
                        ins.then_inc(zT_psum, 1)
                pe.wait_ge(conv_ready, b + 2)
                pe.wait_ge(o_ready, b + 1)
                for i in range(s.CCH):
                    ins = pe.transpose(ps[:, T_, i * P:(i + 1) * P], o[:, i * P:(i + 1) * P], g.ident[:, :])
                ins.then_inc(oT_psum, 1)
                pe.wait_ge(w_here, 16)
                pe.wait_ge(oT_ready, b + 1)
                for half in range(s.D // BANK):
                    for i in range(s.DCH):
                        ins = pe.matmul(ps[:, X1_ + half, :], catT[:, i, :], w_out[:, i, half * BANK:(half + 1) * BANK],
                                        start=(i == 0), stop=(i == s.DCH - 1))
                ins.then_inc(x1_psum, 1)

            over_blocks(pe, body)

        @block.scalar
        def _(act):
            act.sem_inc(p_ready, 2)

            def body(b, nkb, kb0, mask_at):
                def exp(h):
                    act.wait_ge(top_ready, 1 + H * b + h + 1)
                    nc.scalar.activation(probs[:, h % 2, 0:nkb * P], scores[:, h % 2, 0:nkb * P], ACT.Exp,
                                         bias=ntop[:, h:h + 1], accum_out=rs[:, h:h + 1]).then_inc(p_ready, 1)

                act.wait_ge(qT_psum, b + 2)
                for i in range(2):
                    ins = nc.scalar.copy(qT[:, 4 * i:4 * i + 4, :], ps[0:s.HD + 1, PT_ + i, :].rearrange("p (h t) -> p h t", t=P))
                ins.then_inc(qT_ready, 1)
                exp(0)
                for h in range(H):
                    if h + 1 < H:
                        exp(h + 1)
                    act.wait_ge(pT_psum, H * b + h + 1)
                    width = min(nkb, 4) * P
                    nc.scalar.copy(probsT[:, 0:width], ps[:, PT_, 0:width]).then_inc(pTa_ready, 1)
                    if h == 1:
                        act.wait_ge(zT_psum, b + 1)
                        act.wait_ge(conv_ready, b + 1)
                        for i in range(s.CCH):
                            ins = nc.scalar.activation(sig[:, i, :], ps[:, T_, i * P:(i + 1) * P], ACT.Sigmoid,
                                                       bias=c.ln_b[:, i:i + 1], scale=c.ln_g[:, i:i + 1])
                        ins.then_inc(sig_ready, 1)
                act.wait_ge(oT_psum, b + 1)
                nc.scalar.copy(catT[:, 0:s.CCH, :], ps[:, T_, :].rearrange("p (c t) -> p c t", t=P)).then_inc(oT_ready, 1)

            over_blocks(act, body)

        @block.vector
        def _(dve):
            chain = Chain(dve, dve_chain)
            for free in (conv_ready, x1_ready, top_ready):
                dve.sem_inc(free, 1)
            LINKS = H + 3

            def body(b, nkb, kb0, mask_at):
                chain.at(b * LINKS)

                def row_max(h):
                    dve.wait_ge(s_psum, H * b + h + 1)
                    dve.wait_ge(p_ready, H * b + h + 1)
                    banks = ps[:, S_ + 2 * (h % 2):S_ + 2 * (h % 2) + 2, :].rearrange("p a n -> p (a n)")
                    chain.link(nc.vector.tensor_scalar(scores[:, h % 2, 0:nkb * P], banks[:, 0:nkb * P], cb[:, h:h + 1], None,
                                                       ALU.add, ALU.max, accum_out=top[:, h:h + 1]))
                    nc.vector.tensor_scalar(ntop[:, h:h + 1], top[:, h:h + 1], -1.0, None, ALU.mult).then_inc(top_ready, 1)

                dve.wait_ge(c_staged, b + 1)
                row_max(0)
                row_max(1)
                dve.wait_ge(y_psum, b + 2)
                chain.link(nc.vector.bn_stats(stats[:, :], ps[:, T_, :]))
                dve.sem_inc(dve_held, 1)
                nc.vector.bn_aggr(mv[:, :], stats[:, :]).then_inc(mv_ready, 1)
                dve.wait_ge(mv_ready, b + 1)
                dve.wait_ge(lnr_ready, b + 1)
                nc.vector.tensor_scalar(z[:, :], ps[:, T_, :], mv[:, 0:1], lnr[:, 0:1], ALU.subtract, ALU.mult).then_inc(z_ready, 1)
                for h in range(H):
                    if nkb > HALF:
                        dve.wait_ge(pT_psum, H * b + h + 1)
                        nc.vector.tensor_copy(probsT[:, BANK:nkb * P], ps[:, PT_ + 1, 0:nkb * P - BANK]).then_inc(pTd_ready, 1)
                    if h + 2 < H:
                        row_max(h + 2)
                    if h == 1:
                        dve.wait_ge(sig_ready, b + 1)
                        for i in range(s.CCH):
                            ins = nc.vector.tensor_scalar(yn[:, i, :], ps[:, T_, i * P:(i + 1) * P], c.ln_g[:, i:i + 1],
                                                          c.ln_b[:, i:i + 1], ALU.mult, ALU.add)
                        chain.link(ins)
                        nc.vector.tensor_tensor(out=catT[:, s.CCH:s.DCH, :], in0=yn[:, :, :], in1=sig[:, :, :],
                                                op=ALU.mult).then_inc(conv_ready, 1)
                dve.wait_ge(pv_psum, H * (b + 1))
                chain.link(nc.vector.reciprocal(rinv[:, :], rs[:, :]))
                nc.vector.tensor_tensor(out=o[:, :].rearrange("p (h e) -> p h e", e=s.HD),
                                        in0=ps[:, O_, :].rearrange("p (h e) -> p h e", e=s.HD),
                                        in1=rinv[:, :].unsqueeze(2).broadcast_to([P, H, s.HD]), op=ALU.mult).then_inc(o_ready, 1)
                dve.wait_ge(x1_psum, b + 1)
                dve.wait_ge(x_here, 16 * (b + 1))
                dve.wait_ge(x1_stored, 16 * (b + 1))
                dve.wait_ge(xn_ready, b + 1)
                nc.vector.tensor_tensor(out=x1[:, :], in0=ps[:, X1_:X1_ + 2, :].rearrange("p a n -> p (a n)"), in1=xres[:, :],
                                        op=ALU.add).then_inc(x1_ready, 1)
                dve.wait_ge(x1_ready, b + 2)
                nc.vector.tensor_tensor_reduce(out=sq[:, :], in0=x1[:, :], in1=x1[:, :], scale=1.0, scalar=0.0, op0=ALU.mult,
                                               op1=ALU.add, accum_out=rms[:, 0:1]).then_inc(ss_ready, 1)
                assert chain.n == LINKS

            over_blocks(dve, body)


def phase_c(nc, s, d, g):
    with ExitStack() as ctx:
        def sb(name, shape, dt=F32):
            return ctx.enter_context(nc.sbuf_tensor(name, shape, dt))

        def sem(name):
            return ctx.enter_context(nc.semaphore(name))

        K, PH = s.K, s.PH
        RING = 8
        DIAGS = 4
        AHEAD = 6
        PAIR = 2 * s.HALF
        NEG = -3.0e38

        w_pq = sb("w_pq_sb", [P, s.DCH, PH * PAIR])
        keysT = sb("sub_keysT", [P, 2, PH, s.NKEYS])
        xn_next = sb("xn_next", [P, s.D])
        xn_after = sb("xn_after", [P, s.D])
        xn = sb("xn_c", [P, s.D])
        xnT = sb("xnT_c", [P, s.DCH, P])
        u_rows = sb("u_rows", [P, RING, s.D])
        v_rows = sb("v_rows", [P, RING, s.D])
        keys = v_rows[:, 0:2, :].rearrange("p a n -> p (a n)").rearrange("p (x e) -> p x e", e=s.HALF)
        q = sb("q_c", [P, PAIR])
        qT = sb("qT_c", [P, 2, P])
        half_s = sb("half_scores", [P, 2, 2, s.NKEYS])
        left = sb("left_scores", [P, 2, s.NKEYS])
        top = sb("top_scores", [P, 2, K])
        top_i = sb("top_keys", [P, 2, K], U32)
        top_f = sb("top_keys_f", [P, 2, K])
        cand = sb("cand", [P, K, K])
        cand_left = sb("cand_left", [P, K, K])
        best = sb("best", [P, K])
        best_j = sb("best_j", [P, K], U32)
        ij = sb("best_ij", [P, 2, K], U32)
        ij_f = sb("best_ij_f", [P, 2, K])
        hit = sb("hit", [P, 2, K, K])
        key_f = sb("best_key_f", [P, 2, K])
        nbest = sb("neg_best", [P, 1])
        count = sb("count_to_k", [P, K])
        experts = sb("experts", [P, PH, K], U32)
        exps = sb("gate_exps", [P, PH, K])
        expsum = sb("gate_sums", [P, PH])
        gate_inv = sb("gate_inv", [P, 1])
        dots = sb("dots", [P, 2, K])
        gelu = sb("gelu_c", [P, 2, K])
        act_w = sb("act_c", [P, 2, K])
        diag = sb("diag", [P, DIAGS, P])
        zeros = sb("zeros_c", [P, BANK])
        out_rows = sb("out_rows", [P, s.D])
        x2 = sb("x2_c", [P, s.D])
        y = sb("y_c", [P, s.D])
        gf = sb("g_final_rows", [P, s.D])
        rms = sb("rms_c", [P, 3])

        keys_here, xn_here = sem("keys_here"), sem("xn_here")
        w_here = [sem(f"w_here_c{h}") for h in range(PH)]
        gf_here, x1_here, y_ready, y_stored = sem("gf_here"), sem("x1_here_c"), sem("y_ready"), sem("y_stored")
        out_used, ms_ready, rstd_ready, final_chain = sem("out_used"), sem("ms_ready_c"), sem("rstd_ready_c"), sem("final_chain")
        consts = sem("consts_c")
        keys_psum, keys_ready = sem("keys_psum"), sem("keys_ready")
        xn_moved, xn_taken, xnT_psum, xnT_ready = sem("xn_moved"), sem("xn_taken"), sem("xnT_psum"), sem("xnT_ready")
        q_psum, q_out, qT_psum, qT_out, s_psum, s_out, s_used = (
            sem(n + "_c") for n in ("q_psum", "q_out", "qT_psum", "qT_out", "s_psum", "s_out", "s_used"))
        best_ready, exps_ready, experts_ready = sem("best_ready"), sem("exps_ready"), sem("experts_ready")
        u_here = [sem(f"u_here{i}") for i in range(RING)]
        v_here = [sem(f"v_here{i}") for i in range(RING)]
        u_used, v_used = sem("u_used"), sem("v_used")
        gelu_ready, act_ready, diag_ready = sem("gelu_ready"), sem("act_ready"), sem("diag_ready")
        sum_psum, out_ready = sem("sum_psum"), sem("out_ready")
        dve_chain, dve_held, pool_held = sem("dve_chain_c"), sem("dve_held_c"), sem("pool_held_c")

        ps = g.ps
        ACC_, Q_, QT_, S_, XT_ = 0, 2, 3, 4, 5
        USES = K // RING
        U_FREE, V_FREE = RING, RING + K

        FIRST = 2
        CATCH_UP = [[2, 3], [4, 5], [6, 7, 8]] + [[h + AHEAD] for h in range(3, PH)]

        STRIDE = {1: 3, 2: 3, 3: 1}

        def head_pairs(eng, body, first=0, last=PH // 2):
            with eng.Fori(first, last) as j:
                for parity in range(2):
                    body(j * 2 + parity, parity)

        block = ctx.enter_context(nc.Block())

        @block.sync
        def _(sp):
            xn_rows, x1_rows = (rows.rearrange("b p n -> (b p) n") for rows in (d.xn2, d.x1))

            def load_rows(b):
                sp.wait_ge(xn_moved, b)
                sp.wait_ge(xnT_psum, b)
                sp.dma_start(xn_next[:, :], xn_rows[bass.ds(b * P, P), :]).then_inc(xn_here, 16)

            def finish(b, x1_src, dst, rows):
                sp.wait_ge(y_ready, b + 1)
                sp.dma_start(x2[0:rows, :], x1_src).then_inc(x1_here, 16)
                sp.wait_ge(y_ready, b + 2)
                sp.dma_start(dst, y[0:rows, :]).then_inc(y_stored, 16)

            sp.dma_start(xn_next[:, :], d.xn2[0]).then_inc(xn_here, 16)
            for p in range(2):
                sp.dma_start(keys[:, p * PH:(p + 1) * PH, :], d.sub_keys[0, p].rearrange("h k e -> k h e")).then_inc(keys_here, 16)
            for h in range(PH):
                sp.dma_start(w_pq[:, :, h * PAIR:(h + 1) * PAIR],
                             d.w_pq[0][:, h * PAIR:(h + 1) * PAIR].rearrange("(c p) n -> p c n", p=P)).then_inc(w_here[h], 16)
            sp.dma_start(gf[:, :], d.g_final.partition_broadcast(P)).then_inc(gf_here, 16)
            sp.sem_inc(y_stored, 16)
            load_rows(1)
            with sp.Fori(0, s.NB - 1) as i:
                load_rows(i + 2)
                finish(i, x1_rows[bass.ds(i * P, P), :], d.y_prompt[0, bass.ds(i * P, P), :], P)
            finish(s.NB - 1, d.x1[s.NB - 1], d.y_prompt[0, (s.NB - 1) * P:s.NB * P, :], P)
            finish(s.NB, d.x1[s.NB, 0:s.TS, :], d.y_sample[0], s.TS)
            sp.wait_ge(y_stored, 16 * (s.NB + 2))

        @block.gpsimd
        def _(pool):
            def wait(semaphore, value):
                pool.wait_ge(semaphore, value)
                pool.sem_inc(pool_held, 1)

            nc.gpsimd.memset(zeros[:, :], 0.0).then_inc(consts, 1)
            nc.gpsimd.iota(count[:, :], pattern=[[1, K]], base=0, channel_multiplier=0,
                           allow_small_or_imprecise_dtypes=True).then_inc(consts, 1)

            def gather(table, ring, here, used, free, n, h, k, rows):
                wait(used, free - RING + K * n + k + 1)
                nc.gpsimd.indirect_dma_start(
                    out=ring[0:rows, k % RING, :], out_offset=None, in_=table,
                    in_offset=bass.IndirectOffsetOnAxis(ap=experts[0:rows, h, k:k + 1], axis=0),
                ).then_inc(here[k % RING], 16)

            def gather_u(n, h, k, rows):
                gather(d.u_emb[0], u_rows, u_here, u_used, U_FREE, n, h, k, rows)

            def gather_v(n, h, k, rows):
                gather(d.v_emb[0], v_rows, v_here, v_used, V_FREE, n, h, k, rows)

            pool.wait_ge(experts_ready, 1)
            for k in range(K):
                gather_u(0, 0, k, P)
            def prompt_head(i, h):
                wait(experts_ready, i * PH + h + 2)
                for k in range(K):
                    gather_u(i * PH + h + 1, (h + 1) % PH, k, P)
                    gather_v(i * PH + h, h, k, P)

            def inverse_rms(b, rows):
                pool.wait_ge(ms_ready, b + 1)
                nc.gpsimd.tensor_tensor(out=rms[0:rows, 2:3], in0=rms[0:rows, 1:2], in1=g.neg_half[0:rows, :],
                                        op=ALU.pow).then_inc(rstd_ready, 1)

            for h in range(PH):
                prompt_head(0, h)
            with pool.Fori(1, s.NB) as i:
                for h in range(PH):
                    prompt_head(i, h)
                    if h == 3:
                        inverse_rms(i - 1, P)
            for h in range(PH):
                n = s.NB * PH + h
                for k in range(K):
                    if h + 1 < PH:
                        gather_u(n + 1, h + 1, k, s.TS)
                    gather_v(n, h, k, s.TS)
                if h == 3:
                    inverse_rms(s.NB - 1, P)
            inverse_rms(s.NB, s.TS)

        @block.tensor
        def _(pe):
            pe.wait_ge(keys_here, 32)
            for x in range(2 * PH):
                ins = pe.transpose(ps[:, 2 + x // 4, (x % 4) * P:(x % 4 + 1) * P], keys[:, x, :], g.ident[:, :])
            ins.then_inc(keys_psum, 1)

            def turn_rows(b):
                pe.wait_ge(xn_here, 16 * (b + 1))
                for x in range(s.DCH):
                    ins = pe.transpose(ps[:, XT_ + x // 4, (x % 4) * P:(x % 4 + 1) * P], xn_next[:, x * P:(x + 1) * P], g.ident[:, :])
                ins.then_inc(xnT_psum, 1)

            def query(b, r, h):
                pe.wait_ge(xnT_ready, b + 1)
                for x in range(s.DCH):
                    ins = pe.matmul(ps[:, Q_, 0:PAIR], xnT[:, x, :], w_pq[:, x, bass.ds(h * PAIR, PAIR)],
                                    start=(x == 0), stop=(x == s.DCH - 1))
                ins.then_inc(q_psum, 1)

            def turn_query(r):
                pe.wait_ge(q_out, r + 1)
                for p in range(2):
                    ins = pe.transpose(ps[:, QT_, p * P:(p + 1) * P], q[:, p * P:(p + 1) * P], g.ident[:, :])
                ins.then_inc(qT_psum, 1)

            def score(r, h):
                pe.wait_ge(qT_out, r + 1)
                pe.wait_ge(s_out, r + 1)
                for p in range(2):
                    keys_h = keysT[:, p, bass.ds(h, 1), :].rearrange("p a k -> p (a k)")
                    ins = pe.matmul(ps[:, S_, p * P:(p + 1) * P], qT[:, p, :], keys_h, start=True, stop=True)
                ins.then_inc(s_psum, 1)

            def weigh(n, k, rows):
                pe.wait_ge(v_here[k % RING], 16 * (USES * n + k // RING + 1))
                pe.wait_ge(diag_ready, 2 * K + K * n + k + 1)
                for half in range(s.D // BANK):
                    ins = pe.matmul(ps[0:rows, ACC_ + half, :], diag[0:rows, k % DIAGS, 0:rows],
                                    v_rows[0:rows, k % RING, half * BANK:(half + 1) * BANK], start=False, stop=False)
                ins.then_inc(v_used, 1)

            def sums(rows, first):
                for half in range(s.D // BANK):
                    ins = pe.matmul(ps[0:rows, ACC_ + half, :], zeros[0:rows, 0:rows], zeros[0:rows, 0:BANK],
                                    start=first, stop=not first)
                return ins

            def weigh_and_route(n, routes):
                todo = []
                for b, r, h in routes:
                    todo += [lambda b=b, r=r, h=h: query(b, r, h), lambda r=r: turn_query(r), lambda r=r, h=h: score(r, h)]
                for k in range(K):
                    weigh(n, k, P)
                    if k % STRIDE[len(routes)] == 0 and todo:
                        todo.pop(0)()
                assert not todo

            pe.sem_inc(v_used, V_FREE)
            pe.wait_ge(keys_ready, 1)
            turn_rows(0)
            pe.wait_ge(w_here[0], 16)
            query(0, 0, 0)
            for r in range(FIRST + 2):
                turn_query(r)
                if r + 1 < FIRST + 2:
                    pe.wait_ge(w_here[r + 1], 16)
                    query(0, r + 1, r + 1)
                score(r, r)
            pe.wait_ge(consts, 2)
            pe.wait_ge(out_ready, 1)
            sums(P, True)
            for h in range(PH):
                if h == 2:
                    turn_rows(1)
                routed = [r + 2 for r in CATCH_UP[h]]
                for r in routed:
                    if r < PH:
                        pe.wait_ge(w_here[r], 16)
                weigh_and_route(h, [(r // PH, r, r % PH) for r in routed])
            sums(P, False).then_inc(sum_psum, 1)
            with pe.Fori(1, s.NB) as i:
                turn_rows(i + 1)
                pe.wait_ge(out_ready, i + 1)
                sums(P, True)
                head_pairs(pe, lambda h, parity: weigh_and_route(i * PH + h, [(i + 1, i * PH + h + PH, h)]))
                sums(P, False).then_inc(sum_psum, 1)
            pe.wait_ge(out_ready, s.NB + 1)
            sums(s.TS, True)
            for h in range(PH):
                for k in range(K):
                    weigh(s.NB * PH + h, k, s.TS)
            sums(s.TS, False).then_inc(sum_psum, 1)

        @block.scalar
        def _(act):
            act.wait_ge(keys_psum, 1)
            for x in range(2 * PH // 4):
                dst = keysT[:, x // 2, 4 * (x % 2):4 * (x % 2) + 4, :]
                ins = nc.scalar.copy(dst, ps[:, 2 + x, :].rearrange("p (h k) -> p h k", k=s.NKEYS))
            ins.then_inc(keys_ready, 1)

            def rows_out(b):
                act.wait_ge(xnT_psum, b + 1)
                for x in range(2):
                    ins = nc.scalar.copy(xnT[:, 4 * x:4 * x + 4, :], ps[:, XT_ + x, :].rearrange("p (c t) -> p c t", t=P))
                ins.then_inc(xnT_ready, 1)
                act.wait_ge(xn_taken, b + 1)
                nc.scalar.copy(xn_after[:, :], xn_next[:, :]).then_inc(xn_moved, 1)

            def query_out(r):
                act.wait_ge(q_psum, r + 1)
                nc.scalar.copy(q[:, :], ps[:, Q_, 0:PAIR]).then_inc(q_out, 1)

            def turned_out(r):
                act.wait_ge(qT_psum, r + 1)
                nc.scalar.copy(qT[:, :, :], ps[:, QT_, 0:PAIR].rearrange("p (a t) -> p a t", t=P)).then_inc(qT_out, 1)

            def scores_out(r, parity):
                act.wait_ge(s_psum, r + 1)
                act.wait_ge(s_used, r + 1)
                nc.scalar.copy(half_s[:, parity, :, :], ps[:, S_, 0:2 * s.NKEYS].rearrange("p (a k) -> p a k", a=2)).then_inc(s_out, 1)

            def gate_exps(r, slot):
                act.wait_ge(best_ready, r + 1)
                nc.scalar.activation(exps[:, bass.ds(slot, 1), :].rearrange("p a k -> p (a k)"), best[:, :], ACT.Exp,
                                     bias=nbest[:, 0:1], accum_out=expsum[:, bass.ds(slot, 1)]).then_inc(exps_ready, 1)

            def gelus(n, parity, rows):
                act.wait_ge(u_used, U_FREE + K * (n + 1))
                act.wait_ge(act_ready, n + 1)
                nc.scalar.activation(gelu[0:rows, parity, :], dots[0:rows, parity, :], ACT.Gelu).then_inc(gelu_ready, 1)

            def diagonals(n, parity, ks, rows):
                for k in ks:
                    act.wait_ge(act_ready, n + 2)
                    act.wait_ge(v_used, V_FREE + K * n + k - DIAGS + 1)
                    nc.scalar.mul(diag[0:rows, k % DIAGS, 0:rows], g.ident[0:rows, 0:rows],
                                  act_w[0:rows, parity, k:k + 1]).then_inc(diag_ready, 1)

            def close(b, rows):
                act.wait_ge(sum_psum, b + 1)
                act.wait_ge(out_used, b + 1)
                nc.scalar.copy(out_rows[0:rows, :], ps[0:rows, ACC_:ACC_ + 2, :].rearrange("p a n -> p (a n)")).then_inc(out_ready, 1)

            act.sem_inc(s_out, 1)
            act.sem_inc(diag_ready, 2 * K)
            act.sem_inc(out_ready, 1)
            rows_out(0)
            for r in range(FIRST + 2):
                query_out(r)
                turned_out(r)
                if r >= 3:
                    gate_exps(r - 3, r - 3)
                scores_out(r, r % 2)
            gate_exps(FIRST - 1, FIRST - 1)
            for h in range(PH):
                if h == 2:
                    rows_out(1)
                gelus(h, h % 2, P)
                chosen = CATCH_UP[h]
                k = 0
                for r in chosen:
                    for part in range(3):
                        ahead = min(k + STRIDE[len(chosen)], K)
                        diagonals(h, h % 2, range(k, ahead), P)
                        k = ahead
                        if part == 0:
                            if r != chosen[0]:
                                gate_exps(r - 1, (r - 1) % PH)
                            query_out(r + 2)
                        elif part == 1:
                            turned_out(r + 2)
                        else:
                            if len(chosen) == 1:
                                gate_exps(r, r % PH)
                            scores_out(r + 2, r % 2)
                diagonals(h, h % 2, range(k, K), P)
                if len(chosen) > 1:
                    gate_exps(chosen[-1], chosen[-1] % PH)
            close(0, P)
            with act.Fori(1, s.NB) as i:
                rows_out(i + 1)

                def head(h, parity):
                    n = i * PH + h
                    gelus(n, parity, P)
                    diagonals(n, parity, range(0, 3), P)
                    query_out(n + PH)
                    diagonals(n, parity, range(3, 6), P)
                    turned_out(n + PH)
                    gate_exps(n + AHEAD, (h + AHEAD) % PH)
                    diagonals(n, parity, range(6, 9), P)
                    scores_out(n + PH, parity)
                    diagonals(n, parity, range(9, K), P)

                head_pairs(act, head)
                close(i, P)
            for h in range(PH):
                n = s.NB * PH + h
                gelus(n, h % 2, s.TS)
                diagonals(n, h % 2, range(0, 6), s.TS)
                if h + AHEAD < PH:
                    gate_exps(n + AHEAD, h + AHEAD)
                diagonals(n, h % 2, range(6, K), s.TS)
            close(s.NB, s.TS)

        @block.vector
        def _(dve):
            chain = Chain(dve, dve_chain)

            def settle(ins):
                chain.link(ins)
                dve.sem_inc(dve_held, 1)

            def choose(r, parity, slot, refill=True):
                dve.wait_ge(s_out, r + 2)
                dve.sem_inc(dve_held, 1)
                sc = half_s[:, parity, :, :]
                for p in range(2):
                    ins = nc.vector.max(top[:, p, 0:8], sc[:, p, :])
                settle(ins)
                for p in range(2):
                    nc.vector.max_index(top_i[:, p, 0:8], top[:, p, 0:8], sc[:, p, :])
                for p in range(2):
                    ins = nc.vector.match_replace(left[:, p, :], top[:, p, 0:8], sc[:, p, :], NEG)
                ins.then_inc(s_used, 1)
                dve.wait_ge(s_used, 2 + r + 1)
                dve.sem_inc(dve_held, 1)
                for p in range(2):
                    ins = nc.vector.max(top[:, p, 8:K], left[:, p, :])
                settle(ins)
                for p in range(2):
                    ins = nc.vector.max_index(top_i[:, p, 8:K], top[:, p, 8:K], left[:, p, :])
                nc.vector.tensor_tensor(out=cand[:, :, :], in0=top[:, 0, :].unsqueeze(2).broadcast_to([P, K, K]),
                                        in1=top[:, 1, :].unsqueeze(1).broadcast_to([P, K, K]), op=ALU.add).then_inc(dve_chain, 1)
                chain.n += 1
                dve.wait_ge(dve_chain, chain.base + chain.n)
                chain.link(nc.vector.tensor_copy(top_f[:, :, :], top_i[:, :, :]))
                dve.wait_ge(exps_ready, r + 1)
                dve.sem_inc(dve_held, 1)
                flat, flat_left = (t[:, :, :].rearrange("p a b -> p (a b)") for t in (cand, cand_left))
                settle(nc.vector.max(best[:, 0:8], flat))
                nc.vector.max_index(best_j[:, 0:8], best[:, 0:8], flat)
                settle(nc.vector.match_replace(flat_left, best[:, 0:8], flat, NEG))
                settle(nc.vector.max(best[:, 8:K], flat_left))
                settle(nc.vector.max_index(best_j[:, 8:K], best[:, 8:K], flat_left))
                nc.vector.tensor_scalar(nbest[:, :], best[:, 0:1], -1.0, None, ALU.mult).then_inc(best_ready, 1)
                nc.vector.tensor_scalar(ij[:, 0, :], best_j[:, :], 4, None, ALU.logical_shift_right)
                chain.link(nc.vector.tensor_scalar(ij[:, 1, :], best_j[:, :], K - 1, None, ALU.bitwise_and))
                chain.link(nc.vector.tensor_copy(ij_f[:, :, :], ij[:, :, :]))
                chain.link(nc.vector.tensor_tensor(out=hit[:, :, :, :], in0=ij_f[:, :, :].unsqueeze(3).broadcast_to([P, 2, K, K]),
                                                   in1=count[:, :].unsqueeze(1).unsqueeze(1).broadcast_to([P, 2, K, K]), op=ALU.is_equal))
                chain.link(nc.vector.tensor_tensor(out=hit[:, :, :, :], in0=hit[:, :, :, :],
                                                   in1=top_f[:, :, :].unsqueeze(2).broadcast_to([P, 2, K, K]), op=ALU.mult))
                chain.link(nc.vector.tensor_reduce(key_f[:, :, :], hit[:, :, :, :], AX.X, ALU.add))
                if refill:
                    dve.wait_ge(v_used, V_FREE + K * (r - PH + 1))
                nc.vector.scalar_tensor_tensor(out=experts[:, bass.ds(slot, 1), :].rearrange("p a k -> p (a k)"), in0=key_f[:, 0, :],
                                               scalar=float(s.NKEYS), in1=key_f[:, 1, :], op0=ALU.mult,
                                               op1=ALU.add).then_inc(experts_ready, 1)

            def dot(n, parity, rows):
                for k in range(K):
                    dve.wait_ge(u_here[k % RING], 16 * (USES * n + k // RING + 1))
                    row = u_rows[0:rows, k % RING, :]
                    nc.vector.tensor_tensor_reduce(out=row, in0=row, in1=xn[0:rows, :], scale=1.0, scalar=0.0, op0=ALU.mult,
                                                   op1=ALU.add, accum_out=dots[0:rows, parity, k:k + 1]).then_inc(u_used, 1)

            def weights(n, parity, h, rows):
                dve.wait_ge(exps_ready, n + 2)
                chain.link(nc.vector.reciprocal(gate_inv[0:rows, :], expsum[0:rows, bass.ds(h, 1)]))
                dve.wait_ge(gelu_ready, n + 1)
                dve.wait_ge(diag_ready, K * n + K)
                nc.vector.scalar_tensor_tensor(out=act_w[0:rows, parity, :], in0=gelu[0:rows, parity, :], scalar=gate_inv[0:rows, 0:1],
                                               in1=exps[0:rows, bass.ds(h, 1), :].rearrange("p a k -> p (a k)"),
                                               op0=ALU.mult, op1=ALU.mult).then_inc(act_ready, 1)

            def take_rows(b):
                dve.wait_ge(xn_moved, b + 1)
                nc.vector.tensor_copy(xn[:, :], xn_after[:, :]).then_inc(xn_taken, 1)
                dve.wait_ge(xn_taken, b + 2)
                dve.sem_inc(dve_held, 1)

            def add_residual(b, rows):
                final = Chain(dve, final_chain, 2 * b)
                dve.wait_ge(x1_here, 16 * (b + 1))
                dve.wait_ge(out_ready, b + 2)
                final.link(nc.vector.tensor_tensor(out=x2[0:rows, :], in0=x2[0:rows, :], in1=out_rows[0:rows, :], op=ALU.add))
                dve.sem_inc(out_used, 1)
                dve.wait_ge(y_stored, 16 * (b + 1))
                final.link(nc.vector.tensor_tensor_reduce(out=y[0:rows, :], in0=x2[0:rows, :], in1=x2[0:rows, :], scale=1.0, scalar=0.0,
                                                          op0=ALU.mult, op1=ALU.add, accum_out=rms[0:rows, 0:1]))
                nc.vector.tensor_scalar(rms[0:rows, 1:2], rms[0:rows, 0:1], 1.0 / s.D, RMS_EPS, ALU.mult, ALU.add).then_inc(ms_ready, 1)

            def normalise(b, rows):
                dve.wait_ge(rstd_ready, b + 1)
                nc.vector.scalar_tensor_tensor(out=y[0:rows, :], in0=x2[0:rows, :], scalar=rms[0:rows, 2:3], in1=gf[0:rows, :],
                                               op0=ALU.mult, op1=ALU.mult).then_inc(y_ready, 1)

            dve.sem_inc(u_used, U_FREE)
            dve.sem_inc(s_used, 2)
            dve.sem_inc(act_ready, 1)
            dve.sem_inc(exps_ready, 1)
            dve.sem_inc(out_used, 1)
            dve.sem_inc(xn_taken, 1)
            dve.sem_inc(y_ready, 1)
            dve.wait_ge(consts, 2)
            CHOOSE = 13
            for r in range(FIRST):
                choose(r, r % 2, r, refill=False)
            assert chain.n == FIRST * CHOOSE, chain.n
            take_rows(0)
            for h in range(PH):
                dot(h, h % 2, P)
                weights(h, h % 2, h, P)
                for r in CATCH_UP[h]:
                    choose(r, r % 2, r % PH, refill=r >= PH)
            dve.wait_ge(gf_here, 16)
            dve.sem_inc(dve_held, 1)
            with dve.Fori(1, s.NB) as i:
                take_rows(i)

                def head(h, parity):
                    n = i * PH + h
                    dot(n, parity, P)
                    chain.at((n + AHEAD) * CHOOSE + n)
                    weights(n, parity, h, P)
                    choose(n + AHEAD, parity, (h + AHEAD) % PH)

                head_pairs(dve, head, 0, 1)
                add_residual(i - 1, P)
                dve.sem_inc(dve_held, 1)
                head_pairs(dve, head, 1, PH // 2 - 1)
                normalise(i - 1, P)
                dve.sem_inc(dve_held, 1)
                head_pairs(dve, head, PH // 2 - 1, PH // 2)
            take_rows(s.NB)
            chain.at((s.NB * PH + AHEAD) * CHOOSE + s.NB * PH)
            for h in range(PH):
                n = s.NB * PH + h
                dot(n, h % 2, s.TS)
                weights(n, h % 2, h, s.TS)
                if h + AHEAD < PH:
                    choose(n + AHEAD, h % 2, h + AHEAD)
                if h == 1:
                    add_residual(s.NB - 1, P)
                if h == 5:
                    normalise(s.NB - 1, P)
            add_residual(s.NB, s.TS)
            normalise(s.NB, s.TS)


INPUTS = ["x_prompt", "x_sample", "cache_k", "cache_v", "cache_logf", "state_conv", "g_mix", "w_in", "b_f", "w_dw",
          "b_dw", "ln_g", "ln_b", "w_out", "g_ffn", "w_pq", "sub_keys", "u_emb", "v_emb", "g_final"]


def kernel(**inputs):
    import concourse.bacc as bacc
    from concourse.bass_utils import run_bass_kernel_spmd

    nc = bacc.Bacc("TRN2", target_bir_lowering=False, num_devices=1)
    arrays, args = {}, []
    for name in INPUTS:
        a = np.ascontiguousarray(inputs[name])
        arrays["in_" + name] = a
        args.append(nc.dram_tensor("in_" + name, a.shape, mybir.dt.from_np(a.dtype), kind="ExternalInput").ap())
    x_p, x_s, ck = (inputs[n].shape for n in ("x_prompt", "x_sample", "cache_k"))
    depth, heads, hd = ck[0], ck[3], ck[4]
    conv = inputs["state_conv"].shape[2:]
    outs = [x_p, x_s,
            (depth, *x_p[:2], heads, hd), (depth, *x_p[:2], heads, hd), (depth, *x_p[:2], heads), (depth, x_p[0], *conv),
            (depth, *x_s[:2], heads, hd), (depth, *x_s[:2], heads, hd), (depth, *x_s[:2], heads), (depth, x_s[0], *conv)]
    for i, shape in enumerate(outs):
        args.append(nc.dram_tensor(f"out_{i}", shape, F32, kind="ExternalOutput").ap())
    build(nc, *args)
    r = run_bass_kernel_spmd(nc, [arrays], core_ids=[0])
    return tuple(r.results[0][f"out_{i}"] for i in range(len(outs)))
```

```python
from contextlib import ExitStack

import numpy as np
import concourse.bass as bass
from concourse import mybir

F32 = mybir.dt.float32
U32 = mybir.dt.uint32
ALU = mybir.AluOpType
ACT = mybir.ActivationFunctionType
AX = mybir.AxisListType

P = 128
BANK = 512
MASKED = -1e30
LEAST = -87.0
RMS_EPS = 1e-6
LN_EPS = 1e-5


class Named:
    pass


class Chain:

    def __init__(self, eng, sem, base=0, held=None):
        self.eng, self.sem, self.base, self.n, self.held = eng, sem, base, 0, held

    def wait(self, sem, value):
        self.eng.wait_ge(sem, value)
        if self.held is not None:
            self.eng.sem_inc(self.held, 1)

    def link(self, ins):
        ins.then_inc(self.sem, 1)
        self.n += 1
        self.wait(self.sem, self.base + self.n)

    def at(self, base):
        self.base, self.n = base, 0
        return self


def sizes(x_prompt, x_sample, cache_k, w_in, w_dw, w_pq, sub_keys, u_emb):
    s = Named()
    s.D = x_prompt.shape[2]
    s.T = x_prompt.shape[1]
    s.TS = x_sample.shape[1]
    s.PAST, s.H, s.HD = cache_k.shape[2:]
    s.DA = s.H * s.HD
    s.TAPS, s.DC = w_dw.shape[1:]
    s.NIN = w_in.shape[2]
    s.DCH = s.D // P
    s.CCH = s.DC // P
    s.NB = s.T // P
    s.SAMPLE_KB = s.NB + 1
    s.NKB = s.NB + 2
    s.PH = sub_keys.shape[2]
    s.NKEYS = sub_keys.shape[3]
    s.HALF = sub_keys.shape[4]
    s.K = 16
    s.E = u_emb.shape[1]
    assert s.PAST == P and s.HALF == P and s.NKEYS == P and s.TS == P // 2 and s.H == 8 and s.PH == 8
    return s


def build(nc, x_prompt, x_sample, cache_k, cache_v, cache_logf, state_conv, g_mix, w_in, b_f, w_dw, b_dw,
          ln_g, ln_b, w_out, g_ffn, w_pq, sub_keys, u_emb, v_emb, g_final,
          y_prompt, y_sample, k_prompt, v_prompt, logf_prompt, conv_prompt,
          k_sample, v_sample, logf_sample, conv_sample):
    s = sizes(x_prompt, x_sample, cache_k, w_in, w_dw, w_pq, sub_keys, u_emb)
    d = Named()
    d.x_prompt, d.x_sample, d.cache_k, d.cache_v, d.cache_logf, d.state_conv = x_prompt, x_sample, cache_k, cache_v, cache_logf, state_conv
    d.g_mix, d.w_in, d.b_f, d.w_dw, d.b_dw, d.ln_g = g_mix, w_in, b_f, w_dw, b_dw, ln_g
    d.ln_b, d.w_out, d.g_ffn, d.w_pq, d.sub_keys, d.u_emb = ln_b, w_out, g_ffn, w_pq, sub_keys, u_emb
    d.v_emb, d.g_final, d.k_prompt, d.v_prompt, d.logf_prompt, d.conv_prompt = v_emb, g_final, k_prompt, v_prompt, logf_prompt, conv_prompt
    d.k_sample, d.v_sample, d.logf_sample, d.conv_sample, d.y_prompt, d.y_sample = k_sample, v_sample, logf_sample, conv_sample, y_prompt, y_sample
    d.x1 = nc.dram_tensor("x1_rows", (s.NB + 1, P, s.D), F32, kind="Internal").ap()
    d.xn2 = nc.dram_tensor("xn2_rows", (s.NB + 1, P, s.D), F32, kind="Internal").ap()
    with ExitStack() as ctx:
        g = Named()
        g.ident = ctx.enter_context(nc.sbuf_tensor("ident", [P, P], F32))
        g.neg_half = ctx.enter_context(nc.sbuf_tensor("neg_half", [P, 1], F32))
        g.ps = ctx.enter_context(nc.psum_tensor("ps", [P, 8, BANK], F32))
        with ExitStack() as mix:
            c = caches(nc, s, mix)
            phase_a(nc, s, d, g, c)
            phase_b(nc, s, d, g, c)
        phase_c(nc, s, d, g)


def caches(nc, s, ctx):
    c = Named()

    def sb(name, shape):
        return ctx.enter_context(nc.sbuf_tensor(name, shape, F32))

    c.keysT = sb("keysT", [s.HD + 1, s.H, s.NKB * P])
    c.values = sb("values", [P, s.NKB, s.DA])
    c.queries = sb("queries", [P, s.NB + 1, s.DA])
    c.convT = sb("convT", [P, s.CCH, (s.NB + 1) * P])
    c.cum = sb("cum", [P, s.NB + 1, s.H])
    c.vecT = sb("vecT", [P, s.DCH + 3 * s.CCH])
    c.g_mix = c.vecT[:, 0:s.DCH]
    c.b_dw, c.ln_g, c.ln_b = (c.vecT[:, s.DCH + i * s.CCH:s.DCH + (i + 1) * s.CCH] for i in range(3))
    return c


def phase_a(nc, s, d, g, c):
    with ExitStack() as ctx:
        def sb(name, shape):
            return ctx.enter_context(nc.sbuf_tensor(name, shape, F32))

        def sem(name):
            return ctx.enter_context(nc.semaphore(name))

        COLS = {}
        at = 0
        for name, width in (("q", s.DA), ("k", s.DA), ("v", s.DA), ("f", s.H), ("a", s.DC), ("gate", s.DC)):
            COLS[name] = (at, width)
            at += width
        ORDER = ("gate", "a", "f", "k", "q", "v")
        NPROJ = len(ORDER)
        HALO = s.TAPS - 1

        w_in = sb("w_in_sb", [P, s.DCH, s.NIN])
        x = sb("x_a", [P, s.D])
        xn = sb("xn_a", [P, s.D])
        hT = sb("hT_a", [P, s.DCH, P])
        k_aug = sb("k_aug", [P, s.H, s.HD + 1])
        sig = sb("sig_a", [P, s.DC])
        u = sb("u_a", [P, s.DC])
        uT = sb("uT_a", [P, s.CCH, HALO + P])
        upto = sb("upto", [P, P])
        last_row = sb("last_row", [P, P])
        bf = sb("bf_rows", [P, s.H])
        ss = sb("ss_a", [P, 1])
        ms = sb("ms_a", [P, 1])
        rstd = sb("rstd_a", [P, 1])
        z = sb("z_a", [P, s.H])
        az = sb("az_a", [P, s.H])
        ez = sb("ez_a", [P, s.H])
        ln = sb("ln_a", [P, s.H])
        pz = sb("pz_a", [P, 4, s.H])
        logf = sb("logf_a", [P, s.H])
        logfs = sb("logfs", [P, s.NB + 1, s.H])
        cum = sb("cum_a", [P, s.H])
        cum_past = sb("cum_past", [P, s.H])
        logf_past = sb("logf_past", [P, s.H])
        taps = sb("taps", [s.TAPS, s.DC])
        tapsT = sb("tapsT", [P, s.CCH, s.TAPS])
        NVEC = s.DCH + 3 * s.CCH
        vecs = sb("vecs", [NVEC, P])
        state = sb("state", [HALO, s.DC])
        stateT = sb("stateT", [P, s.CCH, HALO])

        w_here = {n: sem("w_here_" + n) for n in ORDER}
        x_here = sem("x_here_a")
        small_here = sem("small_here")
        past_here = sem("past_here")
        consts = sem("consts_a")
        setup_psum = sem("setup_psum")
        setup_sb = sem("setup_sb")
        ms_ready = sem("ms_ready_a")
        rstd_ready = sem("rstd_ready_a")
        xn_ready = sem("xn_ready_a")
        hT_psum = sem("hT_psum_a")
        hT_ready = sem("hT_ready_a")
        proj_psum = sem("proj_psum")
        sig_ready = sem("sig_ready_a")
        u_ready = sem("u_ready")
        uT_psum = sem("uT_psum")
        uT_ready = sem("uT_ready")
        z_ready = sem("z_ready")
        ez_ready = sem("ez_ready")
        ln_ready = sem("ln_ready")
        logf_ready = sem("logf_ready")
        cum_psum = sem("cum_psum")
        cum_ready = sem("cum_ready")
        kaug_ready = sem("kaug_ready")
        q_ready = sem("q_ready_a")
        k_ready = sem("k_ready")
        v_ready = sem("v_ready")
        kT_psum = sem("kT_psum")
        kT_ready = sem("kT_ready")
        k_stored = sem("k_stored")
        v_stored = sem("v_stored")
        misc_stored = sem("misc_stored")
        act_chain, dve_chain, pool_chain = sem("act_chain_a"), sem("dve_chain_a"), sem("pool_chain_a")
        pool_held = sem("pool_held_a")

        ps = g.ps
        BLOCKS = s.NB + 1
        HB, GATE, A_, F_, Q_, K_, V_ = 0, 2, 3, 4, 5, 6, 7
        BANK_OF = {"gate": GATE, "a": A_, "f": F_, "q": Q_, "k": K_, "v": V_}
        KTB, UTB = 2, 0
        PAST = 1

        block = ctx.enter_context(nc.Block())

        @block.sync
        def _(sp):
            sp.dma_start(x[:, :], d.x_prompt[0, 0:P, :]).then_inc(x_here, 16)
            sp.dma_start(vecs[0:s.DCH, :], d.g_mix[0].rearrange("(c p) -> c p", p=P)).then_inc(small_here, 16)
            for i, v in enumerate((d.b_dw, d.ln_g, d.ln_b)):
                lo = s.DCH + i * s.CCH
                sp.dma_start(vecs[lo:lo + s.CCH, :], v[0].rearrange("(c p) -> c p", p=P)).then_inc(small_here, 16)
            sp.dma_start(taps[:, :], d.w_dw[0]).then_inc(small_here, 16)
            sp.dma_start(state[:, :], d.state_conv[0, 0]).then_inc(small_here, 16)
            sp.dma_start(bf[:, :], d.b_f[0].partition_broadcast(P)).then_inc(small_here, 16)
            sp.dma_start(k_aug[:, :, 0:s.HD], d.cache_k[0, 0]).then_inc(past_here, 16)
            sp.dma_start(logf_past[:, :], d.cache_logf[0, 0]).then_inc(past_here, 16)
            sp.dma_start(c.values[:, s.NB, :], d.cache_v[0, 0].rearrange("t h e -> t (h e)")).then_inc(past_here, 16)
            w_rows = d.w_in[0].rearrange("(c p) n -> p c n", p=P)
            for name in ORDER:
                lo, width = COLS[name]
                sp.dma_start(w_in[:, :, lo:lo + width], w_rows[:, :, lo:lo + width]).then_inc(w_here[name], 16)

            def stores(b, kb, k_out, v_out, rows):
                sp.wait_ge(k_ready, b + 2)
                sp.dma_start(k_out, k_aug[0:rows, :, 0:s.HD]).then_inc(k_stored, 16)
                sp.wait_ge(v_ready, b + 2)
                sp.dma_start(v_out, c.values[0:rows, kb, :]).then_inc(v_stored, 16)

            def prompt_stores(b):
                if isinstance(b, int):
                    v = c.values[:, b, :]
                else:
                    v = c.values[:, bass.ds(b, 1), :].rearrange("p a n -> p (a n)")
                sp.wait_ge(k_ready, b + 2)
                sp.dma_start(k_rows[bass.ds(b * P, P)], k_aug[:, :, 0:s.HD]).then_inc(k_stored, 16)
                sp.wait_ge(v_ready, b + 2)
                sp.dma_start(v_rows[bass.ds(b * P, P), :], v).then_inc(v_stored, 16)

            sp.sem_inc(k_stored, 16)
            k_rows = d.k_prompt[0, 0]
            v_rows = d.v_prompt[0, 0].rearrange("t h e -> t (h e)")
            with sp.Fori(0, s.NB - 1) as b:
                sp.wait_ge(xn_ready, b + 1)
                sp.dma_start(x[:, :], d.x_prompt[0, bass.ds((b + 1) * P, P), :]).then_inc(x_here, 16)
                prompt_stores(b)
            sp.wait_ge(xn_ready, s.NB)
            sp.dma_start(x[0:s.TS, :], d.x_sample[0]).then_inc(x_here, 16)
            prompt_stores(s.NB - 1)
            sp.wait_ge(u_ready, 1 + s.NB)
            sp.dma_start(d.conv_prompt[0, 0], u[P - HALO:P, :]).then_inc(misc_stored, 16)
            stores(s.NB, s.SAMPLE_KB, d.k_sample[0, 0], d.v_sample[0, 0].rearrange("t h e -> t (h e)"), s.TS)
            sp.wait_ge(u_ready, 1 + BLOCKS)
            sp.dma_start(d.conv_sample[0, 0], u[s.TS - HALO:s.TS, :]).then_inc(misc_stored, 16)
            sp.wait_ge(logf_ready, 1 + 2 * BLOCKS)
            sp.dma_start(d.logf_prompt[0, 0].rearrange("(b p) h -> p b h", p=P), logfs[:, 0:s.NB, :]).then_inc(misc_stored, 16)
            sp.dma_start(d.logf_sample[0, 0], logfs[0:s.TS, s.NB, :]).then_inc(misc_stored, 16)
            sp.wait_ge(k_stored, 16 * (1 + BLOCKS))
            sp.wait_ge(v_stored, 16 * BLOCKS)
            sp.wait_ge(misc_stored, 64)

        @block.gpsimd
        def _(pool):
            chain = Chain(pool, pool_chain, held=pool_held)
            chain.link(nc.gpsimd.memset(g.ident[:, :], 0.0))
            nc.gpsimd.affine_select(out=g.ident[:, :], in_=g.ident[:, :], compare_op=ALU.not_equal, fill=1.0,
                                    base=0, pattern=[[-1, P]], channel_multiplier=1).then_inc(consts, 1)
            nc.gpsimd.memset(g.neg_half[:, :], -0.5)
            chain.link(nc.gpsimd.memset(upto[:, :], 1.0))
            nc.gpsimd.affine_select(out=upto[:, :], in_=upto[:, :], compare_op=ALU.is_ge, fill=0.0,
                                    base=0, pattern=[[1, P]], channel_multiplier=-1).then_inc(consts, 1)
            chain.link(nc.gpsimd.memset(last_row[:, :], 0.0))
            nc.gpsimd.affine_select(out=last_row[:, :], in_=last_row[:, :], compare_op=ALU.not_equal, fill=1.0,
                                    base=1 - P, pattern=[[0, P]], channel_multiplier=1).then_inc(consts, 1)
            pool.wait_ge(past_here, 48)
            pool.wait_ge(cum_ready, 1)
            nc.gpsimd.tensor_scalar(k_aug[:, :, s.HD], cum_past[:, :], -1.0, None, ALU.mult).then_inc(kaug_ready, 1)
            SETUP_LINKS = chain.n
            LINKS = 3

            def rms_scale(b):
                chain.wait(ms_ready, b + 1)
                nc.gpsimd.tensor_tensor(out=rstd[:, :], in0=ms[:, :], in1=g.neg_half[:, :], op=ALU.pow).then_inc(rstd_ready, 1)

            def log_forget(b, blk):
                chain.wait(ez_ready, b + 1)
                chain.link(nc.gpsimd.tensor_scalar(pz[:, 0, :], ez[:, :], 1.0, -1.0, ALU.add, ALU.add))
                nc.gpsimd.tensor_tensor(out=pz[:, 1, :], in0=ez[:, :], in1=pz[:, 0, :], op=ALU.subtract)
                chain.wait(ln_ready, b + 1)
                chain.link(nc.gpsimd.tensor_scalar(pz[:, 3, :], z[:, :], 0.0, None, ALU.min))
                chain.link(nc.gpsimd.tensor_tensor(out=pz[:, 2, :], in0=ln[:, :], in1=pz[:, 1, :], op=ALU.add))
                chain.wait(cum_psum, b + 1)
                nc.gpsimd.tensor_tensor(out=logf[:, :], in0=pz[:, 3, :], in1=pz[:, 2, :], op=ALU.subtract).then_inc(logf_ready, 1)
                chain.wait(logf_ready, 2 * b + 2)
                nc.gpsimd.tensor_copy(blk(logfs), logf[:, :]).then_inc(logf_ready, 1)

            def cum_columns(b, blk):
                chain.wait(cum_ready, PAST + b + 1)
                nc.gpsimd.tensor_copy(blk(c.cum), cum[:, :])
                chain.wait(kT_psum, PAST + b)
                nc.gpsimd.tensor_scalar(k_aug[:, :, s.HD], cum[:, :], -1.0, None, ALU.mult).then_inc(kaug_ready, 1)

            pool.sem_inc(logf_ready, 1)
            rms_scale(0)
            with pool.Fori(0, s.NB) as b:
                chain.at(SETUP_LINKS + b * LINKS)
                blk = lambda t: t[:, bass.ds(b, 1), :].rearrange("p a n -> p (a n)")
                rms_scale(b + 1)
                log_forget(b, blk)
                cum_columns(b, blk)
                assert chain.n == LINKS
            chain.at(SETUP_LINKS + s.NB * LINKS)
            log_forget(s.NB, lambda t: t[:, s.NB, :])
            cum_columns(s.NB, lambda t: t[:, s.NB, :])

        @block.scalar
        def _(act):
            chain = Chain(act, act_chain)
            act.wait_ge(setup_psum, 3)
            nc.scalar.copy(tapsT[:, :, :], ps[:, Q_, 0:s.CCH * s.TAPS].rearrange("p (c j) -> p c j", c=s.CCH)).then_inc(setup_sb, 1)
            nc.scalar.copy(c.vecT[:, :], ps[:, K_, 0:NVEC]).then_inc(setup_sb, 1)
            nc.scalar.copy(stateT[:, :, :], ps[:, V_, 0:s.CCH * HALO].rearrange("p (c j) -> p c j", c=s.CCH)).then_inc(setup_sb, 1)
            act.wait_ge(cum_psum, 1)
            nc.scalar.copy(cum_past[:, :], ps[:, F_, s.H:2 * s.H]).then_inc(cum_ready, 1)

            def keys_out(kcount, kb):
                act.wait_ge(kT_psum, kcount)
                for i in range(2):
                    src = ps[0:s.HD + 1, KTB + i, :].rearrange("p (h t) -> p h t", t=P)
                    ins = nc.scalar.copy(c.keysT[:, 4 * i:4 * i + 4, bass.ds(kb * P, P)], src)
                ins.then_inc(kT_ready, 1)

            def row_scale(b):
                act.wait_ge(x_here, 16 * (b + 1))
                chain.link(nc.scalar.activation(xn[:, :], x[:, :], ACT.Square, accum_out=ss[:, :]))
                nc.scalar.activation(ms[:, :], ss[:, :], ACT.Copy, bias=RMS_EPS, scale=1.0 / s.D).then_inc(ms_ready, 1)

            def normed(b):
                act.wait_ge(rstd_ready, b + 1)
                nc.scalar.mul(xn[:, :], x[:, :], rstd[:, 0:1]).then_inc(xn_ready, 1)

            def iteration(b, kb, q_dst, v_dst, prepare_next):
                act.wait_ge(setup_sb, 2)
                for i in range(s.DCH):
                    if i % 4 == 0:
                        act.wait_ge(hT_psum, 2 * b + i // 4 + 1)
                    nc.scalar.mul(hT[:, i, :], ps[:, HB + i // 4, (i % 4) * P:(i % 4 + 1) * P], c.g_mix[:, i:i + 1]).then_inc(hT_ready, 1)
                if prepare_next:
                    row_scale(b + 1)
                act.wait_ge(proj_psum, NPROJ * b + 1)
                act.wait_ge(u_ready, b + 1)
                nc.scalar.activation(sig[:, :], ps[:, GATE, :], ACT.Sigmoid).then_inc(sig_ready, 1)
                if prepare_next:
                    normed(b + 1)
                act.wait_ge(z_ready, b + 1)
                act.wait_ge(logf_ready, 2 * b + 1)
                chain.link(nc.scalar.activation(az[:, :], z[:, :], ACT.Abs))
                nc.scalar.activation(ez[:, :], az[:, :], ACT.Exp, scale=-1.0).then_inc(ez_ready, 1)
                act.wait_ge(ez_ready, b + 1)
                nc.scalar.activation(ln[:, :], ez[:, :], ACT.Ln, bias=1.0).then_inc(ln_ready, 1)
                act.wait_ge(proj_psum, NPROJ * b + 4)
                act.wait_ge(kT_psum, PAST + b)
                act.wait_ge(k_stored, 16 * b + 16)
                nc.scalar.copy(k_aug[:, :, 0:s.HD], ps[:, K_, :].rearrange("p (h e) -> p h e", e=s.HD)).then_inc(k_ready, 1)
                act.wait_ge(cum_psum, PAST + b + 1)
                act.wait_ge(kaug_ready, PAST + b)
                nc.scalar.copy(cum[:, :], ps[:, F_, s.H:2 * s.H]).then_inc(cum_ready, 1)
                act.wait_ge(proj_psum, NPROJ * b + 5)
                nc.scalar.mul(q_dst, ps[:, Q_, :], s.HD ** -0.5).then_inc(q_ready, 1)
                keys_out(PAST + b + 1, kb)
                act.wait_ge(proj_psum, NPROJ * b + 6)
                nc.scalar.copy(v_dst, ps[:, V_, :]).then_inc(v_ready, 1)

            keys_out(PAST, s.NB)
            for free in (q_ready, k_ready, v_ready):
                act.sem_inc(free, 1)
            row_scale(0)
            normed(0)
            SETUP_LINKS, LINKS = chain.n, 2
            with act.Fori(0, s.NB) as b:
                chain.at(SETUP_LINKS + b * LINKS)
                iteration(b, b, c.queries[:, bass.ds(b, 1), :].rearrange("p a n -> p (a n)"),
                          c.values[:, bass.ds(b, 1), :].rearrange("p a n -> p (a n)"), True)
                assert chain.n == LINKS
            chain.at(SETUP_LINKS + s.NB * LINKS)
            iteration(s.NB, s.SAMPLE_KB, c.queries[:, s.NB, :], c.values[:, s.SAMPLE_KB, :], False)

        @block.tensor
        def _(pe):
            pe.wait_ge(consts, 3)
            pe.wait_ge(small_here, 16 * 7)
            for i in range(s.CCH):
                pe.transpose(ps[:, Q_, i * s.TAPS:(i + 1) * s.TAPS], taps[:, i * P:(i + 1) * P], g.ident[0:s.TAPS, 0:s.TAPS])
            pe.transpose(ps[:, K_, 0:NVEC], vecs[:, :], g.ident[0:NVEC, 0:NVEC])
            for i in range(s.CCH):
                ins = pe.transpose(ps[:, V_, i * HALO:(i + 1) * HALO], state[:, i * P:(i + 1) * P], g.ident[0:HALO, 0:HALO])
            ins.then_inc(setup_psum, 3)
            pe.wait_ge(past_here, 48)
            pe.matmul(ps[:, F_, s.H:2 * s.H], upto[:, :], logf_past[:, :], start=True, stop=True).then_inc(cum_psum, 1)

            def keys_in(kcount):
                pe.wait_ge(kaug_ready, kcount)
                for h in range(s.H):
                    ins = pe.transpose(ps[0:s.HD + 1, KTB + h // 4, (h % 4) * P:(h % 4 + 1) * P], k_aug[:, h, :], g.ident[:, :])
                ins.then_inc(kT_psum, 1)

            def iteration(b, cum_before):
                pe.wait_ge(uT_ready, b + 1)
                pe.wait_ge(xn_ready, b + 1)
                for i in range(s.DCH):
                    ins = pe.transpose(ps[:, HB + i // 4, (i % 4) * P:(i % 4 + 1) * P], xn[:, i * P:(i + 1) * P], g.ident[:, :])
                    if i % 4 == 3:
                        ins.then_inc(hT_psum, 1)
                for name in ORDER:
                    lo, width = COLS[name]
                    pe.wait_ge(w_here[name], 16)
                    if name == "gate":
                        pe.wait_ge(kT_ready, PAST + b)
                    if name == "f":
                        pe.wait_ge(cum_ready, PAST + b)
                    if name == "q":
                        pe.wait_ge(q_ready, b + 1)
                    if name == "k":
                        pe.wait_ge(k_ready, b + 1)
                    if name == "v":
                        pe.wait_ge(v_ready, b + 1)
                    for i in range(s.DCH):
                        if name == "gate":
                            pe.wait_ge(hT_ready, s.DCH * b + i + 1)
                        if name == "v" and i == 0:
                            pe.wait_ge(logf_ready, 2 * b + 2)
                            pe.matmul(ps[:, F_, s.H:2 * s.H], upto[:, :], logf[:, :], start=True, stop=False)
                            pe.matmul(ps[:, F_, s.H:2 * s.H], last_row[:, :], cum_before, start=False, stop=True).then_inc(cum_psum, 1)
                        if name == "v" and i == s.DCH // 2:
                            keys_in(PAST + b + 1)
                        ins = pe.matmul(ps[:, BANK_OF[name], 0:width], hT[:, i, :], w_in[:, i, lo:lo + width],
                                        start=(i == 0), stop=(i == s.DCH - 1))
                    ins.then_inc(proj_psum, 1)
                    if name == "k":
                        pe.wait_ge(u_ready, b + 2)
                        for i in range(s.CCH):
                            ins = pe.transpose(ps[:, UTB, i * P:(i + 1) * P], u[:, i * P:(i + 1) * P], g.ident[:, :])
                        ins.then_inc(uT_psum, 1)

            keys_in(PAST)
            with pe.Fori(0, s.NB) as b:
                iteration(b, cum[:, :])
            iteration(s.NB, cum_past[:, :])

        @block.vector
        def _(dve):
            chain = Chain(dve, dve_chain)
            chain.link(nc.vector.memset(cum[:, :], 0.0))
            chain.link(nc.vector.memset(uT[:, :, 0:HALO], 0.0))
            chain.link(nc.vector.memset(c.convT[:, :, s.NB * P + s.TS:], 0.0))
            dve.wait_ge(setup_sb, 3)

            def iteration(b, y_of, rows, last):
                dve.wait_ge(proj_psum, NPROJ * b + 2)
                dve.wait_ge(sig_ready, b + 1)
                nc.vector.tensor_tensor(out=u[:, :], in0=ps[:, A_, :], in1=sig[:, :], op=ALU.mult).then_inc(u_ready, 1)
                dve.wait_ge(proj_psum, NPROJ * b + 3)
                nc.vector.tensor_tensor(out=z[:, :], in0=ps[:, F_, 0:s.H], in1=bf[:, :], op=ALU.add).then_inc(z_ready, 1)
                dve.wait_ge(uT_psum, b + 1)
                nc.vector.tensor_copy(uT[:, :, HALO:HALO + P], ps[:, UTB, :].rearrange("p (c t) -> p c t", t=P)).then_inc(uT_ready, 1)
                dve.wait_ge(uT_ready, b + 2)
                for j in range(s.TAPS):
                    for i in range(s.CCH):
                        src, dst = uT[:, i, j:j + rows], y_of(i)
                        if j == 0:
                            ins = nc.vector.tensor_scalar(dst, src, tapsT[:, i, 0:1], c.b_dw[:, i:i + 1], ALU.mult, ALU.add)
                        else:
                            dve.wait_ge(dve_chain, chain.base + chain.n - s.CCH + 1)
                            ins = nc.vector.scalar_tensor_tensor(out=dst, in0=src, scalar=tapsT[:, i, j:j + 1], in1=dst,
                                                                 op0=ALU.mult, op1=ALU.add)
                        ins.then_inc(dve_chain, 1)
                        chain.n += 1
                dve.wait_ge(dve_chain, chain.base + chain.n)
                if not last:
                    chain.link(nc.vector.tensor_copy(uT[:, :, 0:HALO], uT[:, :, P:P + HALO]))

            for free in (u_ready, uT_ready):
                dve.sem_inc(free, 1)
            SETUP_LINKS, LINKS = chain.n, s.TAPS * s.CCH + 1
            with dve.Fori(0, s.NB) as b:
                chain.at(SETUP_LINKS + b * LINKS)
                iteration(b, lambda i: c.convT[:, i, bass.ds(b * P, P)], P, False)
                assert chain.n == LINKS
            chain.at(SETUP_LINKS + s.NB * LINKS)
            chain.link(nc.vector.tensor_copy(uT[:, :, 0:HALO], stateT[:, :, :]))
            dve.wait_ge(misc_stored, 16)
            iteration(s.NB, lambda i: c.convT[:, i, s.NB * P:s.NB * P + s.TS], s.TS, True)


def phase_b(nc, s, d, g, c):
    with ExitStack() as ctx:
        def sb(name, shape):
            return ctx.enter_context(nc.sbuf_tensor(name, shape, F32))

        def sem(name):
            return ctx.enter_context(nc.semaphore(name))

        PAIR = 2
        HALF = BANK // P
        SPAN = PAIR * P
        assert SPAN <= BANK and BANK % SPAN == 0 and s.CCH == 4 and s.DA == BANK

        w_out = sb("w_out_sb", [P, s.DCH, s.D])
        mask = sb("mask", [P, 2 * SPAN - P])
        q_aug = sb("q_aug", [P, s.H, s.HD + 1])
        qT = sb("qT_b", [s.HD + 1, s.H, P])
        y_st = sb("y_st", [P, s.CCH, P])
        cb = sb("cum_b", [P, s.H])
        scores = sb("scores", [P, 2, s.T])
        probs = sb("probs", [P, 2, s.T])
        probsT = sb("probsT", [P, s.T])
        top = sb("row_max", [P, s.H])
        ntop = sb("neg_row_max", [P, s.H])
        rs = sb("row_sum", [P, s.H])
        rinv = sb("row_sum_inv", [P, s.H])
        stats = sb("ln_stats", [P, 6])
        mv = sb("ln_mv", [P, 2])
        var = sb("ln_var", [P, 1])
        lnr = sb("ln_rstd", [P, 1])
        z = sb("z_b", [P, s.DC])
        ew = sb("ew_b", [P, s.CCH, P])
        held_yn = sb("held_yn", [P, s.CCH, P])
        yn = sb("yn_b", [P, s.CCH, P])
        o = sb("o_b", [P, s.DA])
        catT = sb("catT", [P, s.DCH, P])
        xres = sb("xres_b", [P, s.D])
        x1 = sb("x1_b", [P, s.D])
        sq = sb("sq_b", [P, s.D])
        xn = sb("xn_b", [P, s.D])
        gf = sb("g_ffn_rows", [P, s.D])
        rms = sb("rms_b", [P, 3])

        w_here, x_here, gf_here = sem("w_here_b"), sem("x_here_b"), sem("gf_here")
        consts = sem("consts_b")
        q_staged, y_staged, c_staged = sem("q_staged"), sem("y_staged"), sem("c_staged")
        qT_psum, qT_ready = sem("qT_psum"), sem("qT_ready")
        s_psum, top_ready, p_ready = sem("s_psum"), sem("top_ready"), sem("p_ready")
        pT_psum, pTa_ready, pTd_ready, pv_psum = sem("pT_psum"), sem("pTa_ready"), sem("pTd_ready"), sem("pv_psum")
        y_psum, mv_ready, lnr_ready, z_ready = sem("y_psum"), sem("mv_ready"), sem("lnr_ready"), sem("z_ready_b")
        zT_psum, ew_ready, conv_ready = sem("zT_psum"), sem("ew_ready"), sem("conv_ready")
        yn_ready, last_rms_ready = sem("yn_ready"), sem("last_rms_ready")
        o_ready, oT_psum, oT_ready = sem("o_ready"), sem("oT_psum"), sem("oT_ready")
        x1_psum, x1_ready, ss_ready, xn_ready = sem("x1_psum"), sem("x1_ready"), sem("ss_ready"), sem("xn_ready_b")
        x1_stored, xn_stored = sem("x1_stored"), sem("xn_stored")
        dve_chain, pool_chain, pool_held, dve_held = (sem(n + "_b") for n in ("dve_chain", "pool_chain", "pool_held", "dve_held"))

        ps = g.ps
        S_, PT_, O_, T_, X1_ = 0, 4, 6, 7, 2
        H = s.H
        BLOCKS = s.NB + 1

        def over_blocks(eng, body):
            for first in range(0, s.NB, PAIR):
                with eng.Fori(first, first + PAIR) as b:
                    body(b, nkb=first + PAIR, kb0=0, mask_at=lambda b: SPAN - P - (b - first) * P)
            body(s.NB, nkb=PAIR, kb0=s.NB, mask_at=lambda b: SPAN - 2 * P)

        block = ctx.enter_context(nc.Block())

        @block.sync
        def _(sp):
            sp.dma_start(xres[:, :], d.x_prompt[0, 0:P, :]).then_inc(x_here, 16)
            sp.dma_start(gf[:, :], d.g_ffn[0].partition_broadcast(P)).then_inc(gf_here, 16)
            sp.dma_start(w_out[:, :, :], d.w_out[0].rearrange("(c p) n -> p c n", p=P)).then_inc(w_here, 16)
            x1_rows = d.x1.rearrange("b p n -> (b p) n")
            xn_rows = d.xn2.rearrange("b p n -> (b p) n")

            def store_x1(b):
                sp.dma_start(x1_rows[bass.ds(b * P, P), :], x1[:, :]).then_inc(x1_stored, 16)

            def store_xn(b):
                sp.wait_ge(xn_ready, b + 2)
                sp.dma_start(xn_rows[bass.ds(b * P, P), :], xn[:, :]).then_inc(xn_stored, 16)

            sp.sem_inc(x1_stored, 16)
            sp.sem_inc(xn_stored, 16)
            with sp.Fori(0, s.NB - 1) as b:
                sp.wait_ge(x1_ready, b + 2)
                sp.dma_start(xres[:, :], d.x_prompt[0, bass.ds((b + 1) * P, P), :]).then_inc(x_here, 16)
                store_x1(b)
                store_xn(b)
            sp.wait_ge(x1_ready, s.NB + 1)
            sp.dma_start(xres[0:s.TS, :], d.x_sample[0]).then_inc(x_here, 16)
            store_x1(s.NB - 1)
            store_xn(s.NB - 1)
            sp.wait_ge(x1_ready, s.NB + 2)
            store_x1(s.NB)
            store_xn(s.NB)
            sp.wait_ge(x1_stored, 16 * (BLOCKS + 1))
            sp.wait_ge(xn_stored, 16 * (BLOCKS + 1))

        @block.gpsimd
        def _(pool):
            chain = Chain(pool, pool_chain, held=pool_held)
            FIRST_LINKS, LINKS = 4, 4

            def stage_queries(b, queries):
                chain.wait(qT_psum, b + 1)
                nc.gpsimd.tensor_copy(q_aug[:, :, 0:s.HD], queries.rearrange("p (h e) -> p h e", e=s.HD)).then_inc(q_staged, 1)

            def stage_others(b, conv, cum):
                chain.wait(y_psum, b + 1)
                nc.gpsimd.tensor_copy(y_st[:, :, :], conv).then_inc(y_staged, 1)
                chain.wait(top_ready, H * b + 1)
                nc.gpsimd.tensor_copy(cb[:, :], cum).then_inc(c_staged, 1)

            def layer_norm_scale(b):
                chain.wait(mv_ready, b + 1)
                chain.link(nc.gpsimd.tensor_scalar(var[:, :], mv[:, 1:2], LN_EPS, None, ALU.add))
                nc.gpsimd.tensor_tensor(out=lnr[:, :], in0=var[:, :], in1=g.neg_half[:, :], op=ALU.pow).then_inc(lnr_ready, 1)

            def inverse_rms(b):
                chain.wait(ss_ready, b + 1)
                chain.link(nc.gpsimd.tensor_scalar(rms[:, 1:2], rms[:, 0:1], 1.0 / s.D, RMS_EPS, ALU.mult, ALU.add))
                chain.link(nc.gpsimd.tensor_tensor(out=rms[:, 2:3], in0=rms[:, 1:2], in1=g.neg_half[:, :], op=ALU.pow))

            def normed(b):
                chain.wait(xn_stored, 16 * (b + 1))
                chain.link(nc.gpsimd.tensor_scalar(xn[:, :], x1[:, :], rms[:, 2:3], None, ALU.mult))
                nc.gpsimd.tensor_tensor(out=xn[:, :], in0=xn[:, :], in1=gf[:, :], op=ALU.mult).then_inc(xn_ready, 1)

            def stage_next(b):
                stage_queries(b + 1, c.queries[:, bass.ds(b + 1, 1), :].rearrange("p a n -> p (a n)"))
                stage_others(b + 1, c.convT[:, :, bass.ds((b + 1) * P, P)],
                             c.cum[:, bass.ds(b + 1, 1), :].rearrange("p a n -> p (a n)"))

            pool.sem_inc(xn_ready, 1)
            nc.gpsimd.memset(q_aug[:, :, s.HD], 1.0)
            stage_queries(0, c.queries[:, 0, :])
            chain.link(nc.gpsimd.memset(mask[:, :], 0.0))
            nc.gpsimd.affine_select(out=mask[:, :], in_=mask[:, :], compare_op=ALU.is_ge, fill=MASKED,
                                    base=SPAN - P, pattern=[[-1, 2 * SPAN - P]], channel_multiplier=1).then_inc(consts, 1)
            stage_others(0, c.convT[:, :, 0:P], c.cum[:, 0, :])
            layer_norm_scale(0)
            stage_next(0)
            inverse_rms(0)
            assert chain.n == FIRST_LINKS, chain.n
            pool.wait_ge(gf_here, 16)
            with pool.Fori(1, s.NB) as b:
                chain.at(FIRST_LINKS + (b - 1) * LINKS)
                layer_norm_scale(b)
                normed(b - 1)
                stage_next(b)
                inverse_rms(b)
                assert chain.n == LINKS
            chain.at(FIRST_LINKS + (s.NB - 1) * LINKS)
            layer_norm_scale(s.NB)
            normed(s.NB - 1)
            inverse_rms(s.NB)
            pool.sem_inc(last_rms_ready, 1)

        @block.tensor
        def _(pe):
            for free in (qT_psum, y_psum):
                pe.sem_inc(free, 1)

            def body(b, nkb, kb0, mask_at):
                def scores_of(h):
                    masked_from = nkb * P - SPAN
                    starts = list(range(0, masked_from, BANK)) + [masked_from]
                    for at, end in zip(starts, starts[1:] + [nkb * P]):
                        out = ps[:, S_ + 2 * (h % 2) + at // BANK, at % BANK:at % BANK + end - at]
                        ins = pe.matmul(out, qT[:, h, :], c.keysT[:, h, kb0 * P + at:kb0 * P + end],
                                        start=True, stop=at != masked_from)
                    pe.matmul(out, g.ident[:, :], mask[:, bass.ds(mask_at(b), SPAN)], start=False, stop=True).then_inc(s_psum, 1)

                def turn_probs(h):
                    pe.wait_ge(p_ready, 2 + H * b + h + 1)
                    for i in range(nkb):
                        ins = pe.transpose(ps[:, PT_ + i // 4, (i % 4) * P:(i % 4 + 1) * P],
                                           probs[:, h % 2, i * P:(i + 1) * P], g.ident[:, :])
                    ins.then_inc(pT_psum, 1)

                def weigh_values(h):
                    pe.wait_ge(pTa_ready, H * b + h + 1)
                    if nkb > HALF:
                        pe.wait_ge(pTd_ready, H * (b - HALF) + h + 1)
                    for i in range(nkb):
                        ins = pe.matmul(ps[:, O_, h * s.HD:(h + 1) * s.HD], probsT[:, i * P:(i + 1) * P],
                                        c.values[:, kb0 + i, h * s.HD:(h + 1) * s.HD], start=(i == 0), stop=(i == nkb - 1))
                    ins.then_inc(pv_psum, 1)

                def project(half, chunks):
                    for i in chunks:
                        ins = pe.matmul(ps[:, X1_ + half, :], catT[:, i, :], w_out[:, i, half * BANK:(half + 1) * BANK],
                                        start=(i == s.CCH), stop=(i == s.CCH - 1))
                    return ins

                pe.wait_ge(consts, 1)
                pe.wait_ge(qT_ready, b + 1)
                scores_of(0)
                pe.wait_ge(y_staged, b + 1)
                for i in range(s.CCH):
                    ins = pe.transpose(ps[:, T_, i * P:(i + 1) * P], y_st[:, i, :], g.ident[:, :])
                ins.then_inc(y_psum, 1)
                pe.wait_ge(x1_ready, b + 1)
                scores_of(1)
                for h in range(H):
                    turn_probs(h)
                    if h + 2 < H:
                        scores_of(h + 2)
                    if h + 1 == H:
                        pe.wait_ge(conv_ready, b + 2)
                        pe.wait_ge(w_here, 16)
                        pe.wait_ge(top_ready, 1 + H * (b + 1))
                        project(0, range(s.CCH, s.DCH))
                    weigh_values(h)
                    if h == 1:
                        pe.wait_ge(z_ready, b + 1)
                        for i in range(s.CCH):
                            ins = pe.transpose(ps[:, T_, i * P:(i + 1) * P], z[:, i * P:(i + 1) * P], g.ident[:, :])
                        ins.then_inc(zT_psum, 1)
                project(1, range(s.CCH, s.DCH - 2))
                pe.wait_ge(o_ready, b + 1)
                for i in range(s.CCH):
                    ins = pe.transpose(ps[:, T_, i * P:(i + 1) * P], o[:, i * P:(i + 1) * P], g.ident[:, :])
                ins.then_inc(oT_psum, 1)
                if kb0 == 0:
                    turn_queries(b + 1)
                project(1, range(s.DCH - 2, s.DCH))
                pe.wait_ge(oT_ready, b + 1)
                project(0, range(s.CCH))
                project(1, range(s.CCH)).then_inc(x1_psum, 1)

            def turn_queries(b):
                pe.wait_ge(q_staged, b + 1)
                for h in range(H):
                    ins = pe.transpose(ps[0:s.HD + 1, PT_ + h // 4, (h % 4) * P:(h % 4 + 1) * P], q_aug[:, h, :], g.ident[:, :])
                ins.then_inc(qT_psum, 1)

            turn_queries(0)
            over_blocks(pe, body)

        @block.scalar
        def _(act):
            act.sem_inc(p_ready, 2)

            def body(b, nkb, kb0, mask_at):
                def exp(h):
                    act.wait_ge(top_ready, 1 + H * b + h + 1)
                    nc.scalar.activation(probs[:, h % 2, 0:nkb * P], scores[:, h % 2, 0:nkb * P], ACT.Exp,
                                         bias=ntop[:, h:h + 1], accum_out=rs[:, h:h + 1]).then_inc(p_ready, 1)

                exp(0)
                for h in range(H):
                    if h + 1 < H:
                        exp(h + 1)
                    act.wait_ge(pT_psum, H * b + h + 1)
                    width = min(nkb, 4) * P
                    nc.scalar.copy(probsT[:, 0:width], ps[:, PT_, 0:width]).then_inc(pTa_ready, 1)
                    if h == 3:
                        act.wait_ge(yn_ready, b + 1)
                        act.wait_ge(conv_ready, b + 1)
                        nc.scalar.activation(ew[:, :, :], held_yn[:, :, :], ACT.Exp, scale=-1.0).then_inc(ew_ready, 1)
                act.wait_ge(oT_psum, b + 1)
                nc.scalar.copy(catT[:, 0:s.CCH, :], ps[:, T_, :].rearrange("p (c t) -> p c t", t=P)).then_inc(oT_ready, 1)
                if kb0 == 0:
                    queries_out(b + 1)

            def queries_out(b):
                act.wait_ge(qT_psum, b + 2)
                for i in range(2):
                    ins = nc.scalar.copy(qT[:, 4 * i:4 * i + 4, :], ps[0:s.HD + 1, PT_ + i, :].rearrange("p (h t) -> p h t", t=P))
                ins.then_inc(qT_ready, 1)

            queries_out(0)
            over_blocks(act, body)

        @block.vector
        def _(dve):
            chain = Chain(dve, dve_chain)
            for free in (conv_ready, x1_ready, top_ready):
                dve.sem_inc(free, 1)
            LINKS = H + 6

            def body(b, nkb, kb0, mask_at):
                chain.at(b * LINKS)

                def row_max(h):
                    dve.wait_ge(s_psum, H * b + h + 1)
                    dve.wait_ge(p_ready, H * b + h + 1)
                    banks = ps[:, S_ + 2 * (h % 2):S_ + 2 * (h % 2) + 2, :].rearrange("p a n -> p (a n)")
                    chain.link(nc.vector.tensor_scalar(scores[:, h % 2, 0:nkb * P], banks[:, 0:nkb * P], cb[:, h:h + 1], None,
                                                       ALU.add, ALU.max, accum_out=top[:, h:h + 1]))
                    nc.vector.tensor_scalar(ntop[:, h:h + 1], top[:, h:h + 1], -1.0, None, ALU.mult).then_inc(top_ready, 1)

                dve.wait_ge(c_staged, b + 1)
                row_max(0)
                row_max(1)
                dve.wait_ge(y_psum, b + 2)
                chain.link(nc.vector.bn_stats(stats[:, :], ps[:, T_, :]))
                dve.sem_inc(dve_held, 1)
                nc.vector.bn_aggr(mv[:, :], stats[:, :]).then_inc(mv_ready, 1)
                dve.wait_ge(mv_ready, b + 1)
                dve.wait_ge(lnr_ready, b + 1)
                nc.vector.tensor_scalar(z[:, :], ps[:, T_, :], mv[:, 0:1], lnr[:, 0:1], ALU.subtract, ALU.mult).then_inc(z_ready, 1)
                for h in range(H):
                    if nkb > HALF:
                        dve.wait_ge(pT_psum, H * b + h + 1)
                        nc.vector.tensor_copy(probsT[:, BANK:nkb * P], ps[:, PT_ + 1, 0:nkb * P - BANK]).then_inc(pTd_ready, 1)
                    if h + 2 < H:
                        row_max(h + 2)
                    if h == 2:
                        dve.wait_ge(zT_psum, b + 1)
                        for i in range(s.CCH):
                            ins = nc.vector.tensor_scalar(yn[:, i, :], ps[:, T_, i * P:(i + 1) * P], c.ln_g[:, i:i + 1],
                                                          c.ln_b[:, i:i + 1], ALU.mult, ALU.add)
                        chain.link(ins)
                        nc.vector.tensor_scalar(held_yn[:, :, :], yn[:, :, :], LEAST, None, ALU.max).then_inc(yn_ready, 1)
                    if h == 4:
                        dve.wait_ge(ew_ready, b + 1)
                        chain.link(nc.vector.tensor_scalar(ew[:, :, :], ew[:, :, :], 1.0, None, ALU.add))
                    if h in (4, 5):
                        half = slice((h - 4) * s.CCH // 2, (h - 3) * s.CCH // 2)
                        chain.link(nc.vector.reciprocal(ew[:, half, :], ew[:, half, :]))
                    if h == 5:
                        nc.vector.tensor_tensor(out=catT[:, s.CCH:s.DCH, :], in0=yn[:, :, :], in1=ew[:, :, :],
                                                op=ALU.mult).then_inc(conv_ready, 1)
                dve.wait_ge(pv_psum, H * (b + 1))
                chain.link(nc.vector.reciprocal(rinv[:, :], rs[:, :]))
                nc.vector.tensor_tensor(out=o[:, :].rearrange("p (h e) -> p h e", e=s.HD),
                                        in0=ps[:, O_, :].rearrange("p (h e) -> p h e", e=s.HD),
                                        in1=rinv[:, :].unsqueeze(2).broadcast_to([P, H, s.HD]), op=ALU.mult).then_inc(o_ready, 1)
                dve.wait_ge(x1_psum, b + 1)
                dve.wait_ge(x_here, 16 * (b + 1))
                dve.wait_ge(x1_stored, 16 * (b + 1))
                dve.wait_ge(xn_ready, b + 1)
                nc.vector.tensor_tensor(out=x1[:, :], in0=ps[:, X1_:X1_ + 2, :].rearrange("p a n -> p (a n)"), in1=xres[:, :],
                                        op=ALU.add).then_inc(x1_ready, 1)
                dve.wait_ge(x1_ready, b + 2)
                nc.vector.tensor_tensor_reduce(out=sq[:, :], in0=x1[:, :], in1=x1[:, :], scale=1.0, scalar=0.0, op0=ALU.mult,
                                               op1=ALU.add, accum_out=rms[:, 0:1]).then_inc(ss_ready, 1)
                assert chain.n == LINKS

            over_blocks(dve, body)
            dve.wait_ge(last_rms_ready, 1)
            dve.wait_ge(gf_here, 16)
            dve.wait_ge(xn_stored, 16 * (s.NB + 1))
            nc.vector.scalar_tensor_tensor(out=xn[:, :], in0=x1[:, :], scalar=rms[:, 2:3], in1=gf[:, :],
                                           op0=ALU.mult, op1=ALU.mult).then_inc(xn_ready, 1)


def phase_c(nc, s, d, g):
    with ExitStack() as ctx:
        def sb(name, shape, dt=F32):
            return ctx.enter_context(nc.sbuf_tensor(name, shape, dt))

        def sem(name):
            return ctx.enter_context(nc.semaphore(name))

        K, PH = s.K, s.PH
        RING = 8
        DIAGS = 8
        AHEAD = 6
        PAIR = 2 * s.HALF
        NEG = -3.0e38

        w_pq = sb("w_pq_sb", [P, s.DCH, PH * PAIR])
        keysT = sb("sub_keysT", [P, 2, PH, s.NKEYS])
        xn_next = sb("xn_next", [P, s.D])
        xn_after = sb("xn_after", [P, s.D])
        xn = sb("xn_c", [P, s.D])
        xnT = sb("xnT_c", [P, s.DCH, P])
        u_rows = sb("u_rows", [P, RING, s.D])
        v_rows = sb("v_rows", [P, RING, s.D])
        keys = v_rows[:, 0:2, :].rearrange("p a n -> p (a n)").rearrange("p (x e) -> p x e", e=s.HALF)
        q = sb("q_c", [P, PAIR])
        qT = sb("qT_c", [P, 2, P])
        half_s = sb("half_scores", [P, 2, 2, s.NKEYS])
        left = sb("left_scores", [P, 2, s.NKEYS])
        top = sb("top_scores", [P, 2, K])
        top_i = sb("top_keys", [P, 2, K], U32)
        top_f = sb("top_keys_f", [P, 2, K])
        cand = sb("cand", [P, K, K])
        cand_left = sb("cand_left", [P, K, K])
        best = sb("best", [P, 2, K])
        best_j = sb("best_j", [P, K], U32)
        ij = sb("best_ij", [P, 2, K], U32)
        ij_f = sb("best_ij_f", [P, 2, K])
        hit = sb("hit", [P, 2, K, K])
        key_f = sb("best_key_f", [P, 2, K])
        nbest = sb("neg_best", [P, 2])
        count = sb("count_to_k", [P, K])
        experts = sb("experts", [P, PH, K], U32)
        exps = sb("gate_exps", [P, PH, K])
        expsum = sb("gate_sums", [P, PH])
        gate_inv = sb("gate_inv", [P, 1])
        dots = sb("dots", [P, 2, K])
        gelu = sb("gelu_c", [P, 2, K])
        act_w = sb("act_c", [P, 2, K])
        diag = sb("diag", [P, DIAGS, P])
        ident_twice = sb("ident_twice", [P, s.TS])
        zeros = sb("zeros_c", [P, BANK])
        out_rows = sb("out_rows", [P, s.D])
        x2 = sb("x2_c", [P, s.D])
        y = sb("y_c", [P, s.D])
        gf = sb("g_final_rows", [P, s.D])
        rms = sb("rms_c", [P, 3])

        keys_here, xn_here = sem("keys_here"), sem("xn_here")
        w_here = [sem(f"w_here_c{h}") for h in range(PH)]
        gf_here, x1_here, y_ready, y_stored = sem("gf_here"), sem("x1_here_c"), sem("y_ready"), sem("y_stored")
        out_used, ms_ready, rstd_ready, final_chain = sem("out_used"), sem("ms_ready_c"), sem("rstd_ready_c"), sem("final_chain")
        consts = sem("consts_c")
        keys_psum, keys_ready = sem("keys_psum"), sem("keys_ready")
        xn_moved, xn_taken, xnT_psum, xnT_ready = sem("xn_moved"), sem("xn_taken"), sem("xnT_psum"), sem("xnT_ready")
        q_psum, q_out, qT_psum, qT_out, s_psum, s_out, s_used = (
            sem(n + "_c") for n in ("q_psum", "q_out", "qT_psum", "qT_out", "s_psum", "s_out", "s_used"))
        best_ready, exps_ready, experts_ready = sem("best_ready"), sem("exps_ready"), sem("experts_ready")
        u_here = [sem(f"u_here{i}") for i in range(RING)]
        v_here = [sem(f"v_here{i}") for i in range(RING)]
        u_used, v_used = sem("u_used"), sem("v_used")
        gelu_ready, act_ready, diag_ready = sem("gelu_ready"), sem("act_ready"), sem("diag_ready")
        sum_psum, out_ready = sem("sum_psum"), sem("out_ready")
        dve_chain, dve_held, pool_held = sem("dve_chain_c"), sem("dve_held_c"), sem("pool_held_c")

        ps = g.ps
        ACC_, Q_, QT_, S_, XT_ = 0, 2, 3, 4, 5
        KEY_BANKS = (ACC_, ACC_ + 1, QT_, S_)
        USES = K // RING
        U_FREE, V_FREE = RING, RING + K

        FIRST = 2
        CATCH_UP = [[2, 3], [4, 5], [6], [7, 8], [9], [10, 11], [12], [13]]

        STRIDE = {1: 3, 2: 2}

        SAMPLE_CHOSEN = lambda v: s.NB * PH + PH // 2 + 2 * (v + 1)

        def head_pairs(eng, body, first=0, last=PH // 2):
            with eng.Fori(first, last) as j:
                for parity in range(2):
                    body(j * 2 + parity, parity)

        block = ctx.enter_context(nc.Block())

        @block.sync
        def _(sp):
            xn_rows, x1_rows = (rows.rearrange("b p n -> (b p) n") for rows in (d.xn2, d.x1))

            def load_rows(b, src):
                sp.wait_ge(xn_moved, b)
                sp.wait_ge(xnT_psum, b)
                sp.dma_start(xn_next[:, :], src).then_inc(xn_here, 16)

            def finish(b, x1_src, dst, rows):
                sp.wait_ge(y_ready, b + 1)
                sp.dma_start(x2[0:rows, :], x1_src).then_inc(x1_here, 16)
                sp.wait_ge(y_ready, b + 2)
                sp.dma_start(dst, y[0:rows, :]).then_inc(y_stored, 16)

            sp.dma_start(xn_next[:, :], d.xn2[0]).then_inc(xn_here, 16)
            for p in range(2):
                sp.dma_start(keys[:, p * PH:(p + 1) * PH, :], d.sub_keys[0, p].rearrange("h k e -> k h e")).then_inc(keys_here, 16)
            for h in range(PH):
                sp.dma_start(w_pq[:, :, h * PAIR:(h + 1) * PAIR],
                             d.w_pq[0][:, h * PAIR:(h + 1) * PAIR].rearrange("(c p) n -> p c n", p=P)).then_inc(w_here[h], 16)
            sp.dma_start(gf[:, :], d.g_final.partition_broadcast(P)).then_inc(gf_here, 16)
            sp.sem_inc(y_stored, 16)
            load_rows(1, d.xn2[1])
            with sp.Fori(0, s.NB - 2) as i:
                load_rows(i + 2, xn_rows[bass.ds((i + 2) * P, P), :])
                finish(i, x1_rows[bass.ds(i * P, P), :], d.y_prompt[0, bass.ds(i * P, P), :], P)
            load_rows(s.NB, d.xn2[s.NB, 0:s.TS, :].unsqueeze(0).broadcast_to([2, s.TS, s.D]))
            finish(s.NB - 2, d.x1[s.NB - 2], d.y_prompt[0, (s.NB - 2) * P:(s.NB - 1) * P, :], P)
            finish(s.NB - 1, d.x1[s.NB - 1], d.y_prompt[0, (s.NB - 1) * P:s.NB * P, :], P)
            finish(s.NB, d.x1[s.NB, 0:s.TS, :], d.y_sample[0], s.TS)
            sp.wait_ge(y_stored, 16 * (s.NB + 2))

        @block.gpsimd
        def _(pool):
            def wait(semaphore, value):
                pool.wait_ge(semaphore, value)
                pool.sem_inc(pool_held, 1)

            nc.gpsimd.memset(zeros[:, :], 0.0).then_inc(consts, 1)
            nc.gpsimd.tensor_tensor(out=ident_twice[:, :], in0=g.ident[:, 0:s.TS], in1=g.ident[:, s.TS:P],
                                    op=ALU.add).then_inc(consts, 1)
            nc.gpsimd.iota(count[:, :], pattern=[[1, K]], base=0, channel_multiplier=0,
                           allow_small_or_imprecise_dtypes=True).then_inc(consts, 1)

            def gather(table, ring, here, used, free, n, h, k):
                wait(used, free - RING + K * n + k + 1)
                nc.gpsimd.indirect_dma_start(
                    out=ring[:, k % RING, :], out_offset=None, in_=table,
                    in_offset=bass.IndirectOffsetOnAxis(ap=experts[:, h, k:k + 1], axis=0),
                ).then_inc(here[k % RING], 16)

            def gather_u(n, h, k):
                gather(d.u_emb[0], u_rows, u_here, u_used, U_FREE, n, h, k)

            def gather_v(n, h, k):
                gather(d.v_emb[0], v_rows, v_here, v_used, V_FREE, n, h, k)

            pool.wait_ge(experts_ready, 1)
            for k in range(K):
                gather_u(0, 0, k)
            def prompt_head(i, h, chosen):
                wait(experts_ready, chosen)
                for k in range(K):
                    gather_u(i * PH + h + 1, (h + 1) % PH, k)
                    gather_v(i * PH + h, h, k)

            def inverse_rms(b, rows):
                pool.wait_ge(ms_ready, b + 1)
                nc.gpsimd.tensor_tensor(out=rms[0:rows, 2:3], in0=rms[0:rows, 1:2], in1=g.neg_half[0:rows, :],
                                        op=ALU.pow).then_inc(rstd_ready, 1)

            for h in range(PH):
                prompt_head(0, h, h + 2)
            with pool.Fori(1, s.NB - 1) as i:
                for h in range(PH):
                    prompt_head(i, h, i * PH + h + 2)
                    if h == 3:
                        inverse_rms(i - 1, P)
            for h in range(PH):
                n = (s.NB - 1) * PH + h
                prompt_head(s.NB - 1, h, n + 2 if h + 1 < PH else SAMPLE_CHOSEN(0))
                if h == 3:
                    inverse_rms(s.NB - 2, P)
            for v in range(PH // 2):
                n = s.NB * PH + v
                if v + 1 < PH // 2:
                    wait(experts_ready, SAMPLE_CHOSEN(v + 1))
                for k in range(K):
                    if v + 1 < PH // 2:
                        gather_u(n + 1, v + 1, k)
                    gather_v(n, v, k)
                if v == 2:
                    inverse_rms(s.NB - 1, P)
            inverse_rms(s.NB, s.TS)

        @block.tensor
        def _(pe):
            def turn_rows(b):
                pe.wait_ge(xn_here, 16 * (b + 1))
                for x in range(s.DCH):
                    ins = pe.transpose(ps[:, XT_ + x // 4, (x % 4) * P:(x % 4 + 1) * P], xn_next[:, x * P:(x + 1) * P], g.ident[:, :])
                ins.then_inc(xnT_psum, 1)

            def query(b, r, h):
                pe.wait_ge(xnT_ready, b + 1)
                for x in range(s.DCH):
                    ins = pe.matmul(ps[:, Q_, 0:PAIR], xnT[:, x, :], w_pq[:, x, bass.ds(h * PAIR, PAIR)],
                                    start=(x == 0), stop=(x == s.DCH - 1))
                ins.then_inc(q_psum, 1)

            def turn_query(r):
                pe.wait_ge(q_out, r + 1)
                for p in range(2):
                    ins = pe.transpose(ps[:, QT_, p * P:(p + 1) * P], q[:, p * P:(p + 1) * P], g.ident[:, :])
                ins.then_inc(qT_psum, 1)

            def score(r, h):
                pe.wait_ge(qT_out, r + 1)
                pe.wait_ge(s_out, r + 1)
                for p in range(2):
                    keys_h = keysT[:, p, bass.ds(h, 1), :].rearrange("p a k -> p (a k)")
                    ins = pe.matmul(ps[:, S_, p * P:(p + 1) * P], qT[:, p, :], keys_h, start=True, stop=True)
                ins.then_inc(s_psum, 1)

            def weigh(n, k, rows):
                pe.wait_ge(v_here[k % RING], 16 * (USES * n + k // RING + 1))
                pe.wait_ge(diag_ready, 2 * K + K * n + k + 1)
                for half in range(s.D // BANK):
                    ins = pe.matmul(ps[0:rows, ACC_ + half, :], diag[:, k % DIAGS, 0:rows],
                                    v_rows[:, k % RING, half * BANK:(half + 1) * BANK], start=False, stop=False)
                ins.then_inc(v_used, 1)

            def sums(rows, first):
                for half in range(s.D // BANK):
                    ins = pe.matmul(ps[0:rows, ACC_ + half, :], zeros[0:rows, 0:rows], zeros[0:rows, 0:BANK],
                                    start=first, stop=not first)
                return ins

            def weigh_and_route(n, routes):
                todo = []
                for b, r, h in routes:
                    todo += [lambda b=b, r=r, h=h: query(b, r, h), lambda r=r: turn_query(r), lambda r=r, h=h: score(r, h)]
                for k in range(K):
                    weigh(n, k, P)
                    if k % STRIDE[len(routes)] == 0 and todo:
                        todo.pop(0)()
                assert not todo

            pe.sem_inc(v_used, V_FREE)
            turn_rows(0)
            pe.wait_ge(keys_here, 32)
            for x in range(2 * PH):
                ins = pe.transpose(ps[:, KEY_BANKS[x // 4], (x % 4) * P:(x % 4 + 1) * P], keys[:, x, :], g.ident[:, :])
            ins.then_inc(keys_psum, 1)
            pe.wait_ge(w_here[0], 16)
            query(0, 0, 0)
            pe.wait_ge(keys_ready, 1)
            for r in range(FIRST + 2):
                turn_query(r)
                if r + 1 < FIRST + 2:
                    pe.wait_ge(w_here[r + 1], 16)
                    query(0, r + 1, r + 1)
                score(r, r)
            pe.wait_ge(consts, 3)
            pe.wait_ge(out_ready, 1)
            sums(P, True)
            for h in range(PH):
                if h == 2:
                    turn_rows(1)
                routed = [r + 2 for r in CATCH_UP[h]]
                for r in routed:
                    if r < PH:
                        pe.wait_ge(w_here[r], 16)
                weigh_and_route(h, [(r // PH, r, r % PH) for r in routed])
            sums(P, False).then_inc(sum_psum, 1)
            with pe.Fori(1, s.NB) as i:
                turn_rows(i + 1)
                pe.wait_ge(out_ready, i + 1)
                sums(P, True)
                head_pairs(pe, lambda h, parity: weigh_and_route(i * PH + h, [(i + 1, i * PH + h + PH, h)]))
                sums(P, False).then_inc(sum_psum, 1)
            pe.wait_ge(out_ready, s.NB + 1)
            sums(s.TS, True)
            for v in range(PH // 2):
                for k in range(K):
                    weigh(s.NB * PH + v, k, s.TS)
            sums(s.TS, False).then_inc(sum_psum, 1)

        @block.scalar
        def _(act):
            def rows_out(b):
                act.wait_ge(xnT_psum, b + 1)
                for x in range(2):
                    ins = nc.scalar.copy(xnT[:, 4 * x:4 * x + 4, :], ps[:, XT_ + x, :].rearrange("p (c t) -> p c t", t=P))
                ins.then_inc(xnT_ready, 1)
                act.wait_ge(xn_taken, b + 1)
                nc.scalar.copy(xn_after[:, :], xn_next[:, :]).then_inc(xn_moved, 1)

            def query_out(r):
                act.wait_ge(q_psum, r + 1)
                nc.scalar.copy(q[:, :], ps[:, Q_, 0:PAIR]).then_inc(q_out, 1)

            def turned_out(r):
                act.wait_ge(qT_psum, r + 1)
                nc.scalar.copy(qT[:, :, :], ps[:, QT_, 0:PAIR].rearrange("p (a t) -> p a t", t=P)).then_inc(qT_out, 1)

            def scores_out(r, parity):
                act.wait_ge(s_psum, r + 1)
                act.wait_ge(s_used, r + 1)
                nc.scalar.copy(half_s[:, parity, :, :], ps[:, S_, 0:2 * s.NKEYS].rearrange("p (a k) -> p a k", a=2)).then_inc(s_out, 1)

            def gate_exps(r, slot, parity):
                act.wait_ge(best_ready, r + 1)
                nc.scalar.activation(exps[:, bass.ds(slot, 1), :].rearrange("p a k -> p (a k)"), best[:, parity, :], ACT.Exp,
                                     bias=nbest[:, parity:parity + 1], accum_out=expsum[:, bass.ds(slot, 1)]).then_inc(exps_ready, 1)

            def gelus(n, parity):
                act.wait_ge(u_used, U_FREE + K * (n + 1))
                act.wait_ge(act_ready, n + 1)
                nc.scalar.activation(gelu[:, parity, :], dots[:, parity, :], ACT.Gelu).then_inc(gelu_ready, 1)

            def diagonals(n, parity, ks, rows):
                for k in ks:
                    act.wait_ge(act_ready, n + 2)
                    act.wait_ge(v_used, V_FREE + K * n + k - DIAGS + 1)
                    source = g.ident if rows == P else ident_twice
                    nc.scalar.mul(diag[:, k % DIAGS, 0:rows], source[:, 0:rows], act_w[:, parity, k:k + 1]).then_inc(diag_ready, 1)

            def close(b, rows):
                act.wait_ge(sum_psum, b + 1)
                act.wait_ge(out_used, b + 1)
                nc.scalar.copy(out_rows[0:rows, :], ps[0:rows, ACC_:ACC_ + 2, :].rearrange("p a n -> p (a n)")).then_inc(out_ready, 1)

            act.sem_inc(s_out, 1)
            act.sem_inc(diag_ready, 2 * K)
            act.sem_inc(out_ready, 1)
            rows_out(0)
            act.wait_ge(keys_psum, 1)
            for x in range(2 * PH // 4):
                dst = keysT[:, x // 2, 4 * (x % 2):4 * (x % 2) + 4, :]
                ins = nc.scalar.copy(dst, ps[:, KEY_BANKS[x], :].rearrange("p (h k) -> p h k", k=s.NKEYS))
            ins.then_inc(keys_ready, 1)
            for r in range(FIRST + 2):
                query_out(r)
                turned_out(r)
                if r >= 3:
                    gate_exps(r - 3, r - 3, (r - 3) % 2)
                scores_out(r, r % 2)
            gate_exps(FIRST - 1, FIRST - 1, (FIRST - 1) % 2)
            for h in range(PH):
                if h == 2:
                    rows_out(1)
                gelus(h, h % 2)
                chosen = CATCH_UP[h]
                k = 0
                for r in chosen:
                    for part in range(3):
                        ahead = min(k + STRIDE[len(chosen)], K)
                        diagonals(h, h % 2, range(k, ahead), P)
                        k = ahead
                        if part == 0:
                            if r != chosen[0]:
                                gate_exps(r - 1, (r - 1) % PH, (r - 1) % 2)
                            query_out(r + 2)
                        elif part == 1:
                            turned_out(r + 2)
                        else:
                            if len(chosen) == 1:
                                gate_exps(r, r % PH, r % 2)
                            scores_out(r + 2, r % 2)
                diagonals(h, h % 2, range(k, K), P)
                if len(chosen) > 1:
                    gate_exps(chosen[-1], chosen[-1] % PH, chosen[-1] % 2)
            close(0, P)
            with act.Fori(1, s.NB) as i:
                rows_out(i + 1)

                def head(h, parity):
                    n = i * PH + h
                    gelus(n, parity)
                    diagonals(n, parity, range(0, 3), P)
                    query_out(n + PH)
                    diagonals(n, parity, range(3, 6), P)
                    turned_out(n + PH)
                    gate_exps(n + AHEAD, (h + AHEAD) % PH, parity)
                    diagonals(n, parity, range(6, 9), P)
                    scores_out(n + PH, parity)
                    diagonals(n, parity, range(9, K), P)

                head_pairs(act, head)
                close(i, P)
            act.wait_ge(consts, 3)
            for v in range(PH // 2):
                n = s.NB * PH + v
                gelus(n, v % 2)
                diagonals(n, v % 2, range(0, 6), s.TS)
                if v + AHEAD < PH:
                    gate_exps(n + AHEAD, v + AHEAD, v % 2)
                diagonals(n, v % 2, range(6, K), s.TS)
            close(s.NB, s.TS)

        @block.vector
        def _(dve):
            chain = Chain(dve, dve_chain)

            def settle(ins):
                chain.link(ins)
                dve.sem_inc(dve_held, 1)

            def choose(r, parity, slot, refill=True):
                dve.wait_ge(s_out, r + 2)
                dve.sem_inc(dve_held, 1)
                sc = half_s[:, parity, :, :]
                for p in range(2):
                    ins = nc.vector.max(top[:, p, 0:8], sc[:, p, :])
                settle(ins)
                for p in range(2):
                    nc.vector.max_index(top_i[:, p, 0:8], top[:, p, 0:8], sc[:, p, :])
                for p in range(2):
                    ins = nc.vector.match_replace(left[:, p, :], top[:, p, 0:8], sc[:, p, :], NEG)
                ins.then_inc(s_used, 1)
                dve.wait_ge(s_used, 2 + r + 1)
                dve.sem_inc(dve_held, 1)
                for p in range(2):
                    ins = nc.vector.max(top[:, p, 8:K], left[:, p, :])
                settle(ins)
                for p in range(2):
                    ins = nc.vector.max_index(top_i[:, p, 8:K], top[:, p, 8:K], left[:, p, :])
                nc.vector.tensor_tensor(out=cand[:, :, :], in0=top[:, 0, :].unsqueeze(2).broadcast_to([P, K, K]),
                                        in1=top[:, 1, :].unsqueeze(1).broadcast_to([P, K, K]), op=ALU.add).then_inc(dve_chain, 1)
                chain.n += 1
                dve.wait_ge(dve_chain, chain.base + chain.n)
                chain.link(nc.vector.tensor_copy(top_f[:, :, :], top_i[:, :, :]))
                dve.wait_ge(exps_ready, r + 1)
                dve.sem_inc(dve_held, 1)
                best_, nbest_ = best[:, parity, :], nbest[:, parity:parity + 1]
                flat, flat_left = (t[:, :, :].rearrange("p a b -> p (a b)") for t in (cand, cand_left))
                settle(nc.vector.max(best_[:, 0:8], flat))
                nc.vector.max_index(best_j[:, 0:8], best_[:, 0:8], flat)
                settle(nc.vector.match_replace(flat_left, best_[:, 0:8], flat, NEG))
                settle(nc.vector.max(best_[:, 8:K], flat_left))
                settle(nc.vector.max_index(best_j[:, 8:K], best_[:, 8:K], flat_left))
                nc.vector.tensor_scalar(nbest_, best_[:, 0:1], -1.0, None, ALU.mult).then_inc(best_ready, 1)
                nc.vector.tensor_scalar(ij[:, 0, :], best_j[:, :], 4, None, ALU.logical_shift_right)
                chain.link(nc.vector.tensor_scalar(ij[:, 1, :], best_j[:, :], K - 1, None, ALU.bitwise_and))
                chain.link(nc.vector.tensor_copy(ij_f[:, :, :], ij[:, :, :]))
                chain.link(nc.vector.tensor_tensor(out=hit[:, :, :, :], in0=ij_f[:, :, :].unsqueeze(3).broadcast_to([P, 2, K, K]),
                                                   in1=count[:, :].unsqueeze(1).unsqueeze(1).broadcast_to([P, 2, K, K]), op=ALU.is_equal))
                chain.link(nc.vector.tensor_tensor(out=hit[:, :, :, :], in0=hit[:, :, :, :],
                                                   in1=top_f[:, :, :].unsqueeze(2).broadcast_to([P, 2, K, K]), op=ALU.mult))
                chain.link(nc.vector.tensor_reduce(key_f[:, :, :], hit[:, :, :, :], AX.X, ALU.add))
                if refill:
                    dve.wait_ge(v_used, V_FREE + K * (r - PH + 1))
                nc.vector.scalar_tensor_tensor(out=experts[:, bass.ds(slot, 1), :].rearrange("p a k -> p (a k)"), in0=key_f[:, 0, :],
                                               scalar=float(s.NKEYS), in1=key_f[:, 1, :], op0=ALU.mult,
                                               op1=ALU.add).then_inc(experts_ready, 1)

            def dot(n, parity):
                for k in range(K):
                    dve.wait_ge(u_here[k % RING], 16 * (USES * n + k // RING + 1))
                    row = u_rows[:, k % RING, :]
                    nc.vector.tensor_tensor_reduce(out=row, in0=row, in1=xn[:, :], scale=1.0, scalar=0.0, op0=ALU.mult,
                                                   op1=ALU.add, accum_out=dots[:, parity, k:k + 1]).then_inc(u_used, 1)

            def weights(n, parity, exps_here, parts):
                dve.wait_ge(exps_ready, exps_here)
                for rows, h in parts:
                    ins = nc.vector.reciprocal(gate_inv[rows, :], expsum[rows, bass.ds(h, 1)])
                chain.link(ins)
                dve.wait_ge(gelu_ready, n + 1)
                dve.wait_ge(diag_ready, K * n + K)
                for rows, h in parts:
                    ins = nc.vector.scalar_tensor_tensor(out=act_w[rows, parity, :], in0=gelu[rows, parity, :], scalar=gate_inv[rows, 0:1],
                                                         in1=exps[rows, bass.ds(h, 1), :].rearrange("p a k -> p (a k)"),
                                                         op0=ALU.mult, op1=ALU.mult)
                ins.then_inc(act_ready, 1)

            ALL, LOWER, UPPER = slice(0, P), slice(0, s.TS), slice(s.TS, P)

            def copy_upper(v):
                dve.wait_ge(experts_ready, SAMPLE_CHOSEN(v) - 1)
                nc.vector.tensor_copy(experts[UPPER, v, :], experts[UPPER, v + PH // 2, :]).then_inc(experts_ready, 1)

            def take_rows(b):
                dve.wait_ge(xn_moved, b + 1)
                nc.vector.tensor_copy(xn[:, :], xn_after[:, :]).then_inc(xn_taken, 1)
                dve.wait_ge(xn_taken, b + 2)
                dve.sem_inc(dve_held, 1)

            def add_residual(b, rows):
                final = Chain(dve, final_chain, 2 * b)
                dve.wait_ge(x1_here, 16 * (b + 1))
                dve.wait_ge(out_ready, b + 2)
                final.link(nc.vector.tensor_tensor(out=x2[0:rows, :], in0=x2[0:rows, :], in1=out_rows[0:rows, :], op=ALU.add))
                dve.sem_inc(out_used, 1)
                dve.wait_ge(y_stored, 16 * (b + 1))
                final.link(nc.vector.tensor_tensor_reduce(out=y[0:rows, :], in0=x2[0:rows, :], in1=x2[0:rows, :], scale=1.0, scalar=0.0,
                                                          op0=ALU.mult, op1=ALU.add, accum_out=rms[0:rows, 0:1]))
                nc.vector.tensor_scalar(rms[0:rows, 1:2], rms[0:rows, 0:1], 1.0 / s.D, RMS_EPS, ALU.mult, ALU.add).then_inc(ms_ready, 1)

            def normalise(b, rows):
                dve.wait_ge(rstd_ready, b + 1)
                nc.vector.scalar_tensor_tensor(out=y[0:rows, :], in0=x2[0:rows, :], scalar=rms[0:rows, 2:3], in1=gf[0:rows, :],
                                               op0=ALU.mult, op1=ALU.mult).then_inc(y_ready, 1)

            dve.sem_inc(u_used, U_FREE)
            dve.sem_inc(s_used, 2)
            dve.sem_inc(act_ready, 1)
            dve.sem_inc(exps_ready, 2)
            dve.sem_inc(out_used, 1)
            dve.sem_inc(xn_taken, 1)
            dve.sem_inc(y_ready, 1)
            dve.wait_ge(consts, 3)
            CHOOSE = 13
            for r in range(FIRST):
                choose(r, r % 2, r, refill=False)
            assert chain.n == FIRST * CHOOSE, chain.n
            take_rows(0)
            for h in range(PH):
                dot(h, h % 2)
                weights(h, h % 2, h + 3, [(ALL, h)])
                for r in CATCH_UP[h]:
                    choose(r, r % 2, r % PH, refill=r >= PH)
            dve.wait_ge(gf_here, 16)
            dve.sem_inc(dve_held, 1)

            def prompt_block(i, last_pair):
                take_rows(i)
                head_pairs(dve, lambda h, parity: prompt_head(i, h, parity), 0, 1)
                add_residual(i - 1, P)
                dve.sem_inc(dve_held, 1)
                head_pairs(dve, lambda h, parity: prompt_head(i, h, parity), 1, PH // 2 - 1)
                normalise(i - 1, P)
                dve.sem_inc(dve_held, 1)
                last_pair(i)

            def prompt_head(i, h, parity):
                n = i * PH + h
                dot(n, parity)
                chain.at((n + AHEAD) * CHOOSE + n)
                weights(n, parity, n + 3, [(ALL, h)])
                choose(n + AHEAD, parity, (h + AHEAD) % PH)

            def last_pair_before_sample(i):
                for h in range(PH - 2, PH):
                    prompt_head(i, h, h % 2)
                    copy_upper(h - (PH - 2))

            with dve.Fori(1, s.NB - 1) as i:
                prompt_block(i, lambda i: head_pairs(dve, lambda h, parity: prompt_head(i, h, parity), PH // 2 - 1, PH // 2))
            prompt_block(s.NB - 1, last_pair_before_sample)
            take_rows(s.NB)
            chain.at((s.NB * PH + AHEAD) * CHOOSE + s.NB * PH)
            for v in range(PH // 2):
                n = s.NB * PH + v
                dot(n, v % 2)
                weights(n, v % 2, n + PH // 2 + 3, [(LOWER, v), (UPPER, v + PH // 2)])
                if v + AHEAD < PH:
                    choose(n + AHEAD, v % 2, v + AHEAD)
                    copy_upper(v + 2)
                if v == 1:
                    add_residual(s.NB - 1, P)
                if v == 3:
                    normalise(s.NB - 1, P)
            add_residual(s.NB, s.TS)
            normalise(s.NB, s.TS)


INPUTS = ["x_prompt", "x_sample", "cache_k", "cache_v", "cache_logf", "state_conv", "g_mix", "w_in", "b_f", "w_dw",
          "b_dw", "ln_g", "ln_b", "w_out", "g_ffn", "w_pq", "sub_keys", "u_emb", "v_emb", "g_final"]


def kernel(**inputs):
    import concourse.bacc as bacc
    from concourse.bass_utils import run_bass_kernel_spmd

    nc = bacc.Bacc("TRN2", target_bir_lowering=False, num_devices=1)
    arrays, args = {}, []
    for name in INPUTS:
        a = np.ascontiguousarray(inputs[name])
        arrays["in_" + name] = a
        args.append(nc.dram_tensor("in_" + name, a.shape, mybir.dt.from_np(a.dtype), kind="ExternalInput").ap())
    x_p, x_s, ck = (inputs[n].shape for n in ("x_prompt", "x_sample", "cache_k"))
    depth, heads, hd = ck[0], ck[3], ck[4]
    conv = inputs["state_conv"].shape[2:]
    outs = [x_p, x_s,
            (depth, *x_p[:2], heads, hd), (depth, *x_p[:2], heads, hd), (depth, *x_p[:2], heads), (depth, x_p[0], *conv),
            (depth, *x_s[:2], heads, hd), (depth, *x_s[:2], heads, hd), (depth, *x_s[:2], heads), (depth, x_s[0], *conv)]
    for i, shape in enumerate(outs):
        args.append(nc.dram_tensor(f"out_{i}", shape, F32, kind="ExternalOutput").ap())
    build(nc, *args)
    r = run_bass_kernel_spmd(nc, [arrays], core_ids=[0])
    return tuple(r.results[0][f"out_{i}"] for i in range(len(outs)))
```
